# Optimizing a Trainium2 kernel written in Bass

```python
import math
import jax, jax.numpy as jnp
from jax import lax
import numpy as np

D_MODEL = 1024
BATCH = 1
SEQ = 1024
DEPTH = 2

N_A = max(1, DEPTH // 2)
N_B = DEPTH - N_A
D_CONV = D_MODEL
CONV_K = 3
N_HEADS = 16
HEAD_DIM = D_MODEL // N_HEADS
D_ATTN = N_HEADS * HEAD_DIM
Q_BLOCK = 128
EPS = 1e-6


def rmsnorm(x, g):
    xf = x.astype(jnp.float32)
    y = xf * lax.rsqrt(jnp.mean(xf * xf, axis=-1, keepdims=True) + EPS)
    return (y * g.astype(jnp.float32)).astype(x.dtype)

def modulation(c, w, b, n):
    m = jax.nn.silu(c) @ w + b
    return jnp.split(m, n, axis=-1)

def modulated_norm(x, g, shift, scale):
    return rmsnorm(x, g) * (1.0 + scale[:, None, :]) + shift[:, None, :]

def causal_dwconv(u, w):
    return lax.conv_general_dilated(
        u, w[:, None, :].astype(u.dtype), window_strides=(1,),
        padding=[(CONV_K - 1, 0)], dimension_numbers=("NWC", "WIO", "NWC"),
        feature_group_count=u.shape[-1])

def short_conv_layer(x, c, mod_w, mod_b, norm_g, w_in, conv_w, w_out):
    shift, scale, gate = modulation(c, mod_w, mod_b, 3)
    h = modulated_norm(x, norm_g, shift, scale)
    proj = h @ w_in
    b_gate, c_gate, u, z = jnp.split(proj, 4, axis=-1)
    y = b_gate * causal_dwconv(c_gate * u, conv_w)
    y = y * jax.nn.silu(z)
    return x + gate[:, None, :] * (y @ w_out)

def stick_breaking_attention(q, k, v):
    seq = q.shape[2]
    inv_sqrt_d = 1.0 / math.sqrt(q.shape[-1])
    outs = []
    for i in range(seq // Q_BLOCK):
        q0 = i * Q_BLOCK
        kend = q0 + Q_BLOCK
        qb = q[:, :, q0:kend].astype(jnp.float32)
        kb = k[:, :, :kend].astype(jnp.float32)
        vb = v[:, :, :kend]
        z = jnp.einsum('bhqd,bhkd->bhqk', qb, kb) * inv_sqrt_d
        qpos = q0 + jnp.arange(Q_BLOCK)[:, None]
        kpos = jnp.arange(kend)[None, :]
        mask = kpos < qpos
        log_beta = jax.nn.log_sigmoid(z)
        log_1m_beta = jnp.where(mask, log_beta - z, 0.0)
        suffix = lax.cumsum(log_1m_beta, axis=3, reverse=True) - log_1m_beta
        a = jnp.where(mask, jnp.exp(log_beta + suffix), 0.0)
        outs.append(jnp.einsum('bhqk,bhkd->bhqd', a.astype(vb.dtype), vb))
    return jnp.concatenate(outs, axis=2)

def split_heads(t):
    b, s, _ = t.shape
    return t.reshape(b, s, N_HEADS, HEAD_DIM).transpose(0, 2, 1, 3)

def stick_breaking_layer(x, c, k, v, mod_w, mod_b, norm_g, w_qz, w_out):
    shift, scale, gate = modulation(c, mod_w, mod_b, 3)
    h = modulated_norm(x, norm_g, shift, scale)
    proj = h @ w_qz
    q, z = jnp.split(proj, 2, axis=-1)
    o = stick_breaking_attention(split_heads(q), k, v)
    b, _, s, _ = o.shape
    o = o.transpose(0, 2, 1, 3).reshape(b, s, D_ATTN)
    o = o * jax.nn.silu(z)
    return x + gate[:, None, :] * (o @ w_out)

def first_inputs(seed: int = 0) -> dict:
    key = jax.random.key(seed)
    ks = jax.random.split(key, 20)
    D = D_MODEL
    nrm = lambda k, shape, s: jax.random.normal(k, shape, jnp.float32) * s
    return {
        "x": nrm(ks[0], (BATCH, SEQ, D), 1.0),
        "c": nrm(ks[1], (BATCH, D), 1.0),
        "a_mod_w": nrm(ks[2], (N_A, D, 3 * D), 0.02),
        "a_mod_b": nrm(ks[3], (N_A, 3 * D), 0.01),
        "a_norm_g": 1.0 + nrm(ks[4], (N_A, D), 0.02),
        "a_w_in": nrm(ks[5], (N_A, D, 4 * D_CONV), D ** -0.5),
        "a_conv_w": nrm(ks[6], (N_A, CONV_K, D_CONV), CONV_K ** -0.5),
        "a_w_out": nrm(ks[7], (N_A, D_CONV, D), D_CONV ** -0.5),
        "kv_mod_w": nrm(ks[8], (D, 2 * D), 0.02),
        "kv_mod_b": nrm(ks[9], (2 * D,), 0.01),
        "kv_norm_g": 1.0 + nrm(ks[10], (D,), 0.02),
        "w_kv": nrm(ks[11], (D, 2 * D_ATTN), D ** -0.5),
        "b_mod_w": nrm(ks[12], (N_B, D, 3 * D), 0.02),
        "b_mod_b": nrm(ks[13], (N_B, 3 * D), 0.01),
        "b_norm_g": 1.0 + nrm(ks[14], (N_B, D), 0.02),
        "b_w_qz": nrm(ks[15], (N_B, D, 2 * D_ATTN), D ** -0.5),
        "b_w_out": nrm(ks[16], (N_B, D_ATTN, D), D_ATTN ** -0.5),
        "final_norm_g": 1.0 + nrm(ks[17], (D,), 0.02),
    }

def first_block(x, c, a_mod_w, a_mod_b, a_norm_g, a_w_in, a_conv_w, a_w_out,
              kv_mod_w, kv_mod_b, kv_norm_g, w_kv,
              b_mod_w, b_mod_b, b_norm_g, b_w_qz, b_w_out, final_norm_g):
    k = v = None
    for layer in range(DEPTH):
        if layer < N_A:
            x = short_conv_layer(x, c, a_mod_w[layer], a_mod_b[layer], a_norm_g[layer],
                                 a_w_in[layer], a_conv_w[layer], a_w_out[layer])
        else:
            if layer == N_A:
                kv_shift, kv_scale = modulation(c, kv_mod_w, kv_mod_b, 2)
                hkv = modulated_norm(x, kv_norm_g, kv_shift, kv_scale)
                k_flat, v_flat = jnp.split(hkv @ w_kv, 2, axis=-1)
                k, v = split_heads(k_flat), split_heads(v_flat)
            j = layer - N_A
            x = stick_breaking_layer(x, c, k, v, b_mod_w[j], b_mod_b[j], b_norm_g[j],
                                     b_w_qz[j], b_w_out[j])
    return rmsnorm(x, final_norm_g)


DEPTH_2 = 1

N_MIXERS = 2
N_MEM = 256
MIX_WIDTH = D_MODEL
MEM_HEADS = 4
MEM_WIDTH = MIX_WIDTH // 4
MEM_HEAD_DIM = MEM_WIDTH // MEM_HEADS
MAIN_WIDTH = MIX_WIDTH - MEM_WIDTH
MLA_HEADS = 12
QK_NOPE = 64
QK_ROPE = 32
V_HEAD = MAIN_WIDTH // MLA_HEADS
Q_LORA = (3 * D_MODEL) // 8
KV_LORA = D_MODEL // 4
ROPE_THETA = 10000.0
FNET_GROUPS = 4
FNET_GROUP_DIM = MAIN_WIDTH // FNET_GROUPS

MLA_IN = Q_LORA + KV_LORA + QK_ROPE + MEM_WIDTH + MIX_WIDTH
FNET_IN = MAIN_WIDTH + MEM_WIDTH + MIX_WIDTH


def rmsnorm_2(x, g):
    xf = x.astype(jnp.float32)
    y = xf * lax.rsqrt(jnp.mean(xf * xf, axis=-1, keepdims=True) + EPS)
    return (y * g.astype(jnp.float32)).astype(x.dtype)

def rope_tables(positions):
    inv_freq = 1.0 / (ROPE_THETA ** (jnp.arange(0, QK_ROPE, 2, dtype=jnp.float32) / QK_ROPE))
    ang = positions.astype(jnp.float32)[..., None] * inv_freq
    return jnp.cos(ang), jnp.sin(ang)

def apply_rope(t, cos, sin):
    tf = t.astype(jnp.float32)
    t1, t2 = tf[..., : QK_ROPE // 2], tf[..., QK_ROPE // 2:]
    return jnp.concatenate([t1 * cos - t2 * sin, t2 * cos + t1 * sin], axis=-1).astype(t.dtype)

def mla_attention(q_nope, q_rope, k_nope, k_rope, v):
    B, S, H, _ = q_nope.shape
    nb = S // Q_BLOCK
    scale = 1.0 / float(np.sqrt(QK_NOPE + QK_ROPE))

    def to_blocks(t):
        return jnp.moveaxis(t.reshape((B, nb, Q_BLOCK) + t.shape[2:]), 1, 0)

    def one_block(args):
        qn, qr = args
        s = (jnp.einsum('bqhd,bkhd->bhqk', qn, k_nope)
             + jnp.einsum('bqhr,bkr->bhqk', qr, k_rope)).astype(jnp.float32) * scale
        p = jax.nn.softmax(s, axis=-1).astype(v.dtype)
        return jnp.einsum('bhqk,bkhd->bqhd', p, v)

    out = lax.map(one_block, (to_blocks(q_nope), to_blocks(q_rope)))
    return jnp.moveaxis(out, 0, 1).reshape(B, S, H * V_HEAD)

def memory_cross_attention(q_mem, mem, mem_norm_g, w_mem_kv):
    B, S, _ = q_mem.shape
    q = q_mem.reshape(B, S, MEM_HEADS, MEM_HEAD_DIM)
    kv = (rmsnorm_2(mem, mem_norm_g) @ w_mem_kv).reshape(B, mem.shape[1], 2, MEM_HEADS, MEM_HEAD_DIM)
    k, v = kv[:, :, 0], kv[:, :, 1]
    s = jnp.einsum('bshd,bmhd->bhsm', q, k).astype(jnp.float32) * (1.0 / float(np.sqrt(MEM_HEAD_DIM)))
    p = jax.nn.softmax(s, axis=-1).astype(v.dtype)
    return jnp.einsum('bhsm,bmhd->bshd', p, v).reshape(B, S, MEM_WIDTH)

def mla_layer(x, mem, cos, sin, norm_g, w_in, q_norm_g, kv_norm_g, w_uq, w_ukv,
              mem_norm_g, w_mem_kv, w_out):
    B, S, _ = x.shape
    h = rmsnorm_2(x, norm_g)
    proj = h @ w_in
    o1 = Q_LORA
    o2 = o1 + KV_LORA
    o3 = o2 + QK_ROPE
    o4 = o3 + MEM_WIDTH
    c_q, c_kv, k_rope = proj[..., :o1], proj[..., o1:o2], proj[..., o2:o3]
    q_mem, gate = proj[..., o3:o4], proj[..., o4:]
    q = (rmsnorm_2(c_q, q_norm_g) @ w_uq).reshape(B, S, MLA_HEADS, QK_NOPE + QK_ROPE)
    kv = (rmsnorm_2(c_kv, kv_norm_g) @ w_ukv).reshape(B, S, MLA_HEADS, QK_NOPE + V_HEAD)
    q_nope = q[..., :QK_NOPE]
    q_rope = apply_rope(q[..., QK_NOPE:], cos[:, :, None, :], sin[:, :, None, :])
    k_nope, v = kv[..., :QK_NOPE], kv[..., QK_NOPE:]
    k_rope = apply_rope(k_rope, cos, sin)
    attn = mla_attention(q_nope, q_rope, k_nope, k_rope, v)
    mem_out = memory_cross_attention(q_mem, mem, mem_norm_g, w_mem_kv)
    branch = jnp.concatenate([attn, mem_out], axis=-1) * jax.nn.silu(gate)
    return x + branch @ w_out

def fnet_layer(x, mem, norm_g, w_in, w_fnet, mem_norm_g, w_mem_kv, w_out):
    B, S, _ = x.shape
    h = rmsnorm_2(x, norm_g)
    proj = h @ w_in
    f = proj[..., :MAIN_WIDTH].reshape(B, S, FNET_GROUPS, FNET_GROUP_DIM).astype(jnp.float32)
    q_mem = proj[..., MAIN_WIDTH:MAIN_WIDTH + MEM_WIDTH]
    gate = proj[..., MAIN_WIDTH + MEM_WIDTH:]
    spec = jnp.fft.fft2(f, axes=(1, 3), norm='ortho').real
    mixed = jnp.einsum('bsgc,gcd->bsgd', spec, w_fnet.astype(jnp.float32))
    mixed = mixed.reshape(B, S, MAIN_WIDTH).astype(x.dtype)
    mem_out = memory_cross_attention(q_mem, mem, mem_norm_g, w_mem_kv)
    branch = jnp.concatenate([mixed, mem_out], axis=-1) * jax.nn.silu(gate)
    return x + branch @ w_out

def second_inputs(seed: int = 0) -> dict:
    key = jax.random.key(seed)
    ks = jax.random.split(key, 24)
    f32 = jnp.float32

    def w(k, shape, fan_in):
        return jax.random.normal(k, shape, f32) * (fan_in ** -0.5)

    def gain(k, n):
        return 1.0 + 0.02 * jax.random.normal(k, (n,), f32)

    x = jax.random.normal(ks[0], (BATCH, SEQ, D_MODEL), f32)
    mem = jax.random.normal(ks[1], (BATCH, N_MEM, D_MODEL), f32)
    offsets = jax.random.randint(ks[2], (BATCH, 1), 0, 1024, dtype=jnp.int32)
    positions = (jnp.arange(SEQ, dtype=jnp.int32)[None, :] + offsets).astype(jnp.int32)
    return {
        "x": x,
        "mem": mem,
        "positions": positions,
        "norm_g_l0": gain(ks[3], D_MODEL),
        "w_in_l0": w(ks[4], (D_MODEL, MLA_IN), D_MODEL),
        "q_norm_g_l0": gain(ks[5], Q_LORA),
        "kv_norm_g_l0": gain(ks[6], KV_LORA),
        "w_uq_l0": w(ks[7], (Q_LORA, MLA_HEADS * (QK_NOPE + QK_ROPE)), Q_LORA),
        "w_ukv_l0": w(ks[8], (KV_LORA, MLA_HEADS * (QK_NOPE + V_HEAD)), KV_LORA),
        "mem_norm_g_l0": gain(ks[9], D_MODEL),
        "w_mem_kv_l0": w(ks[10], (D_MODEL, 2 * MEM_WIDTH), D_MODEL),
        "w_out_l0": w(ks[11], (MIX_WIDTH, D_MODEL), MIX_WIDTH),
        "norm_g_l1": gain(ks[12], D_MODEL),
        "w_in_l1": w(ks[13], (D_MODEL, FNET_IN), D_MODEL),
        "w_fnet_l1": w(ks[14], (FNET_GROUPS, FNET_GROUP_DIM, FNET_GROUP_DIM), FNET_GROUP_DIM),
        "mem_norm_g_l1": gain(ks[15], D_MODEL),
        "w_mem_kv_l1": w(ks[16], (D_MODEL, 2 * MEM_WIDTH), D_MODEL),
        "w_out_l1": w(ks[17], (MIX_WIDTH, D_MODEL), MIX_WIDTH),
        "final_norm_g": gain(ks[18], D_MODEL),
    }

def second_block(x, mem, positions,
              norm_g_l0, w_in_l0, q_norm_g_l0, kv_norm_g_l0, w_uq_l0, w_ukv_l0,
              mem_norm_g_l0, w_mem_kv_l0, w_out_l0,
              norm_g_l1, w_in_l1, w_fnet_l1, mem_norm_g_l1, w_mem_kv_l1, w_out_l1,
              final_norm_g):
    cos, sin = rope_tables(positions)
    for i in range(DEPTH_2):
        if i % N_MIXERS == 0:
            x = mla_layer(x, mem, cos, sin, norm_g_l0, w_in_l0, q_norm_g_l0, kv_norm_g_l0,
                          w_uq_l0, w_ukv_l0, mem_norm_g_l0, w_mem_kv_l0, w_out_l0)
        else:
            x = fnet_layer(x, mem, norm_g_l1, w_in_l1, w_fnet_l1,
                           mem_norm_g_l1, w_mem_kv_l1, w_out_l1)
    return rmsnorm_2(x, final_norm_g)


def setup_inputs(seed=0):
    out = dict(first_inputs(seed))
    for name, value in second_inputs(seed + 1).items():
        if name != "x":
            out[name + "_2"] = value
    return out


def reference(
    x, c, a_mod_w, a_mod_b, a_norm_g, a_w_in, a_conv_w, a_w_out, kv_mod_w, kv_mod_b, kv_norm_g,
    w_kv, b_mod_w, b_mod_b, b_norm_g, b_w_qz, b_w_out, final_norm_g, mem_2, positions_2,
    norm_g_l0_2, w_in_l0_2, q_norm_g_l0_2, kv_norm_g_l0_2, w_uq_l0_2, w_ukv_l0_2,
    mem_norm_g_l0_2, w_mem_kv_l0_2, w_out_l0_2, norm_g_l1_2, w_in_l1_2, w_fnet_l1_2,
    mem_norm_g_l1_2, w_mem_kv_l1_2, w_out_l1_2, final_norm_g_2,
):
    x = first_block(
        x, c, a_mod_w, a_mod_b, a_norm_g, a_w_in, a_conv_w, a_w_out, kv_mod_w, kv_mod_b,
        kv_norm_g, w_kv, b_mod_w, b_mod_b, b_norm_g, b_w_qz, b_w_out, final_norm_g,
    )
    return second_block(
        x, mem_2, positions_2, norm_g_l0_2, w_in_l0_2, q_norm_g_l0_2, kv_norm_g_l0_2, w_uq_l0_2,
        w_ukv_l0_2, mem_norm_g_l0_2, w_mem_kv_l0_2, w_out_l0_2, norm_g_l1_2, w_in_l1_2,
        w_fnet_l1_2, mem_norm_g_l1_2, w_mem_kv_l1_2, w_out_l1_2, final_norm_g_2,
    )


_drawn_inputs = setup_inputs


def setup_inputs(seed=0):
    import zlib

    import numpy as np

    out = dict(_drawn_inputs(seed))
    spreads = {}
    factors = {'a_mod_b': 3.899,
     'a_norm_g': 3.713,
     'kv_mod_b': 8.0,
     'kv_norm_g': 8.0,
     'b_mod_b': 8.0,
     'b_norm_g': 8.0,
     'final_norm_g': 2.879,
     'norm_g_l0_2': 8.0,
     'q_norm_g_l0_2': 8.0,
     'kv_norm_g_l0_2': 8.0,
     'mem_norm_g_l0_2': 8.0,
     'final_norm_g_2': 2.791}
    for name, (base, spread) in spreads.items():
        noise = np.random.default_rng([zlib.crc32(name.encode()), seed]).standard_normal(out[name].shape)
        drawn = base * np.exp(spread * noise) if base else spread * noise
        out[name] = __import__('jax').numpy.asarray(drawn.astype(out[name].dtype))
    for name, factor in factors.items():
        out[name] = (out[name] * factor).astype(out[name].dtype)
    return out
```

```python
import math
from contextlib import ExitStack

import numpy as np
import concourse.bass as bass
import concourse.mybir as mybir

F32 = mybir.dt.float32
F32R = mybir.dt.float32r
I32 = mybir.dt.int32
ALU = mybir.AluOpType
ACT = mybir.ActivationFunctionType
AX = mybir.AxisListType

P = 128
D = 1024
KT = D // P
TOK = 1024
HALF = 512
EPS = 1e-6
HEAD = 64
SB_HEADS = 16
MLA_HEADS = 12
ROPE = 32
RH = ROPE // 2
MEM_HEADS = 4
N_MEM = 256
Q_LORA_T = 3
KV_LORA_T = 2
GATE0 = 8
L0_COLS = [0, 128, 256, 384, 512, 640, 672, 800] + [928 + P * j for j in range(8)]

STAGES = [("a_in", 32), ("a_out", 8), ("kv", 16), ("qz", 16), ("b_out", 8), ("l0", 16),
          ("uq", 9), ("ukv", 12), ("mem", 4), ("l0_out", 8)]
FIRST = {}
_n = 0
for _name, _count in STAGES:
    FIRST[_name] = _n
    _n += _count
CHUNKS = _n
COUNT = dict(STAGES)
KTILES = {"uq": Q_LORA_T, "ukv": KV_LORA_T}

VECTORS = [("c", 8), ("a_b", 24), ("kv_b", 16), ("b_b", 24), ("a_g", 8), ("kv_g", 8), ("b_g", 8),
           ("f1_g", 8), ("l0_g", 8), ("q_g", 3), ("ckv_g", 2), ("mem_g", 8), ("f2_g", 8),
           ("conv", 24), ("freq", 1)]
COL = {}
_n = 0
for _name, _count in VECTORS:
    COL[_name] = _n
    _n += _count
NVEC = _n

TWO_PI = 2.0 * math.pi
C1 = 6.28125
C2 = float(np.float32(np.round((TWO_PI - C1) * 2.0 ** 23) / 2.0 ** 23))
C3 = TWO_PI - C1 - C2
MAGIC = 1.5 * 2.0 ** 23
PI_F = float(np.nextafter(np.float32(math.pi), np.float32(0)))

SLOT_W = TOK + 4


LOOP = True


def repeat(eng, first, end, body):
    if LOOP and end - first > 1:
        with eng.Fori(first, end) as i:
            body(i)
    else:
        for i in range(first, end):
            body(i)


def build(nc, wall, vecs, xT, mod_a, mod_rest, pos, memT, out):
    ctx = ExitStack()

    def sb(name, shape, dt=F32):
        return ctx.enter_context(nc.sbuf_tensor(name, shape, dt))

    def sem(name):
        return ctx.enter_context(nc.semaphore(name))

    def dram(name, shape):
        return nc.dram_tensor(name, shape, F32, kind="Internal").ap()
    y_d = dram("y_d", [KT, P, TOK])
    kv_d = dram("kv_d", [2 * D, TOK])
    qz_d = dram("qz_d", [2 * D, TOK])
    o_d = dram("o_d", [D, TOK])
    l0_d = dram("l0_d", [16 * P, TOK])
    q2_d = dram("q2_d", [9 * P, TOK])
    qr_d = dram("qr_d", [2, MLA_HEADS * RH, TOK])
    kr_d = dram("kr_d", [ROPE, TOK])
    kv2_d = dram("kv2_d", [MLA_HEADS * P, TOK])
    mkv_d = dram("mkv_d", [4 * P, N_MEM])
    br_d = dram("br_d", [D, TOK])
    cs_d = dram("cs_d", [2, 6 * RH, TOK])

    with ctx:
        R = sb("R", [P, KT * TOK])
        HH = sb("HH", [P, KT * TOK], F32R)
        HL = sb("HL", [P, KT * TOK], F32R)
        WST = sb("WST", [P, 2, D])
        WH = sb("WH", [P, 2, D], F32R)
        WL = sb("WL", [P, 2, D], F32R)
        ACC = sb("ACC", [P, 6, TOK])
        XS = sb("XS", [P, 3, TOK])
        SC = sb("SC", [P, 4, SLOT_W])
        QH = sb("QH", [P, 2, TOK], F32R)
        QL = sb("QL", [P, 2, TOK], F32R)
        VV = sb("VV", [P, TOK], F32R)
        VS = sb("VS", [P, 2, TOK], F32R)
        IDF = sb("IDF", [P, P])
        IDR = sb("IDR", [P, P], F32R)
        ONE = sb("ONE", [P, P])
        LATER = sb("LATER", [P, P])
        VEC = sb("VEC", [P, NVEC])
        CS = sb("CS", [P, KT])
        MOD = sb("MOD", [P, 64])
        GS = sb("GS", [P, 24])
        SM = sb("SM", [P, 4, 8])
        COLS = sb("COLS", [P, 8, 4])

        PS = ctx.enter_context(nc.psum_tensor("PS", [P, 8, HALF], F32))

        vec_loaded = sem("vec_loaded")
        w_hi = sem("w_hi")
        w_lo = sem("w_lo")
        chunk_done = sem("chunk_done")
        psum_freed = sem("psum_freed")
        consts = sem("consts")
        consts_r = sem("consts_r")
        silu_c = sem("silu_c")
        mod_acc = sem("mod_acc")
        acc_clear = sem("acc_clear")
        mod_mm = sem("mod_mm")
        mod_ready = sem("mod_ready")
        sq_done = sem("sq_done")
        acc_done = sem("acc_done")
        stat_mm = sem("stat_mm")
        stat_dve = sem("stat_dve")
        stat_act = sem("stat_act")
        t_ready = sem("t_ready")
        hi_ready = sem("hi_ready")
        h_ready = sem("h_ready")
        y_ready = sem("y_ready")
        y_stored = sem("y_stored")
        conv_seq = sem("conv_seq")
        tab_seq = sem("tab_seq")
        tab_stored = sem("tab_stored")
        sin_done = sem("sin_done")
        rope_seq = sem("rope_seq")
        cs_loaded = sem("cs_loaded")
        mem_loaded = sem("mem_loaded")
        qk_hi = sem("qk_hi")
        qk_lo = sem("qk_lo")
        s_done = sem("s_done")
        m_done = sem("m_done")
        nb_done = sem("nb_done")
        e_done = sem("e_done")
        rc_done = sem("rc_done")
        p_done = sem("p_done")
        scan_done = sem("scan_done")
        tr_done = sem("tr_done")
        th_done = sem("th_done")
        tl_done = sem("tl_done")
        av_done = sem("av_done")
        ob_done = sem("ob_done")
        oo_done = sem("oo_done")
        out_ready = sem("out_ready")
        x_loaded = [sem(f"x_loaded{i}") for i in range(8)]
        w_loaded = [sem(f"w_loaded{i}") for i in range(2)]
        xs_loaded = [sem(f"xs_loaded{i}") for i in range(3)]
        gate_loaded = [sem(f"gate_loaded{i}") for i in range(2)]
        es_stored = [sem(f"es_stored{i}") for i in range(2)]
        rope_stored = [sem(f"rope_stored{i}") for i in range(2)]
        o_stored = [sem(f"o_stored{i}") for i in range(2)]
        out_stored = [sem(f"out_stored{i}") for i in range(4)]

        def rk(k):
            return R[:, bass.ds(k * TOK, TOK)]

        def hk(h, k, n=TOK):
            return h[:, k * TOK:k * TOK + n]

        def two(ap):
            return ap.rearrange("p (a b) -> p a b", a=2)

        def chunk_psum(par, ntok=TOK):
            return PS[:, 2 * par:2 * par + 2, :] if ntok == TOK else PS[:, 2 * par, 0:ntok]

        def like(ap, ntok=TOK):
            return two(ap) if ntok == TOK else ap

        def vcol(name, k=0, n=1):
            return VEC[:, COL[name] + k:COL[name] + k + n]

        def work(s, n=TOK):
            return SC[:, s, 0:n]

        def xs(s, n=TOK, rows=P):
            return XS[0:rows, s, 0:n]

        def tiles(t):
            return t.rearrange("(m p) n -> m p n", p=P)

        def mem_tile(k):
            return ACC[:, 4 + k // 4, (k % 4) * N_MEM:(k % 4 + 1) * N_MEM]

        def wall_at(g):
            return wall[bass.ds(g, 1)].rearrange("a p n -> (a p) n")

        XSN = {}
        at = [0, 0, 0]

        def plan(stage, slots, dmas=None):
            for n, s in enumerate(slots):
                at[s] += 16 * (dmas[n] if dmas else 1)
                XSN[stage, n] = (s, at[s])

        plan("mod_a", [n % 3 for n in range(16)])
        plan("pos", [0])
        plan("mod_rest", [(n + 1) % 3 for n in range(48)])
        plan("y", [k % 3 for k in range(8)])
        plan("sb", [0, 1, 2] * SB_HEADS, [2, 2, 2] * SB_HEADS)
        plan("bo", [k % 3 for k in range(8)])
        plan("uq", [0, 1, 2])
        plan("rope", [0, 1] * 3)
        plan("ukv", [0, 1])
        plan("mla", [0, 1, 2] * MLA_HEADS, [3, 2, 2] * MLA_HEADS)
        plan("memory", [0, 1, 2] * MEM_HEADS, [2, 2, 2] * MEM_HEADS)
        plan("lo", [k % 3 for k in range(8)])

        def xs_count(stage, n0, per, i):
            s, c = XSN[stage, n0]
            if (stage, n0 + per) not in XSN:
                return s, c
            return s, c + (XSN[stage, n0 + per][1] - c) * i

        H0, hb = {}, 0
        for name, kts in [("a_in", 8), ("a_out", 8), ("kv", 8), ("qz", 8), ("b_out", 8), ("l0", 8),
                          ("uq", 3), ("ukv", 2), ("mem", 8), ("l0_out", 8)]:
            H0[name] = hb
            hb += kts
        T0, tb = {}, 0
        for name, kts in [("a_in", 8), ("kv", 8), ("qz", 8), ("b_out", 8), ("x3", 8), ("l0", 8),
                          ("uq", 3), ("ukv", 2), ("mem", 8), ("l0_out", 8)]:
            T0[name] = tb
            tb += kts
        SQ, STAT, sq = {}, {}, 0
        for n, (name, c) in enumerate([("a_in", 8), ("kv", 8), ("x3", 8), ("l0", 8), ("uq", 3),
                                       ("ukv", 2), ("mem", 8), ("final", 8)]):
            SQ[name], STAT[name] = (sq, c, sq + n), n
            sq += c
        ES0, es = {}, [0, 0]
        for name in ("kv", "qz", "l0", "uq", "ukv", "mem"):
            ES0[name] = tuple(es)
            for m in range(COUNT[name]):
                es[m % 2] += 16
        ES_END = tuple(es)
        G0 = {"b_out": 0, "l0_out": 64}
        TABLE_STEPS = 18
        ROPE_STEPS = 6

        class Pass:

            def __init__(self, name, heads, rows, causal, scale, nk):
                self.name, self.heads, self.rows, self.causal = name, heads, rows, causal
                self.scale, self.nk, self.stacked = scale, nk, rows == HEAD
                self.nkt = [(t + 1 if causal else nk // P) for t in range(8)]
                self.halves = [(n + 3) // 4 for n in self.nkt]
                self.vsteps = (nk // P + 3) // 4
                self.before = [sum(self.halves[:t]) for t in range(8)]
                self.per = sum(self.halves)
                self.s_ahead = 3
                self.e_ahead = 3 if causal else 2
                self.p_ahead = 2 if causal else 1

        sbk = Pass("sb", SB_HEADS, HEAD, True, 1.0 / math.sqrt(HEAD), TOK)
        mla = Pass("mla", MLA_HEADS, HEAD + ROPE, False, 1.0 / math.sqrt(HEAD + ROPE), TOK)
        mmx = Pass("memory", MEM_HEADS, HEAD, False, 1.0 / math.sqrt(HEAD), N_MEM)
        heads = th = tl = soft = 0
        for a in (sbk, mla, mmx):
            a.head0, a.th0, a.tl0, a.soft0 = heads, th, tl, soft
            heads += a.heads
            th += a.heads * a.per
            tl += a.heads * (a.per + a.vsteps)
            soft += 0 if a.causal else 8 * a.heads

        def th_count(a, h, t, half):
            return a.th0 + h * a.per + a.before[t] + half + 1

        def tl_count(a, h, t, half, last=False):
            n = a.tl0 + h * (a.per + a.vsteps) + a.vsteps + a.before[t] + half + 1
            return n + (a.vsteps if t == 7 and not last else 0)

        def v_count(a, h, step, first=False):
            if first:
                return a.tl0 + step + 1
            return a.tl0 + (h - 1) * (a.per + a.vsteps) + a.vsteps + a.before[7] + step + 1

        def heads_of(eng, a, body):
            body(0, 0, True, False)
            body(1, 1, False, False)

            def pair(i):
                for j in range(2):
                    body(2 * i + j, j, False, False)
            repeat(eng, 1, a.heads // 2 - 1, pair)
            body(a.heads - 2, 0, False, False)
            body(a.heads - 1, 1, False, True)

        def keys_by_queries(H, a, t, half):
            lo, hi = 4 * half, min(a.nkt[t], 4 * half + 4)
            hf, q = t // 4, (t % 4) * P
            v = H[:, 4096 * hf:4096 * hf + 4096].rearrange("p (k q) -> p k q", q=HALF)
            return v[:, lo:hi, q:q + P], hi - lo

        def v_parity(a, step, j, first=False):
            if first:
                return (a.tl0 + step) % 2
            odd = (a.per + a.vsteps) % 2
            return (a.tl0 + odd * (1 - j) + a.vsteps + a.before[7] + step) % 2

        def parity(a, t, half, j=0, last=False):
            odd = (a.per + a.vsteps) % 2
            extra = a.vsteps if t == 7 and not last else 0
            return (a.tl0 + odd * j + a.vsteps + a.before[t] + half + extra) % 2

        block = ctx.enter_context(nc.Block())

        @block.sync
        def _(sp):
            def xs_load(slot, dst, src):
                sp.dma_start(dst, src).then_inc(xs_loaded[slot], 16)

            def load_chunk(g, par):
                sp.wait_ge(w_lo, g - 1)
                sp.dma_start(WST[:, par, :], wall_at(g)).then_inc(w_loaded[par], 16)

            def stream(first, end):
                if (end - first) % 2:
                    load_chunk(first, first % 2)
                    first += 1

                def pair(i):
                    for j in range(2):
                        load_chunk(first + 2 * i + j, (first + j) % 2)
                repeat(sp, 0, (end - first) // 2, pair)

            sp.dma_start(VEC[:], vecs).then_inc(vec_loaded, 16)
            for n in range(16):
                if n >= 3:
                    sp.wait_ge(mod_acc, n - 2)
                xs_load(n % 3, xs(n % 3), mod_a[n])
                if n % 2:
                    sp.dma_start(rk(n // 2), xT[n // 2]).then_inc(x_loaded[n // 2], 16)
            for g in range(2):
                sp.dma_start(WST[:, g, :], wall_at(g)).then_inc(w_loaded[g], 16)
            sp.wait_ge(h_ready, 8)
            sp.dma_start(XS[0:6 * RH, 0, :].bitcast(I32), pos.to_broadcast([6 * RH, TOK]))\
                .then_inc(xs_loaded[0], 16)
            sp.wait_ge(tab_seq, 1)

            def a_in(c, first):
                def mod_tile(i):
                    slot, _ = XSN["mod_rest", i]
                    if first and i < 3:
                        sp.wait_ge(tab_stored, 32)
                    else:
                        sp.wait_ge(mod_acc, 16 + 6 * c + i - 2)
                    xs_load(slot, xs(slot),
                            mod_rest[bass.ds(6 * c + i, 1)].rearrange("a p n -> (a p) n"))
                for i in range(4):
                    load_chunk(4 * c + i + 2, i % 2)
                    if i == 1 and not first:
                        sp.wait_ge(y_ready, c)
                        sp.dma_start(y_d[bass.ds(c - 1, 1)].rearrange("a p n -> (a p) n"), work(2))\
                            .then_inc(y_stored, 16)
                    if i < 3:
                        mod_tile(2 * i)
                        mod_tile(2 * i + 1)
            a_in(0, True)
            repeat(sp, 1, 8, lambda c: a_in(c, False))
            sp.wait_ge(y_ready, 8)
            sp.dma_start(y_d[7], work(2)).then_inc(y_stored, 16)
            sp.wait_ge(y_stored, 16 * 8)
            for k in range(8):
                if k < 3:
                    sp.wait_ge(mod_acc, 16 + 48)
                else:
                    sp.wait_ge(h_ready, H0["a_out"] + k - 2)
                xs_load(k % 3, xs(k % 3), y_d[k])
            stream(FIRST["a_out"] + 2, FIRST["b_out"] + 2)

            def rows(t, r, n):
                return t[bass.ds(r, n), :]

            def load_head(a, h):
                g = 3 * (a.head0 + h)
                sp.wait_ge(qk_lo, g - 2 if not (isinstance(h, int) and h == 0) else g)
                if a is mla:
                    xs_load(0, XS[0:HEAD, 0, :], rows(q2_d, HEAD * h, HEAD))
                    for s in range(2):
                        xs_load(0, XS[HEAD + RH * s:HEAD + RH * s + RH, 0, :],
                                rows(qr_d[s], RH * h, RH))
                else:
                    for s in range(2):
                        xs_load(0, XS[HEAD * s:HEAD * s + HEAD, 0, :],
                                rows(qz_d, HEAD * h, HEAD) if a is sbk else
                                rows(l0_d, 6 * P + HEAD * h, HEAD))
                sp.wait_ge(qk_lo, g - 1 if not (isinstance(h, int) and h == 0) else g)
                if a is mla:
                    xs_load(1, XS[0:HEAD, 1, :], rows(kv2_d, P * h, HEAD))
                    xs_load(1, XS[HEAD:HEAD + ROPE, 1, :], kr_d)
                else:
                    for s in range(2):
                        xs_load(1, XS[HEAD * s:HEAD * s + HEAD, 1, 0:a.nk],
                                rows(kv_d if a is sbk else mkv_d, HEAD * h, HEAD))
                sp.wait_ge(qk_lo, g)
                for s in range(2):
                    src = rows(kv_d, D + HEAD * h, HEAD) if a is sbk else (
                        rows(kv2_d, P * h + HEAD, HEAD) if a is mla else
                        rows(mkv_d, MEM_HEADS * HEAD + HEAD * h, HEAD))
                    xs_load(2, XS[HEAD * s:HEAD * s + HEAD, 2, 0:a.nk], src)

            def store_out(a, h, hf, row0, dst):
                sp.wait_ge(oo_done, 2 * (a.head0 + h) + hf + 1)
                sp.dma_start(dst[bass.ds(row0 + HEAD * h, HEAD), hf * HALF:(hf + 1) * HALF],
                             ACC[0:HEAD, 2 + hf, 0:HALF]).then_inc(o_stored[hf], 16)

            def attend(a, dst, row0):
                load_head(a, 0)

                def head(h, j, first, last):
                    if not last:
                        load_head(a, h + 1)
                    if not first:
                        store_out(a, h - 1, 1, row0, dst)
                    store_out(a, h, 0, row0, dst)
                heads_of(sp, a, head)
                store_out(a, a.heads - 1, 1, row0, dst)

            def load_product(stage, name, product, gate0, gate_d, stored):
                for s in range(2):
                    sp.wait_ge(o_stored[s], 16 * stored)
                for k in range(8):
                    if k >= 2:
                        sp.wait_ge(t_ready, T0[name] + k - 1)
                    sp.dma_start(work(k % 2), gate_d[gate0 + k]).then_inc(gate_loaded[k % 2], 16)
                    if k >= 3:
                        sp.wait_ge(h_ready, H0[name] + k - 2)
                    xs_load(k % 3, xs(k % 3), product[k * P:(k + 1) * P, :])

            for s in range(2):
                sp.wait_ge(es_stored[s], ES0["l0"][s])
            attend(sbk, o_d, 0)
            load_product("bo", "b_out", o_d, KT, tiles(qz_d), SB_HEADS)
            stream(FIRST["b_out"] + 2, FIRST["uq"] + 2)

            for s in range(2):
                sp.wait_ge(es_stored[s], ES0["uq"][s])
            for k in range(Q_LORA_T):
                xs_load(k, xs(k), l0_d[k * P:(k + 1) * P, :])
            sp.dma_start(ACC[:, 4:6, :].rearrange("p a b -> p (a b)"), memT).then_inc(mem_loaded, 16)
            stream(FIRST["uq"] + 2, FIRST["ukv"] + 2)
            for s in range(2):
                sp.wait_ge(es_stored[s], ES0["ukv"][s])
                sp.dma_start(SC[0:6 * RH, s, 0:TOK], cs_d[s]).then_inc(cs_loaded, 16)
            qrope = q2_d[MLA_HEADS * HEAD:MLA_HEADS * (HEAD + ROPE), :]
            for b in range(3):
                n = RH if b == 2 else 6 * RH
                src = l0_d[5 * P:5 * P + ROPE, :] if b == 2 else None
                if b:
                    sp.wait_ge(rope_seq, ROPE_STEPS * b)
                for s in range(2):
                    r0 = MLA_HEADS * RH * s + 6 * RH * b
                    xs_load(s, XS[0:n, s, :], src[RH * s:RH * s + RH, :] if b == 2 else
                            qrope[r0:r0 + n, :])
                for s in range(2):
                    sp.wait_ge(rope_seq, ROPE_STEPS * b + 3 * s + 3)
                    dst = kr_d[RH * s:RH * s + RH, :] if b == 2 else \
                        qr_d[s][6 * RH * b:6 * RH * b + n, :]
                    sp.dma_start(dst, SC[0:n, 2 + s, 0:TOK]).then_inc(rope_stored[s], 16)
            for k in range(KV_LORA_T):
                if k == 0:
                    sp.wait_ge(rope_seq, ROPE_STEPS * 3)
                xs_load(k, xs(k), l0_d[(3 + k) * P:(4 + k) * P, :])
            stream(FIRST["ukv"] + 2, FIRST["l0_out"] + 2)

            for s in range(2):
                sp.wait_ge(es_stored[s], ES_END[s])
                sp.wait_ge(rope_stored[s], 48)
            attend(mla, br_d, 0)
            attend(mmx, br_d, MLA_HEADS * HEAD)
            load_product("lo", "l0_out", br_d, GATE0, tiles(l0_d),
                         SB_HEADS + MLA_HEADS + MEM_HEADS)
            stream(FIRST["l0_out"] + 2, CHUNKS)
            for k in range(8):
                sp.wait_ge(out_ready, k + 1)
                sp.dma_start(out[k], work(k % 4)).then_inc(out_stored[k % 4], 16)
            for s in range(4):
                sp.wait_ge(out_stored[s], 32)

        @block.gpsimd
        def _(pool):
            gp = nc.gpsimd
            gp.memset(ONE[:], 1.0).then_inc(consts, 1)
            gp.memset(IDF[:], 0.0).then_inc(consts, 1)
            pool.wait_ge(consts, 2)
            gp.affine_select(out=IDF[:], in_=IDF[:], compare_op=ALU.not_equal, fill=1.0, base=0,
                             pattern=[[-1, P]], channel_multiplier=1).then_inc(consts, 1)
            gp.affine_select(out=LATER[:], in_=ONE[:], compare_op=ALU.is_ge, fill=0.0, base=0,
                             pattern=[[1, P]], channel_multiplier=-1).then_inc(consts, 1)

            def lo_chunk(g, par):
                pool.wait_ge(w_hi, g + 1)
                gp.tensor_tensor(WL[:, par, :], WST[:, par, :], WH[:, par, :].bitcast(F32),
                                 ALU.subtract).then_inc(w_lo, 1)

            def lo_chunks(first, end):
                if (end - first) % 2:
                    lo_chunk(first, first % 2)
                    first += 1

                def pair(i):
                    for j in range(2):
                        lo_chunk(first + 2 * i + j, (first + j) % 2)
                repeat(pool, 0, (end - first) // 2, pair)

            def lo_head(a, h, j):
                g = 3 * (a.head0 + h)
                pool.wait_ge(qk_lo, g)
                pool.wait_ge(qk_hi, g + 1)
                if a.stacked:
                    q = QH[HEAD:P, j, :]
                    gp.tensor_tensor(q, XS[HEAD:P, 0, :], q.bitcast(F32), ALU.subtract)\
                        .then_inc(qk_lo, 1)
                else:
                    gp.tensor_tensor(QL[0:a.rows, j, :], XS[0:a.rows, 0, :],
                                     QH[0:a.rows, j, :].bitcast(F32), ALU.subtract)\
                        .then_inc(qk_lo, 1)
                pool.wait_ge(qk_lo, g + 1)
                pool.wait_ge(qk_hi, g + 2)
                r = P if a.stacked else a.rows
                gp.tensor_tensor(WL[0:r, j, 0:a.nk], XS[0:r, 1, 0:a.nk],
                                 WH[0:r, j, 0:a.nk].bitcast(F32), ALU.subtract).then_inc(qk_lo, 1)
                pool.wait_ge(qk_lo, g + 2)
                pool.wait_ge(qk_hi, g + 3)
                v = VV[HEAD:P, 0:a.nk]
                gp.tensor_tensor(v, XS[HEAD:P, 2, 0:a.nk], v.bitcast(F32), ALU.subtract)\
                    .then_inc(qk_lo, 1)

            lo_chunks(0, FIRST["b_out"])
            pool.wait_ge(w_lo, FIRST["b_out"])
            def lo_heads(a):
                lo_head(a, 0, 0)
                heads_of(pool, a, lambda h, j, first, last:
                         None if last else lo_head(a, h + 1, 1 - j))
            lo_heads(sbk)
            pool.wait_ge(qk_lo, 3 * SB_HEADS)
            lo_chunks(FIRST["b_out"], FIRST["l0_out"])
            pool.wait_ge(w_lo, FIRST["l0_out"])
            lo_heads(mla)
            lo_heads(mmx)
            pool.wait_ge(qk_lo, 3 * (SB_HEADS + MLA_HEADS + MEM_HEADS))
            lo_chunks(FIRST["l0_out"], CHUNKS)

        @block.scalar
        def _(act):
            sc = nc.scalar

            def stage(name, bodies, round_next=True):
                g0, n = FIRST[name], COUNT[name]

                def step(body, m, j, half, last):
                    g, par = g0 + m, (g0 + j) % 2
                    if round_next or not last:
                        act.wait_ge(w_loaded[1 - par], 16 * (half + par + 1))
                        act.wait_ge(chunk_done, g)
                        sc.activation(WH[:, 1 - par, :], WST[:, 1 - par, :], ACT.Copy)\
                            .then_inc(w_hi, 1)
                    body(m, j, g, par)

                begin = 0
                for end, body in bodies:
                    def pair(i, last=False):
                        for j in range(2):
                            step(body, 2 * i + j, j, (g0 + j) // 2 + i, last and j == 1)
                    pairs = end // 2
                    tail = end == n and n % 2 == 0
                    if begin == 0:
                        pair(0)
                        begin = 1
                    repeat(act, begin, pairs - tail, pair)
                    if tail:
                        pair(pairs - 1, True)
                    begin = pairs
                if n % 2:
                    step(body, n - 1, 0, (g0 + n - 1) // 2, True)

            def first_chunk(g):
                act.wait_ge(w_loaded[g % 2], 16 * (g // 2 + 1))
                sc.activation(WH[:, g % 2, :], WST[:, g % 2, :], ACT.Copy).then_inc(w_hi, 1)

            def store_chunk(name, dst, func=ACT.Copy, ntok=TOK):
                def body(m, j, g, par):
                    act.wait_ge(chunk_done, g + 1)
                    act.wait_ge(es_stored[j], ES0[name][j] + 8 * (m - j))
                    sc.activation(like(work(j, ntok), ntok), chunk_psum(par, ntok), func)\
                        .then_inc(psum_freed, 1)
                    act.wait_ge(psum_freed, g + 1)
                    act.dma_start(dst[bass.ds(m, 1)].rearrange("a p n -> (a p) n"),
                                  work(j, ntok)).then_inc(es_stored[j], 16)
                return body

            def squares(name, k, src, ntok=TOK):
                act.wait_ge(acc_done, SQ[name][2] + k)
                sc.activation(work(k % 2, ntok), src, ACT.Square).then_inc(sq_done, 1)

            def rstd(name):
                act.wait_ge(stat_dve, 2 * STAT[name] + 2)
                sc.activation(SM[:, 2, :], SM[:, 1, :], ACT.Sqrt).then_inc(stat_act, 1)

            def hi_tiles(name, kts, src, shift=None, ntok=TOK, xs_stage=None, t_wait=True):
                for k in range(kts):
                    if t_wait:
                        act.wait_ge(t_ready, T0[name] + k + 1)
                    else:
                        s, c = XSN[xs_stage, k]
                        act.wait_ge(xs_loaded[s], c)
                    if k == 0:
                        act.wait_ge(chunk_done, FIRST[name])
                    if shift is None:
                        sc.activation(hk(HH, k, ntok), src(k), ACT.Copy).then_inc(hi_ready, 1)
                    else:
                        sc.activation(hk(HH, k, ntok), src(k), ACT.Identity, bias=shift(k))\
                            .then_inc(hi_ready, 1)

            act.wait_ge(vec_loaded, 16)
            sc.activation(CS[:], vcol("c", 0, 8), ACT.Silu).then_inc(silu_c, 1)
            for k in range(8):
                act.wait_ge(x_loaded[k], 16)
                squares("a_in", k, rk(k))
            rstd("a_in")
            first_chunk(0)
            hi_tiles("a_in", 8, lambda k: xs(k % 3), lambda k: MOD[:, k:k + 1])
            for n in range(2):
                act.wait_ge(tab_seq, 2 + 7 * (n + 1))
                sc.activation(XS[0:6 * RH, 1 + n, :], SC[0:6 * RH, 3, 0:TOK], ACT.Sin)\
                    .then_inc(sin_done, 1)
                act.wait_ge(sin_done, n + 1)
                act.dma_start(cs_d[1 - n], XS[0:6 * RH, 1 + n, :]).then_inc(tab_stored, 16)

            def a_in(c):
                for i in range(4):
                    g, par = 4 * c + i, i % 2
                    act.wait_ge(w_loaded[1 - par], 16 * (2 * c + (i + 1) // 2 + 1))
                    act.wait_ge(chunk_done, g)
                    sc.activation(WH[:, 1 - par, :], WST[:, 1 - par, :], ACT.Copy).then_inc(w_hi, 1)
                    if i == 0:
                        act.wait_ge(chunk_done, g + 1)
                        sc.activation(two(work(0)), chunk_psum(par), ACT.Copy)\
                            .then_inc(psum_freed, 1)
                    if i == 3:
                        act.wait_ge(chunk_done, g + 1)
                        act.wait_ge(psum_freed, g)
                        sc.activation(two(work(3)), chunk_psum(par), ACT.Silu)\
                            .then_inc(psum_freed, 1)
            a_in(0)
            repeat(act, 1, 8, a_in)
            hi_tiles("a_out", 8, lambda k: xs(k % 3), xs_stage="y", t_wait=False)

            def out_squares(stat):
                def body(m, j, g, par):
                    act.wait_ge(psum_freed, g + 1)
                    act.wait_ge(acc_done, SQ[stat][2] + m)
                    sc.activation(work(j), rk(m), ACT.Square).then_inc(sq_done, 1)
                return body
            stage("a_out", [(8, out_squares("kv"))])
            rstd("kv")
            hi_tiles("kv", 8, lambda k: xs(k % 3), lambda k: MOD[:, 24 + k:25 + k])
            stage("kv", [(16, store_chunk("kv", tiles(kv_d)))])
            hi_tiles("qz", 8, lambda k: xs(k % 3), lambda k: MOD[:, 40 + k:41 + k])
            stage("qz", [(8, store_chunk("qz", tiles(qz_d))),
                         (16, store_chunk("qz", tiles(qz_d), ACT.Silu))], round_next=False)

            def hi_head(a, h, j, which):
                n = 3 * h + which
                s, c = xs_count(a.name, which, 3, h)
                act.wait_ge(xs_loaded[s], c)
                if which == 2:
                    if not (isinstance(h, int) and h == 0):
                        act.wait_ge(tr_done, v_count(a, h - 1, a.vsteps - 1,
                                                     isinstance(h, int) and h == 1))
                    sc.activation(VV[:, 0:a.nk], xs(2, a.nk), ACT.Copy).then_inc(qk_hi, 1)
                    return
                if not (isinstance(h, int) and h < 2):
                    act.wait_ge(s_done, 8 * (a.head0 + h - 1))
                r = P if a.stacked else a.rows
                if which == 0:
                    sc.activation(QH[0:r, j, :], xs(0, TOK, r), ACT.Copy).then_inc(qk_hi, 1)
                else:
                    sc.activation(WH[0:r, j, 0:a.nk], xs(1, a.nk, r), ACT.Copy).then_inc(qk_hi, 1)

            def scores_in(t, n):
                if n <= HALF:
                    return PS[:, 2 * (t % 2), 0:n]
                return PS[:, 2 * (t % 2):2 * (t % 2) + 2, :].rearrange("p a b -> p (a b)")[:, 0:n]

            def prob(a, h, t):
                u = 8 * (a.head0 + h) + t
                n = a.nkt[t] * P
                if a.causal:
                    act.wait_ge(s_done, u + 1)
                    sc.activation(SC[:, t % 4, 0:n], scores_in(t, n), ACT.Sigmoid, scale=-a.scale)\
                        .then_inc(e_done, 1)
                else:
                    act.wait_ge(nb_done, a.soft0 + 8 * h + t + 1)
                    sc.activation(SC[:, t % 4, 0:n], scores_in(t, n), ACT.Exp, scale=a.scale,
                                  bias=COLS[:, t, 1:2], accum_out=COLS[:, t, 2:3])\
                        .then_inc(e_done, 1)

            def hi_tile(a, h, j, t, half, last):
                dst, n = keys_by_queries(HH, a, t, half)
                act.wait_ge(tr_done, tl_count(a, h, t, half, last))
                src = PS[:, 4 + parity(a, t, half, j, last), 0:n * P]
                sc.activation(dst, src.rearrange("p (k q) -> p k q", q=P), ACT.Copy)\
                    .then_inc(th_done, 1)

            def lower(a, h, hf):
                act.wait_ge(av_done, 2 * (a.head0 + h) + hf + 1)
                act.wait_ge(oo_done, 2 * (a.head0 + h))
                sc.activation(ACC[0:HEAD, hf, 0:HALF], PS[HEAD:P, 6 + hf, :], ACT.Copy)\
                    .then_inc(ob_done, 1)

            def attend(a):
                for w in range(3):
                    hi_head(a, 0, 0, w)
                for t in range(a.e_ahead):
                    prob(a, 0, t)

                def head(h, j, first, last):
                    for t in range(8):
                        if t == 0 and not first:
                            lower(a, h - 1, 0)
                        nxt = (h, t + a.e_ahead) if t + a.e_ahead < 8 else \
                            (h + 1, t + a.e_ahead - 8)
                        hi_tile(a, h, j, t, 0, last)
                        if t + a.e_ahead < 8 or not last:
                            prob(a, *nxt)
                        if a.halves[t] == 2:
                            hi_tile(a, h, j, t, 1, last)
                        if t == 4 and not first:
                            lower(a, h - 1, 1)
                        if t in (2, 3, 4) and not last:
                            hi_head(a, h + 1, 1 - j, t - 2)
                heads_of(act, a, head)
                for hf in range(2):
                    lower(a, a.heads - 1, hf)

            attend(sbk)
            act.wait_ge(chunk_done, FIRST["b_out"])
            first_chunk(FIRST["b_out"])
            hi_tiles("b_out", 8, lambda k: xs(k % 3))
            stage("b_out", [(8, out_squares("x3"))])
            rstd("x3")
            for k in range(8):
                act.wait_ge(t_ready, T0["x3"] + k + 1)
                squares("l0", k, rk(k))
            rstd("l0")
            hi_tiles("l0", 8, lambda k: xs(k % 3))
            stage("l0", [(8, store_chunk("l0", tiles(l0_d))),
                         (16, store_chunk("l0", tiles(l0_d), ACT.Silu))])

            for k in range(Q_LORA_T):
                s, c = XSN["uq", k]
                act.wait_ge(xs_loaded[s], c)
                squares("uq", k, xs(k))
            rstd("uq")
            hi_tiles("uq", Q_LORA_T, lambda k: xs(k))
            stage("uq", [(9, store_chunk("uq", tiles(q2_d)))])
            for k in range(KV_LORA_T):
                s, c = XSN["ukv", k]
                act.wait_ge(xs_loaded[s], c)
                if k == 0:
                    act.wait_ge(rope_seq, 3 * ROPE_STEPS)
                squares("ukv", k, xs(k))
            rstd("ukv")
            hi_tiles("ukv", KV_LORA_T, lambda k: xs(k))
            stage("ukv", [(12, store_chunk("ukv", tiles(kv2_d)))])
            act.wait_ge(mem_loaded, 16)
            for s in range(2):
                act.wait_ge(es_stored[s], ES0["mem"][s])
            for k in range(8):
                squares("mem", k, mem_tile(k), N_MEM)
            rstd("mem")
            hi_tiles("mem", 8, mem_tile, ntok=N_MEM)
            stage("mem", [(4, store_chunk("mem", tiles(mkv_d), ntok=N_MEM))], round_next=False)
            for s in range(2):
                act.wait_ge(es_stored[s], ES_END[s])
            attend(mla)
            attend(mmx)
            act.wait_ge(chunk_done, FIRST["l0_out"])
            first_chunk(FIRST["l0_out"])
            hi_tiles("l0_out", 8, lambda k: xs(k % 3))
            stage("l0_out", [(8, out_squares("final"))], round_next=False)
            rstd("final")

        @block.vector
        def _(dve):
            v = nc.vector

            def sum_clear(name):
                v.memset(work(2), 0.0).then_inc(acc_done, 1)

            def sum_add(name, m, j, ntok=TOK):
                q0, _, a0 = SQ[name]
                dve.wait_ge(sq_done, q0 + m + 1)
                dve.wait_ge(acc_done, a0 + m + 1)
                v.tensor_tensor(work(2, ntok), work(2, ntok), work(j, ntok), ALU.add)\
                    .then_inc(acc_done, 1)

            def stats(name, size, ntok=TOK):
                n, s = ntok // P, STAT[name]
                dve.wait_ge(stat_mm, 2 * s + 1)
                v.tensor_scalar(SM[:, 0, 0:n], PS[:, 4, 0:n], 1.0 / size, EPS, ALU.mult, ALU.add)\
                    .then_inc(stat_dve, 1)
                dve.wait_ge(stat_dve, 2 * s + 1)
                v.reciprocal(SM[:, 1, 0:n], SM[:, 0, 0:n]).then_inc(stat_dve, 1)
                dve.wait_ge(stat_mm, 2 * s + 2)

            def rstd_rows(ntok=TOK):
                return PS[:, 5:7, :] if ntok == TOK else PS[:, 5, 0:ntok]

            def normed(name, kts, src, tmp, gain, shift=None, ntok=TOK):
                def scaled(k):
                    if H0[name] + k >= 3:
                        dve.wait_ge(h_ready, H0[name] + max(0, k - 2))
                    v.scalar_tensor_tensor(out=like(tmp(k), ntok), in0=like(src(k), ntok),
                                           scalar=gain(k), in1=rstd_rows(ntok), op0=ALU.mult,
                                           op1=ALU.mult).then_inc(t_ready, 1)
                for k in range(min(2, kts)):
                    scaled(k)
                for k in range(kts):
                    dve.wait_ge(hi_ready, H0[name] + k + 1)
                    if shift is None:
                        v.tensor_tensor(hk(HL, k, ntok), tmp(k), hk(HH, k, ntok).bitcast(F32),
                                        ALU.subtract).then_inc(h_ready, 1)
                    else:
                        v.scalar_tensor_tensor(out=hk(HL, k), in0=tmp(k), scalar=shift(k),
                                               in1=hk(HH, k).bitcast(F32), op0=ALU.add,
                                               op1=ALU.subtract).then_inc(h_ready, 1)
                    if k + 2 < kts:
                        scaled(k + 2)

            def mod_add(n, grp, kt, slot, count, first):
                dve.wait_ge(xs_loaded[slot], count)
                if first:
                    dve.wait_ge(acc_clear, 1 if isinstance(n, int) and n < 16 else 2)
                else:
                    dve.wait_ge(mod_acc, n - (1 if isinstance(n, int) and n < 16 else 5))
                v.scalar_tensor_tensor(out=ACC[:, grp, :], in0=xs(slot), scalar=kt,
                                       in1=ACC[:, grp, :], op0=ALU.mult, op1=ALU.add)\
                    .then_inc(mod_acc, 1)

            dve.wait_ge(consts, 4)
            v.tensor_copy(IDR[:], IDF[:]).then_inc(consts_r, 1)
            v.memset(ACC[:, 0:2, :], 0.0).then_inc(acc_clear, 1)
            sum_clear("a_in")
            dve.wait_ge(silu_c, 1)
            for n in range(16):
                slot, count = XSN["mod_a", n]
                mod_add(n, n % 2, CS[:, n // 2:n // 2 + 1], slot, count, n < 2)
                if n % 2:
                    sum_add("a_in", n // 2, n // 2 % 2)
            dve.wait_ge(mod_mm, 1)
            v.tensor_tensor(MOD[:, 0:16], PS[:, 7, 0:16], vcol("a_b", 0, 16), ALU.add)\
                .then_inc(mod_ready, 1)
            dve.wait_ge(mod_ready, 1)
            v.scalar_tensor_tensor(out=GS[:, 0:8], in0=MOD[:, 8:16], scalar=1.0,
                                   in1=vcol("a_g", 0, 8), op0=ALU.add, op1=ALU.mult)\
                .then_inc(mod_ready, 1)
            v.memset(ACC[:], 0.0).then_inc(acc_clear, 1)
            stats("a_in", D)
            dve.wait_ge(mod_ready, 2)
            normed("a_in", 8, rk, lambda k: xs(k % 3), lambda k: GS[:, k:k + 1],
                   lambda k: MOD[:, k:k + 1])

            rr = 6 * RH
            s_, c_ = XSN["pos", 0]
            dve.wait_ge(xs_loaded[s_], c_)
            v.tensor_copy(SC[0:rr, 0, 0:TOK], XS[0:rr, 0, :].bitcast(I32)).then_inc(tab_seq, 1)
            dve.wait_ge(tab_seq, 1)
            v.tensor_scalar(SC[0:rr, 1, 0:TOK], SC[0:rr, 0, 0:TOK], VEC[0:rr, COL["freq"]:COL["freq"] + 1],
                            None, ALU.mult).then_inc(tab_seq, 1)
            for n, turn in enumerate((0.0, 0.25)):
                ang, k_, r_ = (SC[0:rr, i, 0:TOK] for i in (1, 2, 3))
                b_ = 2 + 7 * n
                dve.wait_ge(tab_seq, b_)
                v.tensor_scalar(k_, ang, 1.0 / TWO_PI, turn, ALU.mult, ALU.add).then_inc(tab_seq, 1)
                dve.wait_ge(tab_seq, b_ + 1)
                v.tensor_scalar(k_, k_, MAGIC, MAGIC, ALU.add, ALU.subtract).then_inc(tab_seq, 1)
                dve.wait_ge(tab_seq, b_ + 2)
                if n:
                    dve.wait_ge(sin_done, 1)
                v.scalar_tensor_tensor(out=r_, in0=k_, scalar=-C1, in1=ang, op0=ALU.mult,
                                       op1=ALU.add).then_inc(tab_seq, 1)
                for i, part in enumerate((C2, C3)):
                    dve.wait_ge(tab_seq, b_ + 3 + i)
                    v.scalar_tensor_tensor(out=r_, in0=k_, scalar=-part, in1=r_, op0=ALU.mult,
                                           op1=ALU.add).then_inc(tab_seq, 1)
                dve.wait_ge(tab_seq, b_ + 5)
                v.tensor_scalar(r_, r_, turn * TWO_PI, PI_F, ALU.add, ALU.min).then_inc(tab_seq, 1)
                dve.wait_ge(tab_seq, b_ + 6)
                v.tensor_scalar(r_, r_, -PI_F, None, ALU.max).then_inc(tab_seq, 1)
            dve.wait_ge(sin_done, 2)
            v.memset(SC[:, 1, 0:2], 0.0).then_inc(acc_clear, 1)
            dve.wait_ge(acc_clear, 3)

            def a_in(c, first):
                def mods(i0):
                    for i in range(i0, i0 + 3):
                        slot, _ = XSN["mod_rest", i]
                        count = XSN["mod_rest", i][1] + 32 * c
                        mod_add(16 + 6 * c + i, i, CS[:, bass.ds(c, 1)], slot, count, first)
                cu, t = SC[:, 1, :], work(2)
                dve.wait_ge(chunk_done, 4 * c + 2)
                dve.wait_ge(psum_freed, 4 * c + 1)
                v.tensor_tensor(two(cu[:, 2:2 + TOK]), chunk_psum(1), two(work(0)), ALU.mult)\
                    .then_inc(psum_freed, 1)
                dve.wait_ge(psum_freed, 4 * c + 2)
                dve.wait_ge(y_stored, 16 * c)
                tap = lambda i: VEC[:, bass.ds(COL["conv"] + 8 * i + c, 1)]
                v.tensor_scalar(t, cu[:, 2:2 + TOK], tap(2), None, ALU.mult).then_inc(conv_seq, 1)
                for i in (1, 0):
                    dve.wait_ge(conv_seq, 3 * c + 2 - i)
                    v.scalar_tensor_tensor(out=t, in0=cu[:, i:i + TOK], scalar=tap(i), in1=t,
                                           op0=ALU.mult, op1=ALU.add).then_inc(conv_seq, 1)
                mods(0)
                dve.wait_ge(chunk_done, 4 * c + 3)
                dve.wait_ge(conv_seq, 3 * c + 3)
                v.tensor_tensor(two(t), chunk_psum(0), two(t), ALU.mult).then_inc(psum_freed, 1)
                mods(3)
                dve.wait_ge(psum_freed, 4 * c + 4)
                v.tensor_tensor(t, t, work(3), ALU.mult).then_inc(y_ready, 1)
            a_in(0, True)
            repeat(dve, 1, 8, lambda c: a_in(c, False))
            dve.wait_ge(mod_mm, 2)
            v.tensor_tensor(MOD[:, 16:64], PS[:, 7, 0:48], vcol("a_b", 16, 48), ALU.add)\
                .then_inc(mod_ready, 1)
            dve.wait_ge(mod_ready, 3)
            for at_, name, g_ in ((32, "kv_g", 8), (48, "b_g", 16)):
                v.scalar_tensor_tensor(out=GS[:, g_:g_ + 8], in0=MOD[:, at_:at_ + 8], scalar=1.0,
                                       in1=vcol(name, 0, 8), op0=ALU.add, op1=ALU.mult)\
                    .then_inc(mod_ready, 1)

            def lo_tiles(name, stage):
                for k in range(8):
                    dve.wait_ge(hi_ready, H0[name] + k + 1)
                    v.tensor_tensor(hk(HL, k), xs(k % 3), hk(HH, k).bitcast(F32), ALU.subtract)\
                        .then_inc(h_ready, 1)

            def out_chunks(name, stat, gate):
                g0, n = FIRST[name], COUNT[name]

                def pair(i):
                    for j in range(2):
                        m, par = 2 * i + j, (g0 + j) % 2
                        dve.wait_ge(chunk_done, g0 + m + 1)
                        v.scalar_tensor_tensor(out=two(rk(m)), in0=chunk_psum(par),
                                               scalar=gate(m), in1=two(rk(m)), op0=ALU.mult,
                                               op1=ALU.add).then_inc(psum_freed, 1)
                        sum_add(stat, m, j)
                repeat(dve, 0, n // 2, pair)

            lo_tiles("a_out", "y")
            sum_clear("kv")
            out_chunks("a_out", "kv", lambda m: MOD[:, bass.ds(16 + m, 1)])
            stats("kv", D)
            dve.wait_ge(mod_ready, 5)
            normed("kv", 8, rk, lambda k: xs(k % 3), lambda k: GS[:, 8 + k:9 + k],
                   lambda k: MOD[:, 24 + k:25 + k])
            normed("qz", 8, rk, lambda k: xs(k % 3), lambda k: GS[:, 16 + k:17 + k],
                   lambda k: MOD[:, 40 + k:41 + k])

            def row_max(a, h, t):
                u = 8 * (a.head0 + h) + t
                s = a.soft0 + 8 * h + t
                dve.wait_ge(s_done, u + 1)
                src = PS[:, 2 * (t % 2):2 * (t % 2) + 2, :] if a.nk > HALF else \
                    PS[:, 2 * (t % 2), 0:a.nk]
                v.reduce_max(COLS[:, t, 0:1], src, AX.XY if a.nk > HALF else AX.X)\
                    .then_inc(m_done, 1)
                dve.wait_ge(m_done, s + 1)
                v.tensor_scalar(COLS[:, t, 1:2], COLS[:, t, 0:1], -a.scale, None, ALU.mult)\
                    .then_inc(nb_done, 1)

            def probs(a, h, t):
                u = 8 * (a.head0 + h) + t
                n = a.nkt[t] * P
                if a.causal:
                    dve.wait_ge(e_done, u + 1)
                    v.memset(SC[:, t % 4, n:n + 1], 1.0).then_inc(scan_done, 1)
                    s = SC[:, t % 4, 0:n]
                    v.tensor_tensor_scan(s[:, ::-1], s[:, ::-1], ACC[:, 5, TOK - n:][:, ::-1], 1.0,
                                         ALU.mult, ALU.max).then_inc(scan_done, 1)
                    dve.wait_ge(scan_done, 2 * u + 2)
                    v.tensor_tensor(s, SC[:, t % 4, 1:n + 1], s, ALU.subtract).then_inc(p_done, 1)
                else:
                    dve.wait_ge(e_done, u + 1)
                    v.reciprocal(COLS[:, t, 3:4], COLS[:, t, 2:3]).then_inc(rc_done, 1)
                    dve.wait_ge(rc_done, a.soft0 + 8 * h + t + 1)
                    v.tensor_scalar(SC[:, t % 4, 0:n], SC[:, t % 4, 0:n], COLS[:, t, 3:4], None,
                                    ALU.mult).then_inc(p_done, 1)

            def lo_half(a, h, j, t, half, last):
                hi, n = keys_by_queries(HH, a, t, half)
                lo, _ = keys_by_queries(HL, a, t, half)
                dve.wait_ge(th_done, th_count(a, h, t, half))
                src = PS[:, 4 + parity(a, t, half, j, last), 0:n * P].rearrange("p (k q) -> p k q", q=P)
                v.tensor_tensor(lo, src, hi.bitcast(F32), ALU.subtract).then_inc(tl_done, 1)

            def v_tiles(a, h, j, first=False):
                for step in range(a.vsteps):
                    n = min(HALF, a.nk - HALF * step)
                    c = v_count(a, h, step, first)
                    dve.wait_ge(tr_done, c)
                    v.tensor_copy(VS[:, j, HALF * step:HALF * step + n],
                                  PS[:, 4 + v_parity(a, step, j, first), 0:n].bitcast(F32R))\
                        .then_inc(tl_done, 1)

            def output(a, h, hf):
                g = a.head0 + h
                dve.wait_ge(ob_done, 2 * g + hf + 1)
                dve.wait_ge(o_stored[hf], 16 * g)
                v.tensor_tensor(ACC[0:HEAD, 2 + hf, 0:HALF], PS[0:HEAD, 6 + hf, :],
                                ACC[0:HEAD, hf, 0:HALF], ALU.add).then_inc(oo_done, 1)

            def attend(a):
                v_tiles(a, 0, 0, True)
                if not a.causal:
                    for t in range(a.s_ahead):
                        row_max(a, 0, t)
                for t in range(a.p_ahead):
                    probs(a, 0, t)

                def head(h, j, first, last):
                    def ahead(t, n):
                        return (h, t + n) if t + n < 8 else (h + 1, t + n - 8)
                    for t in range(8):
                        if t == 7 and not last:
                            v_tiles(a, h + 1, 1 - j)
                        if t == 0 and not first:
                            output(a, h - 1, 0)
                        if a.causal and (t + a.p_ahead < 8 or not last):
                            probs(a, *ahead(t, a.p_ahead))
                        lo_half(a, h, j, t, 0, last)
                        if not a.causal and (t + a.p_ahead < 8 or not last):
                            probs(a, *ahead(t, a.p_ahead))
                        if not a.causal and (t + a.s_ahead < 8 or not last):
                            row_max(a, *ahead(t, a.s_ahead))
                        if a.halves[t] == 2:
                            lo_half(a, h, j, t, 1, last)
                        if t == 4 and not first:
                            output(a, h - 1, 1)
                heads_of(dve, a, head)
                for hf in range(2):
                    output(a, a.heads - 1, hf)

            v.memset(ACC[:, 5, 0:TOK - P], 0.0).then_inc(acc_clear, 1)
            v.tensor_copy(ACC[:, 5, TOK - P:], LATER[:]).then_inc(acc_clear, 1)
            dve.wait_ge(acc_clear, 5)
            attend(sbk)

            def products(name, stage):
                def product(k):
                    s, c = XSN[stage, k]
                    dve.wait_ge(xs_loaded[s], c)
                    dve.wait_ge(gate_loaded[k % 2], G0[name] + 16 * (k // 2 + 1))
                    v.tensor_tensor(xs(k % 3), xs(k % 3), work(k % 2), ALU.mult)\
                        .then_inc(t_ready, 1)
                product(0)
                for k in range(8):
                    if k + 1 < 8:
                        product(k + 1)
                    dve.wait_ge(hi_ready, H0[name] + k + 1)
                    v.tensor_tensor(hk(HL, k), xs(k % 3), hk(HH, k).bitcast(F32), ALU.subtract)\
                        .then_inc(h_ready, 1)
            products("b_out", "bo")
            sum_clear("x3")
            out_chunks("b_out", "x3", lambda m: MOD[:, bass.ds(56 + m, 1)])
            stats("x3", D)
            sum_clear("l0")
            for k in range(8):
                v.scalar_tensor_tensor(out=two(rk(k)), in0=two(rk(k)), scalar=vcol("f1_g", k),
                                       in1=rstd_rows(), op0=ALU.mult, op1=ALU.mult)\
                    .then_inc(t_ready, 1)
                if k:
                    sum_add("l0", k - 1, (k - 1) % 2)
            sum_add("l0", 7, 1)
            stats("l0", D)
            normed("l0", 8, rk, lambda k: xs(k % 3), lambda k: vcol("l0_g", k))
            sum_clear("uq")
            for k in range(Q_LORA_T):
                sum_add("uq", k, k % 2)
            stats("uq", Q_LORA_T * P)
            normed("uq", Q_LORA_T, lambda k: xs(k), lambda k: xs(k), lambda k: vcol("q_g", k))
            dve.wait_ge(cs_loaded, 32)
            for b in range(3):
                n = RH if b == 2 else 6 * RH
                t1, t2, m = (XS[0:n, i, :] for i in range(3))
                cos, sin, o1, o2 = (SC[0:n, i, 0:TOK] for i in range(4))
                r0 = ROPE_STEPS * b
                for s in range(2):
                    s_, c_ = XSN["rope", 2 * b + s]
                    dve.wait_ge(xs_loaded[s_], c_)
                if b:
                    for s in range(2):
                        dve.wait_ge(rope_stored[s], 16 * b)
                v.tensor_tensor(o1, t1, cos, ALU.mult).then_inc(rope_seq, 1)
                v.tensor_tensor(m, t2, sin, ALU.mult).then_inc(rope_seq, 1)
                dve.wait_ge(rope_seq, r0 + 2)
                v.tensor_tensor(o1, o1, m, ALU.subtract).then_inc(rope_seq, 1)
                v.tensor_tensor(o2, t2, cos, ALU.mult).then_inc(rope_seq, 1)
                dve.wait_ge(rope_seq, r0 + 4)
                v.tensor_tensor(m, t1, sin, ALU.mult).then_inc(rope_seq, 1)
                dve.wait_ge(rope_seq, r0 + 5)
                v.tensor_tensor(o2, o2, m, ALU.add).then_inc(rope_seq, 1)
            dve.wait_ge(rope_stored[0], 48)
            sum_clear("ukv")
            for k in range(KV_LORA_T):
                sum_add("ukv", k, k % 2)
            stats("ukv", KV_LORA_T * P)
            normed("ukv", KV_LORA_T, lambda k: xs(k), lambda k: xs(k), lambda k: vcol("ckv_g", k))
            sum_clear("mem")
            for k in range(8):
                sum_add("mem", k, k % 2, N_MEM)
            stats("mem", D, N_MEM)
            normed("mem", 8, mem_tile, mem_tile, lambda k: vcol("mem_g", k), ntok=N_MEM)
            attend(mla)
            attend(mmx)
            products("l0_out", "lo")
            sum_clear("final")
            out_chunks("l0_out", "final", lambda m: ONE[:, 0:1])
            stats("final", D)
            for k in range(8):
                if k >= 4:
                    dve.wait_ge(out_stored[k % 4], 16)
                v.scalar_tensor_tensor(out=two(work(k % 4)), in0=two(rk(k)), scalar=vcol("f2_g", k),
                                       in1=rstd_rows(), op0=ALU.mult, op1=ALU.mult)\
                    .then_inc(out_ready, 1)

        @block.tensor
        def _(pe):
            t_ = nc.tensor

            def mod_columns(groups, done):
                for grp in range(groups):
                    for f in range(8):
                        last = t_.matmul(PS[:, 7, 8 * grp + f:8 * grp + f + 1],
                                         ACC[:, grp, f * P:(f + 1) * P], ONE[:, 0:1],
                                         start=True, stop=True)
                last.then_inc(mod_mm, 1)

            def stats(name, ntok=TOK):
                _, c, a0 = SQ[name]
                s, n = STAT[name], ntok // P
                pe.wait_ge(acc_done, a0 + 1 + c)
                for t in range(n):
                    last = t_.matmul(PS[:, 4, t:t + 1], SC[:, 2, t * P:(t + 1) * P], ONE[:, 0:1],
                                     start=True, stop=True)
                last.then_inc(stat_mm, 1)
                pe.wait_ge(stat_act, s + 1)
                for t in range(n):
                    last = t_.matmul(PS[:, 5 + t // 4, (t % 4) * P:(t % 4 + 1) * P],
                                     SM[:, 2, t:t + 1].to_broadcast([P, P]), IDF[:],
                                     start=True, stop=True)
                last.then_inc(stat_mm, 1)

            def chunk(name, g, par, first, ntok=TOK):
                kts = KTILES.get(name, KT)
                pe.wait_ge(w_lo, g + 1)
                if not (isinstance(g, int) and g < 2):
                    pe.wait_ge(psum_freed, g - 1)
                for hf in range(1 if ntok < TOK else 2):
                    n = min(ntok, HALF)
                    dst = PS[:, 2 * par + hf, 0:n]
                    for k in range(kts):
                        if first and hf == 0:
                            pe.wait_ge(h_ready, H0[name] + k + 1)
                        w = slice(k * P, (k + 1) * P)
                        h = slice(k * TOK + hf * HALF, k * TOK + hf * HALF + n)
                        for i, (a, b) in enumerate(((WH, HH), (WL, HH), (WH, HL))):
                            last = t_.matmul(dst, a[:, par, w], b[:, h], start=(k == 0 and i == 0),
                                             stop=(k == kts - 1 and i == 2))
                last.then_inc(chunk_done, 1)

            def project(name, ntok=TOK):
                g0, n = FIRST[name], COUNT[name]
                for m in range(2):
                    chunk(name, g0 + m, (g0 + m) % 2, m == 0, ntok)

                def pair(i):
                    for j in range(2):
                        chunk(name, g0 + 2 * i + j, (g0 + j) % 2, False, ntok)
                repeat(pe, 1, n // 2, pair)
                if n % 2:
                    chunk(name, g0 + n - 1, (g0 + n - 1) % 2, False, ntok)

            def scores(a, h, j, t, start=False):
                g = a.head0 + h
                u = 8 * g + t
                if t == 0:
                    pe.wait_ge(qk_lo, 3 * g + 2)
                if not (isinstance(u, int) and u < 2):
                    pe.wait_ge(e_done, u - 1)
                n = a.nkt[t] * P
                q = slice(t * P, (t + 1) * P)
                terms = ((QH, WH), (QH, WL)) if a.stacked else ((QH, WH), (QL, WH), (QH, WL))
                r = P if a.stacked else a.rows
                for b in range((n + HALF - 1) // HALF):
                    w = min(HALF, n - b * HALF)
                    for i, (x, y) in enumerate(terms):
                        last = t_.matmul(PS[:, 2 * (t % 2) + b, 0:w], x[0:r, j, q],
                                         y[0:r, j, b * HALF:b * HALF + w],
                                         start=(i == 0), stop=(i == len(terms) - 1))
                last.then_inc(s_done, 1)

            def bank_free(c):
                if not (isinstance(c, int) and c <= 2):
                    pe.wait_ge(tl_done, c - 2)

            def transpose_v(a, h, j, first=False):
                g = a.head0 + h
                pe.wait_ge(qk_lo, 3 * g + 3)
                for step in range(a.vsteps):
                    bank_free(v_count(a, h, step, first))
                    for k in range(4 * step, min(4 * step + 4, a.nk // P)):
                        last = t_.transpose(
                            PS[:, 4 + v_parity(a, step, j, first),
                               (k % 4) * P:(k % 4 + 1) * P].bitcast(F32R),
                            VV[:, k * P:(k + 1) * P], IDR[:])
                    last.then_inc(tr_done, 1)

            def transpose_p(a, h, j, t, half, last_head):
                g = a.head0 + h
                if half == 0:
                    pe.wait_ge(p_done, 8 * g + t + 1)
                bank_free(tl_count(a, h, t, half, last_head))
                for k in range(4 * half, min(4 * half + 4, a.nkt[t])):
                    last = t_.transpose(PS[:, 4 + parity(a, t, half, j, last_head),
                                           (k % 4) * P:(k % 4 + 1) * P],
                                        SC[:, t % 4, k * P:(k + 1) * P], IDF[:])
                last.then_inc(tr_done, 1)

            def values(a, h, j, hf, part, last_head=False):
                g = a.head0 + h
                n = a.nkt[4 * hf + 3]
                each = (n + 3) // 4
                if part == 0:
                    t, half = 4 * hf + 3, a.halves[4 * hf + 3] - 1
                    pe.wait_ge(tl_done, tl_count(a, h, t, half, last_head))
                    if not (isinstance(h, int) and g == 0):
                        pe.wait_ge(oo_done, 2 * g + hf - 1)
                for k in range(each * part, min(n, each * part + each)):
                    c0 = max(0, k * P - hf * HALF) if a.causal else 0
                    for i, H in enumerate((HH, HL)):
                        base = 4096 * hf + HALF * k
                        last = t_.matmul(PS[:, 6 + hf, c0:HALF], VS[:, j, k * P:(k + 1) * P],
                                         H[:, base + c0:base + HALF], start=(k == 0 and i == 0),
                                         stop=(k == n - 1 and i == 1))
                    if k == n - 1:
                        last.then_inc(av_done, 1)

            def attend(a):
                transpose_v(a, 0, 0, True)
                for t in range(a.s_ahead):
                    scores(a, 0, 0, t)

                def head(h, j, first, last):
                    for t in range(8):
                        if t == 7 and not last:
                            transpose_v(a, h + 1, 1 - j)
                        transpose_p(a, h, j, t, 0, last)
                        if t + a.s_ahead < 8:
                            scores(a, h, j, t + a.s_ahead)
                        elif not last:
                            scores(a, h + 1, 1 - j, t + a.s_ahead - 8)
                        if a.halves[t] == 2:
                            transpose_p(a, h, j, t, 1, last)
                        if t >= 4:
                            values(a, h, j, 0, t - 4, last)
                        elif not first:
                            values(a, h - 1, 1 - j, 1, t)
                heads_of(pe, a, head)
                for part in range(4):
                    values(a, a.heads - 1, (a.heads - 1) % 2, 1, part, True)

            pe.wait_ge(consts, 4)
            pe.wait_ge(mod_acc, 16)
            mod_columns(2, 1)
            stats("a_in")
            project("a_in")
            pe.wait_ge(mod_acc, 16 + 48)
            mod_columns(6, 2)
            project("a_out")
            stats("kv")
            project("kv")
            project("qz")
            pe.wait_ge(consts_r, 1)
            pe.wait_ge(psum_freed, FIRST["b_out"])
            attend(sbk)
            project("b_out")
            stats("x3")
            stats("l0")
            project("l0")
            stats("uq")
            project("uq")
            stats("ukv")
            project("ukv")
            stats("mem", N_MEM)
            project("mem", N_MEM)
            pe.wait_ge(psum_freed, FIRST["l0_out"])
            attend(mla)
            attend(mmx)
            project("l0_out")
            stats("final")


def kernel(**inputs):
    import concourse.bacc as bacc
    from concourse.bass_utils import run_bass_kernel_spmd

    a = {k: np.asarray(v) for k, v in inputs.items()}

    def chunks(w, cols):
        kt = w.shape[0] // P
        t = np.stack([w[:, c:c + P] for c in cols]).reshape(len(cols), kt, P, P)
        t = t.transpose(0, 2, 1, 3).reshape(len(cols), P, kt * P)
        full = np.zeros((len(cols), P, D), w.dtype)
        full[:, :, :kt * P] = t
        return full

    every = lambda n: [P * i for i in range(n)]
    nope = [96 * h + i for h in range(MLA_HEADS) for i in range(HEAD)]
    rope = [96 * h + HEAD + RH * s + i for s in range(2) for h in range(MLA_HEADS) for i in range(RH)]
    a_cols = [D * part + P * c for c in range(KT) for part in (1, 2, 0, 3)]
    wall = np.concatenate([
        chunks(a["a_w_in"][0], a_cols), chunks(a["a_w_out"][0], every(8)),
        chunks(a["w_kv"], every(16)), chunks(a["b_w_qz"][0], every(16)),
        chunks(a["b_w_out"][0], every(8)), chunks(a["w_in_l0_2"], L0_COLS),
        chunks(a["w_uq_l0_2"][:, nope + rope], every(9)), chunks(a["w_ukv_l0_2"], every(12)),
        chunks(a["w_mem_kv_l0_2"], every(4)), chunks(a["w_out_l0_2"], every(8))])

    def columns(vec):
        return vec.reshape(-1, P).T

    freq = (1.0 / (np.float32(10000.0) ** (np.arange(0, ROPE, 2, dtype=np.float32) / np.float32(ROPE))))
    vecs = np.concatenate([
        columns(a["c"][0]), columns(a["a_mod_b"][0]), columns(a["kv_mod_b"]),
        columns(a["b_mod_b"][0]), columns(a["a_norm_g"][0]), columns(a["kv_norm_g"]),
        columns(a["b_norm_g"][0]), columns(a["final_norm_g"]), columns(a["norm_g_l0_2"]),
        columns(a["q_norm_g_l0_2"]), columns(a["kv_norm_g_l0_2"]), columns(a["mem_norm_g_l0_2"]),
        columns(a["final_norm_g_2"]), columns(a["a_conv_w"][0].reshape(-1)),
        np.tile(freq.astype(np.float32), P // RH)[:, None]], axis=1)

    am = a["a_mod_w"][0].reshape(KT, P, 3, D).transpose(0, 2, 1, 3)
    km = a["kv_mod_w"].reshape(KT, P, 2, D).transpose(0, 2, 1, 3)
    bm = a["b_mod_w"][0].reshape(KT, P, 3, D).transpose(0, 2, 1, 3)
    arrays = {
        "wall": wall, "vecs": vecs, "xT": a["x"][0].T.reshape(KT, P, TOK),
        "mod_a": am[:, 0:2].reshape(16, P, D),
        "mod_rest": np.concatenate([am[:, 2:3], km, bm], axis=1).reshape(48, P, D),
        "pos": a["positions_2"],
        "memT": a["mem_2"][0].T.reshape(KT, P, N_MEM).transpose(1, 0, 2).reshape(P, KT * N_MEM),
    }
    arrays = {k: np.ascontiguousarray(v) for k, v in arrays.items()}
    nc = bacc.Bacc("TRN2", target_bir_lowering=False, num_devices=1)
    args = [nc.dram_tensor(k, v.shape, mybir.dt.from_np(v.dtype), kind="ExternalInput").ap()
            for k, v in arrays.items()]
    out = nc.dram_tensor("out", (KT, P, TOK), F32, kind="ExternalOutput").ap()
    build(nc, *args, out)
    r = run_bass_kernel_spmd(nc, [arrays], core_ids=[0])
    got = r.results[0]["out"]
    return np.ascontiguousarray(np.asarray(got).reshape(D, TOK).T)[None]
```

```python
import math
from contextlib import ExitStack

import numpy as np
import concourse.bass as bass
import concourse.mybir as mybir

F32 = mybir.dt.float32
F32R = mybir.dt.float32r
I32 = mybir.dt.int32
ALU = mybir.AluOpType
ACT = mybir.ActivationFunctionType
AX = mybir.AxisListType

P = 128
D = 1024
KT = D // P
TOK = 1024
HALF = 512
EPS = 1e-6
HEAD = 64
SB_HEADS = 16
MLA_HEADS = 12
ROPE = 32
RH = ROPE // 2
MEM_HEADS = 4
N_MEM = 256
Q_LORA_T = 3
KV_LORA_T = 2
LATENT = Q_LORA_T + KV_LORA_T
GATE0 = 8
L0_COLS = [0, 128, 256, 384, 512, 640, 672, 800] + [928 + P * j for j in range(8)]

STAGES = [("a_in", 32), ("a_out", 8), ("kv", 16), ("qz", 16), ("b_out", 8), ("l0", 16),
          ("uq", 9), ("ukv", 12), ("mem", 4), ("l0_out", 8)]
FIRST = {}
_n = 0
for _name, _count in STAGES:
    FIRST[_name] = _n
    _n += _count
CHUNKS = _n
COUNT = dict(STAGES)
KTILES = {"uq": Q_LORA_T, "ukv": KV_LORA_T}
LAST = {name: FIRST[name] + count - 1 for name, count in STAGES}
INPUT_AT = {"ukv": Q_LORA_T * 1024, "mem": (Q_LORA_T + KV_LORA_T) * 1024}

VECTORS = [("c", 8), ("a_b", 24), ("kv_b", 16), ("b_b", 24), ("a_g", 8), ("kv_g", 8), ("b_g", 8),
           ("f1_g", 8), ("l0_g", 8), ("q_g", 3), ("ckv_g", 2), ("mem_g", 8), ("f2_g", 8),
           ("conv", 24), ("freq", 1)]
COL = {}
_n = 0
for _name, _count in VECTORS:
    COL[_name] = _n
    _n += _count
NVEC = _n

TWO_PI = 2.0 * math.pi
C1 = 6.28125
C2 = float(np.float32(np.round((TWO_PI - C1) * 2.0 ** 23) / 2.0 ** 23))
C3 = TWO_PI - C1 - C2
MAGIC = 1.5 * 2.0 ** 23
PI_F = float(np.nextafter(np.float32(math.pi), np.float32(0)))

SLOT_W = TOK + 4


LOOP = True


def repeat(eng, first, end, body):
    if LOOP and end - first > 1:
        with eng.Fori(first, end) as i:
            body(i)
    else:
        for i in range(first, end):
            body(i)


def build(nc, wall, vecs, xT, mod_a, mod_rest, pos, memT, out):
    ctx = ExitStack()

    def sb(name, shape, dt=F32):
        return ctx.enter_context(nc.sbuf_tensor(name, shape, dt))

    def sem(name):
        return ctx.enter_context(nc.semaphore(name))

    def dram(name, shape):
        return nc.dram_tensor(name, shape, F32, kind="Internal").ap()
    y_d = dram("y_d", [KT, P, TOK])
    kv_d = dram("kv_d", [2 * D, TOK])
    qz_d = dram("qz_d", [2 * D, TOK])
    o_d = dram("o_d", [D, TOK])
    l0_d = dram("l0_d", [16 * P, TOK])
    q2_d = dram("q2_d", [9 * P, TOK])
    qr_d = dram("qr_d", [2, MLA_HEADS * RH, TOK])
    kr_d = dram("kr_d", [ROPE, TOK])
    kv2_d = dram("kv2_d", [MLA_HEADS * P, TOK])
    mkv_d = dram("mkv_d", [4 * P, N_MEM])
    br_d = dram("br_d", [D, TOK])
    cs_d = dram("cs_d", [2, 6 * RH, TOK])

    with ctx:
        R = sb("R", [P, KT * TOK])
        HH = sb("HH", [P, KT * TOK], F32R)
        HL = sb("HL", [P, KT * TOK], F32R)
        WST = sb("WST", [P, 2, D])
        WH = sb("WH", [P, 2, D], F32R)
        WL = sb("WL", [P, 2, D], F32R)
        ACC = sb("ACC", [P, 6, TOK])
        XS = sb("XS", [P, 3, TOK])
        SC = sb("SC", [P, 4, SLOT_W])
        QH = sb("QH", [P, 2, TOK], F32R)
        QL = sb("QL", [P, 2, TOK], F32R)
        VV = sb("VV", [P, TOK], F32R)
        VS = sb("VS", [P, 2, TOK], F32R)
        IDF = sb("IDF", [P, P])
        IDR = sb("IDR", [P, P], F32R)
        ONE = sb("ONE", [P, P])
        LATER = sb("LATER", [P, P])
        VEC = sb("VEC", [P, NVEC])
        CS = sb("CS", [P, KT])
        MOD = sb("MOD", [P, 64])
        GS = sb("GS", [P, 24])
        G2 = sb("G2", [P, 16])
        SM = sb("SM", [P, 4, 8])
        COLS = sb("COLS", [P, 8, 4])

        PS = ctx.enter_context(nc.psum_tensor("PS", [P, 8, HALF], F32))

        vec_loaded = sem("vec_loaded")
        w_hi = sem("w_hi")
        w_lo = sem("w_lo")
        chunk_done = sem("chunk_done")
        psum_freed = sem("psum_freed")
        consts = sem("consts")
        x3_ready = sem("x3_ready")
        consts_r = sem("consts_r")
        silu_c = sem("silu_c")
        mod_acc = sem("mod_acc")
        acc_clear = sem("acc_clear")
        mod_mm = sem("mod_mm")
        mod_ready = sem("mod_ready")
        sq_done = sem("sq_done")
        acc_done = sem("acc_done")
        stat_mm = sem("stat_mm")
        stat_dve = sem("stat_dve")
        stat_act = sem("stat_act")
        t_ready = sem("t_ready")
        hi_ready = sem("hi_ready")
        h_ready = sem("h_ready")
        y_ready = sem("y_ready")
        y_stored = sem("y_stored")
        conv_seq = sem("conv_seq")
        tab_seq = sem("tab_seq")
        tab_stored = sem("tab_stored")
        sin_done = sem("sin_done")
        rope_seq = sem("rope_seq")
        pos_loaded = sem("pos_loaded")
        cs_loaded = sem("cs_loaded")
        mem_loaded = sem("mem_loaded")
        qk_hi = sem("qk_hi")
        qk_lo = sem("qk_lo")
        s_done = sem("s_done")
        m_done = sem("m_done")
        nb_done = sem("nb_done")
        e_done = sem("e_done")
        rc_done = sem("rc_done")
        p_done = sem("p_done")
        scan_done = sem("scan_done")
        tr_done = sem("tr_done")
        th_done = sem("th_done")
        tl_done = sem("tl_done")
        av_done = sem("av_done")
        ob_done = sem("ob_done")
        oo_done = sem("oo_done")
        out_ready = sem("out_ready")
        x_loaded = [sem(f"x_loaded{i}") for i in range(8)]
        w_loaded = [sem(f"w_loaded{i}") for i in range(2)]
        xs_loaded = [sem(f"xs_loaded{i}") for i in range(3)]
        gate_loaded = [sem(f"gate_loaded{i}") for i in range(2)]
        es_stored = [sem(f"es_stored{i}") for i in range(2)]
        rope_stored = [sem(f"rope_stored{i}") for i in range(2)]
        o_stored = [sem(f"o_stored{i}") for i in range(2)]
        out_stored = [sem(f"out_stored{i}") for i in range(4)]

        MASK = QL[:, 0, :]

        def rk(k):
            return R[:, bass.ds(k * TOK, TOK)]

        def hk(h, k, n=TOK, name=None):
            c = INPUT_AT.get(name, 0) + k * n
            return h[:, c:c + n]

        def width(name):
            return KTILES.get(name, KT) * P

        def two(ap):
            return ap.rearrange("p (a b) -> p a b", a=2)

        def chunk_psum(par, ntok=TOK):
            return PS[:, 2 * par:2 * par + 2, :] if ntok == TOK else PS[:, 2 * par, 0:ntok]

        def like(ap, ntok=TOK):
            return two(ap) if ntok == TOK else ap

        def vcol(name, k=0, n=1):
            return VEC[:, COL[name] + k:COL[name] + k + n]

        def work(s, n=TOK):
            return SC[:, s, 0:n]

        def xs(s, n=TOK, rows=P):
            return XS[0:rows, s, 0:n]

        def tiles(t):
            return t.rearrange("(m p) n -> m p n", p=P)

        def table(i):
            return ACC[0:6 * RH, i, :]

        def square(name, j, ntok=TOK):
            if name in ("uq", "ukv", "mem"):
                return ACC[:, 2 + j, 0:ntok]
            return work(j, ntok)

        def mem_tile(k):
            return ACC[:, 4 + k // 4, (k % 4) * N_MEM:(k % 4 + 1) * N_MEM]

        def wall_at(g, w):
            return wall[bass.ds(g, 1), :, 0:w].rearrange("a p n -> (a p) n")

        def latent(k):
            return xs(k) if k < Q_LORA_T else ACC[:, k - Q_LORA_T, :]

        XSN = {}
        at = [0, 0, 0]

        def plan(stage, slots, dmas=None):
            for n, s in enumerate(slots):
                at[s] += 16 * (dmas[n] if dmas else 1)
                XSN[stage, n] = (s, at[s])

        plan("mod_a", [n % 3 for n in range(16)])
        plan("mod_rest", [(n + 1) % 3 for n in range(48)])
        plan("y", [k % 3 for k in range(8)])
        plan("sb", [0, 1, 2] * SB_HEADS, [2, 2, 2] * SB_HEADS)
        plan("bo", [k % 3 for k in range(8)])
        plan("rope", [0, 1] * 3)
        plan("mla", [0, 1, 2] * MLA_HEADS, [3, 2, 2] * MLA_HEADS)
        plan("memory", [0, 1, 2] * MEM_HEADS, [2, 2, 2] * MEM_HEADS)
        plan("lo", [k % 3 for k in range(8)])

        def xs_count(stage, n0, per, i):
            s, c = XSN[stage, n0]
            if (stage, n0 + per) not in XSN:
                return s, c
            return s, c + (XSN[stage, n0 + per][1] - c) * i

        H0, hb = {}, 0
        for name, kts in [("a_in", 8), ("a_out", 8), ("kv", 8), ("qz", 8), ("b_out", 8), ("l0", 8),
                          ("uq", 3), ("ukv", 2), ("mem", 8), ("l0_out", 8)]:
            H0[name] = hb
            hb += kts
        T0, tb = {}, 0
        for name, kts in [("a_in", 8), ("kv", 8), ("qz", 8), ("b_out", 8), ("l0", 8),
                          ("uq", 3), ("ukv", 2), ("mem", 8), ("l0_out", 8)]:
            T0[name] = tb
            tb += kts
        SQ, STAT, sq, add = {}, {}, 0, 0
        stat_no = [0, 0, 0]
        for name, c in [("a_in", 8), ("kv", 8), ("l0", 8), ("uq", 3), ("ukv", 2), ("mem", 8),
                        ("final", 8)]:
            SQ[name], STAT[name] = (sq, c, add), tuple(stat_no)
            sq += c
            add += 1 + c * (2 if name == "l0" else 1)
            stat_no = [stat_no[0] + 1, stat_no[1] + (3 if name == "l0" else 2),
                       stat_no[2] + (4 if name == "l0" else 2)]
        ES0, STORED, es = {}, {}, [0, 0]
        for name in ("kv", "qz", "l0", "uq", "ukv", "mem"):
            skip = LATENT if name == "l0" else 0
            ES0[name] = (es[0] - 16 * ((skip + 1) // 2), es[1] - 16 * (skip // 2))
            for m in range(skip, COUNT[name]):
                es[m % 2] += 16
            STORED[name] = tuple(es)
        ES_END = tuple(es)
        G0 = {"b_out": 0, "l0_out": 64}
        TABLE_STEPS = 18
        ROPE_STEPS = 6

        class Pass:

            def __init__(self, name, heads, rows, causal, scale, nk):
                self.name, self.heads, self.rows, self.causal = name, heads, rows, causal
                self.scale, self.nk, self.stacked = scale, nk, rows == HEAD
                self.nkt = [(t + 1 if causal else nk // P) for t in range(8)]
                self.halves = [(n + 3) // 4 for n in self.nkt]
                self.vsteps = (nk // P + 3) // 4
                self.before = [sum(self.halves[:t]) for t in range(8)]
                self.per = sum(self.halves)
                self.s_ahead = 3
                self.e_ahead = 3 if causal else 2
                self.p_ahead = 2 if causal else 1

        sbk = Pass("sb", SB_HEADS, HEAD, True, 1.0 / math.sqrt(HEAD), TOK)
        mla = Pass("mla", MLA_HEADS, HEAD + ROPE, False, 1.0 / math.sqrt(HEAD + ROPE), TOK)
        mmx = Pass("memory", MEM_HEADS, HEAD, False, 1.0 / math.sqrt(HEAD), N_MEM)
        heads = th = tl = soft = 0
        for a in (sbk, mla, mmx):
            a.head0, a.th0, a.tl0, a.soft0 = heads, th, tl, soft
            heads += a.heads
            th += a.heads * a.per
            tl += a.heads * (a.per + a.vsteps)
            soft += 0 if a.causal else 8 * a.heads

        def th_count(a, h, t, half):
            return a.th0 + h * a.per + a.before[t] + half + 1

        def tl_count(a, h, t, half, last=False):
            n = a.tl0 + h * (a.per + a.vsteps) + a.vsteps + a.before[t] + half + 1
            return n + (a.vsteps if t == 7 and not last else 0)

        def v_count(a, h, step, first=False):
            if first:
                return a.tl0 + step + 1
            return a.tl0 + (h - 1) * (a.per + a.vsteps) + a.vsteps + a.before[7] + step + 1

        def heads_of(eng, a, body):
            body(0, 0, True, False)
            body(1, 1, False, False)

            def pair(i):
                for j in range(2):
                    body(2 * i + j, j, False, False)
            repeat(eng, 1, a.heads // 2 - 1, pair)
            body(a.heads - 2, 0, False, False)
            body(a.heads - 1, 1, False, True)

        def keys_by_queries(H, a, t, half):
            lo, hi = 4 * half, min(a.nkt[t], 4 * half + 4)
            hf, q = t // 4, (t % 4) * P
            v = H[:, 4096 * hf:4096 * hf + 4096].rearrange("p (k q) -> p k q", q=HALF)
            return v[:, lo:hi, q:q + P], hi - lo

        def v_parity(a, step, j, first=False):
            if first:
                return (a.tl0 + step) % 2
            odd = (a.per + a.vsteps) % 2
            return (a.tl0 + odd * (1 - j) + a.vsteps + a.before[7] + step) % 2

        def parity(a, t, half, j=0, last=False):
            odd = (a.per + a.vsteps) % 2
            extra = a.vsteps if t == 7 and not last else 0
            return (a.tl0 + odd * j + a.vsteps + a.before[t] + half + extra) % 2

        block = ctx.enter_context(nc.Block())

        @block.sync
        def _(sp):
            def xs_load(slot, dst, src):
                sp.dma_start(dst, src).then_inc(xs_loaded[slot], 16)

            def load_chunk(g, par, w=D):
                sp.wait_ge(w_lo, g - 1)
                sp.dma_start(WST[:, par, 0:w], wall_at(g, w)).then_inc(w_loaded[par], 16)

            def stream(first, end, w=D):
                if (end - first) % 2:
                    load_chunk(first, first % 2, w)
                    first += 1

                def pair(i):
                    for j in range(2):
                        load_chunk(first + 2 * i + j, (first + j) % 2, w)
                repeat(sp, 0, (end - first) // 2, pair)

            sp.dma_start(VEC[:], vecs).then_inc(vec_loaded, 16)
            for n in range(16):
                if n >= 3:
                    sp.wait_ge(mod_acc, n - 2)
                xs_load(n % 3, xs(n % 3), mod_a[n])
                if n % 2:
                    sp.dma_start(rk(n // 2), xT[n // 2]).then_inc(x_loaded[n // 2], 16)
            for g in range(2):
                sp.dma_start(WST[:, g, :], wall_at(g, D)).then_inc(w_loaded[g], 16)

            def a_in(c, first):
                def mod_tile(i):
                    slot, _ = XSN["mod_rest", i]
                    if first and i < 3:
                        sp.wait_ge(h_ready, 8)
                    else:
                        sp.wait_ge(mod_acc, 16 + 6 * c + i - 2)
                    xs_load(slot, xs(slot),
                            mod_rest[bass.ds(6 * c + i, 1)].rearrange("a p n -> (a p) n"))
                for i in range(4):
                    load_chunk(4 * c + i + 2, i % 2)
                    if i == 1 and not first:
                        sp.wait_ge(y_ready, c)
                        sp.dma_start(y_d[bass.ds(c - 1, 1)].rearrange("a p n -> (a p) n"), work(2))\
                            .then_inc(y_stored, 16)
                    if i < 3:
                        mod_tile(2 * i)
                        mod_tile(2 * i + 1)
            a_in(0, True)
            repeat(sp, 1, 8, lambda c: a_in(c, False))
            sp.wait_ge(y_ready, 8)
            sp.dma_start(y_d[7], work(2)).then_inc(y_stored, 16)
            sp.wait_ge(y_stored, 16 * 8)
            for k in range(8):
                if k < 3:
                    sp.wait_ge(mod_acc, 16 + 48)
                else:
                    sp.wait_ge(h_ready, H0["a_out"] + k - 2)
                xs_load(k % 3, xs(k % 3), y_d[k])
            sp.wait_ge(mod_ready, 3)
            sp.dma_start(table(4).bitcast(I32), pos.to_broadcast([6 * RH, TOK]))\
                .then_inc(pos_loaded, 16)
            stream(FIRST["a_out"] + 2, FIRST["b_out"] + 2)

            def rows(t, r, n):
                return t[bass.ds(r, n), :]

            def load_head(a, h):
                g = 3 * (a.head0 + h)
                sp.wait_ge(qk_lo, g - 2 if not (isinstance(h, int) and h == 0) else g)
                if a is mla:
                    xs_load(0, XS[0:HEAD, 0, :], rows(q2_d, MLA_HEADS * ROPE + HEAD * h, HEAD))
                    for s in range(2):
                        xs_load(0, XS[HEAD + RH * s:HEAD + RH * s + RH, 0, :],
                                rows(qr_d[s], RH * h, RH))
                else:
                    for s in range(2):
                        xs_load(0, XS[HEAD * s:HEAD * s + HEAD, 0, :],
                                rows(qz_d, HEAD * h, HEAD) if a is sbk else
                                rows(l0_d, 6 * P + HEAD * h, HEAD))
                sp.wait_ge(qk_lo, g - 1 if not (isinstance(h, int) and h == 0) else g)
                if a is mla:
                    xs_load(1, XS[0:HEAD, 1, :], rows(kv2_d, P * h, HEAD))
                    xs_load(1, XS[HEAD:HEAD + ROPE, 1, :], kr_d)
                else:
                    for s in range(2):
                        xs_load(1, XS[HEAD * s:HEAD * s + HEAD, 1, 0:a.nk],
                                rows(kv_d if a is sbk else mkv_d, HEAD * h, HEAD))
                sp.wait_ge(qk_lo, g)
                for s in range(2):
                    src = rows(kv_d, D + HEAD * h, HEAD) if a is sbk else (
                        rows(kv2_d, P * h + HEAD, HEAD) if a is mla else
                        rows(mkv_d, MEM_HEADS * HEAD + HEAD * h, HEAD))
                    xs_load(2, XS[HEAD * s:HEAD * s + HEAD, 2, 0:a.nk], src)

            def store_out(a, h, hf, row0, dst):
                sp.wait_ge(oo_done, 2 * (a.head0 + h) + hf + 1)
                sp.dma_start(dst[bass.ds(row0 + HEAD * h, HEAD), hf * HALF:(hf + 1) * HALF],
                             ACC[0:HEAD, 2 + hf, 0:HALF]).then_inc(o_stored[hf], 16)

            def attend(a, dst, row0, ahead):
                def head(h, j, first, last):
                    if last:
                        ahead()
                    else:
                        load_head(a, h + 1)
                    if not first:
                        store_out(a, h - 1, 1, row0, dst)
                    store_out(a, h, 0, row0, dst)
                heads_of(sp, a, head)
                store_out(a, a.heads - 1, 1, row0, dst)

            def load_product(stage, name, product, gate0, gate_d, head0, heads, tiles_):
                for k in tiles_:
                    if k == 0:
                        sp.wait_ge(qk_lo, 3 * heads)
                    if k >= 2:
                        sp.wait_ge(t_ready, T0[name] + k - 1)
                    sp.dma_start(ACC[:, 4 + k % 2, :], gate_d[gate0 + k])\
                        .then_inc(gate_loaded[k % 2], 16)
                    if k >= 3:
                        sp.wait_ge(h_ready, H0[name] + k - 2)
                    for s in range(2):
                        sp.wait_ge(o_stored[s], 16 * (head0 + 2 * k + 2))
                    xs_load(k % 3, xs(k % 3), product[k * P:(k + 1) * P, :])

            for s in range(2):
                sp.wait_ge(es_stored[s], ES0["qz"][s] + 16)
            sp.wait_ge(h_ready, H0["qz"] + 8)
            load_head(sbk, 0)
            for s in range(2):
                sp.wait_ge(es_stored[s], STORED["qz"][s])

            def load_b_out(tiles_):
                load_product("bo", "b_out", o_d, KT, tiles(qz_d), 0, SB_HEADS, tiles_)
            attend(sbk, o_d, 0, lambda: load_b_out(range(0, 2)))
            load_b_out(range(2, 8))
            sp.wait_ge(t_ready, T0["b_out"] + 8)
            sp.dma_start(ACC[:, 4:6, :].rearrange("p a b -> p (a b)"), memT).then_inc(mem_loaded, 16)
            stream(FIRST["b_out"] + 2, FIRST["uq"])

            def load_rope(b):
                n = 6 * RH if b else RH
                if b:
                    sp.wait_ge(rope_seq, ROPE_STEPS * b)
                for s in range(2):
                    row = MLA_HEADS * RH * s + 6 * RH * (b - 1) if b else 5 * P + RH * s
                    xs_load(s, XS[0:n, s, :], (q2_d if b else l0_d)[row:row + n, :])

            def store_rope(b):
                n = 6 * RH if b else RH
                for s in range(2):
                    sp.wait_ge(rope_seq, ROPE_STEPS * b + 3 * s + 3)
                    dst = qr_d[s][n * (b - 1):n * b, :] if b else kr_d[RH * s:RH * s + RH, :]
                    sp.dma_start(dst, SC[0:n, 2 + s, 0:TOK]).then_inc(rope_stored[s], 16)

            def latent_stored(name, m):
                for s in range(2):
                    sp.wait_ge(es_stored[s], ES0[name][s] + 16 * ((m + 1 - s) // 2))

            def first_rope():
                sp.wait_ge(h_ready, H0["mem"] + 8)
                for s in range(2):
                    sp.dma_start(ACC[0:6 * RH, 4 + s, :], cs_d[s]).then_inc(cs_loaded, 16)
                latent_stored("l0", 6)
                load_rope(0)
            between = {4: [first_rope],
                       7: [lambda: store_rope(0)],
                       8: [lambda: latent_stored("uq", Q_LORA_T), lambda: load_rope(1)],
                       13: [lambda: store_rope(1), lambda: load_rope(2)],
                       18: [lambda: store_rope(2)]}
            n = 0
            for name in ("uq", "ukv", "mem"):
                for g in range(FIRST[name], LAST[name] + 1):
                    load_chunk(g, g % 2, width(name))
                    for step in between.get(n, []):
                        step()
                    n += 1
            stream(FIRST["l0_out"], FIRST["l0_out"] + 2)

            for s in range(2):
                sp.wait_ge(es_stored[s], STORED["ukv"][s])
                sp.wait_ge(rope_stored[s], 48)
            load_head(mla, 0)
            for s in range(2):
                sp.wait_ge(es_stored[s], ES_END[s])

            def load_l0_out(tiles_):
                load_product("lo", "l0_out", br_d, GATE0, tiles(l0_d), SB_HEADS,
                             SB_HEADS + MLA_HEADS + MEM_HEADS, tiles_)
            attend(mla, br_d, 0, lambda: load_head(mmx, 0))
            attend(mmx, br_d, MLA_HEADS * HEAD, lambda: load_l0_out(range(0, 2)))
            load_l0_out(range(2, 8))
            stream(FIRST["l0_out"] + 2, CHUNKS)
            for k in range(8):
                sp.wait_ge(out_ready, k + 1)
                sp.dma_start(out[k], work(k % 4)).then_inc(out_stored[k % 4], 16)
            for s in range(4):
                sp.wait_ge(out_stored[s], 32)

        @block.gpsimd
        def _(pool):
            gp = nc.gpsimd
            gp.memset(ONE[:], 1.0).then_inc(consts, 1)
            gp.memset(IDF[:], 0.0).then_inc(consts, 1)
            pool.wait_ge(consts, 2)
            gp.affine_select(out=IDF[:], in_=IDF[:], compare_op=ALU.not_equal, fill=1.0, base=0,
                             pattern=[[-1, P]], channel_multiplier=1).then_inc(consts, 1)
            gp.affine_select(out=LATER[:], in_=ONE[:], compare_op=ALU.is_ge, fill=0.0, base=0,
                             pattern=[[1, P]], channel_multiplier=-1).then_inc(consts, 1)

            def lo_chunk(g, par, w):
                pool.wait_ge(w_hi, g + 1)
                gp.tensor_tensor(WL[:, par, 0:w], WST[:, par, 0:w], WH[:, par, 0:w].bitcast(F32),
                                 ALU.subtract).then_inc(w_lo, 1)

            def lo_chunks(first, end, w=D):
                if (end - first) % 2:
                    lo_chunk(first, first % 2, w)
                    first += 1

                def pair(i):
                    for j in range(2):
                        lo_chunk(first + 2 * i + j, (first + j) % 2, w)
                repeat(pool, 0, (end - first) // 2, pair)

            def lo_head(a, h, j):
                g = 3 * (a.head0 + h)
                pool.wait_ge(qk_lo, g)
                pool.wait_ge(qk_hi, g + 1)
                if a.stacked:
                    q = QH[HEAD:P, j, :]
                    gp.tensor_tensor(q, XS[HEAD:P, 0, :], q.bitcast(F32), ALU.subtract)\
                        .then_inc(qk_lo, 1)
                else:
                    gp.tensor_tensor(QL[0:a.rows, j, :], XS[0:a.rows, 0, :],
                                     QH[0:a.rows, j, :].bitcast(F32), ALU.subtract)\
                        .then_inc(qk_lo, 1)
                pool.wait_ge(qk_lo, g + 1)
                pool.wait_ge(qk_hi, g + 2)
                r = P if a.stacked else a.rows
                gp.tensor_tensor(WL[0:r, j, 0:a.nk], XS[0:r, 1, 0:a.nk],
                                 WH[0:r, j, 0:a.nk].bitcast(F32), ALU.subtract).then_inc(qk_lo, 1)
                pool.wait_ge(qk_lo, g + 2)
                pool.wait_ge(qk_hi, g + 3)
                v = VV[HEAD:P, 0:a.nk]
                gp.tensor_tensor(v, XS[HEAD:P, 2, 0:a.nk], v.bitcast(F32), ALU.subtract)\
                    .then_inc(qk_lo, 1)

            lo_chunks(0, FIRST["b_out"])
            pool.wait_ge(w_lo, FIRST["b_out"])
            def lo_heads(a):
                lo_head(a, 0, 0)
                heads_of(pool, a, lambda h, j, first, last:
                         None if last else lo_head(a, h + 1, 1 - j))
            lo_heads(sbk)
            pool.wait_ge(qk_lo, 3 * SB_HEADS)
            lo_chunks(FIRST["b_out"], FIRST["uq"])
            for name in ("uq", "ukv", "mem"):
                lo_chunks(FIRST[name], LAST[name] + 1, width(name))
            pool.wait_ge(w_lo, FIRST["l0_out"])
            lo_heads(mla)
            lo_heads(mmx)
            pool.wait_ge(qk_lo, 3 * (SB_HEADS + MLA_HEADS + MEM_HEADS))
            lo_chunks(FIRST["l0_out"], CHUNKS)

        @block.scalar
        def _(act):
            sc = nc.scalar

            def stage(name, bodies, following=None, begin=0):
                g0, n = FIRST[name], COUNT[name]

                def step(body, m, j, half, last):
                    g, par = g0 + m, (g0 + j) % 2
                    if following or not last:
                        w = width(following if last else name)
                        act.wait_ge(w_loaded[1 - par], 16 * (half + par + 1))
                        act.wait_ge(chunk_done, g)
                        sc.activation(WH[:, 1 - par, 0:w], WST[:, 1 - par, 0:w], ACT.Copy)\
                            .then_inc(w_hi, 1)
                    body(m, j, g, par)

                begin //= 2
                for end, body in bodies:
                    def pair(i, last=False):
                        for j in range(2):
                            step(body, 2 * i + j, j, (g0 + j) // 2 + i, last and j == 1)
                    pairs = end // 2
                    tail = end == n and n % 2 == 0
                    if begin == 0:
                        pair(0)
                        begin = 1
                    repeat(act, begin, pairs - tail, pair)
                    if tail:
                        pair(pairs - 1, True)
                    begin = pairs
                if n % 2:
                    step(body, n - 1, 0, (g0 + n - 1) // 2, True)

            def head_chunks(name, end, body):
                for m in range(end):
                    g = FIRST[name] + m
                    par = g % 2
                    act.wait_ge(w_loaded[1 - par], 16 * (g // 2 + par + 1))
                    act.wait_ge(chunk_done, g)
                    sc.activation(WH[:, 1 - par, :], WST[:, 1 - par, :], ACT.Copy)\
                        .then_inc(w_hi, 1)
                    body(m, m % 2, g, par)

            def first_chunk(g):
                act.wait_ge(w_loaded[g % 2], 16 * (g // 2 + 1))
                sc.activation(WH[:, g % 2, :], WST[:, g % 2, :], ACT.Copy).then_inc(w_hi, 1)

            def store_chunk(name, dst, func=ACT.Copy, ntok=TOK):
                def body(m, j, g, par):
                    act.wait_ge(chunk_done, g + 1)
                    act.wait_ge(es_stored[j], ES0[name][j] + 8 * (m - j))
                    sc.activation(like(work(j, ntok), ntok), chunk_psum(par, ntok), func)\
                        .then_inc(psum_freed, 1)
                    act.wait_ge(psum_freed, g + 1)
                    act.dma_start(dst[bass.ds(m, 1)].rearrange("a p n -> (a p) n"),
                                  work(j, ntok)).then_inc(es_stored[j], 16)
                return body

            def squares(name, k, src, ntok=TOK):
                act.wait_ge(acc_done, SQ[name][2] + k)
                sc.activation(square(name, k % 2, ntok), src, ACT.Square).then_inc(sq_done, 1)

            def rstd(name):
                act.wait_ge(stat_dve, STAT[name][2] + (4 if name == "l0" else 2))
                rows = 2 if name == "l0" else 1
                sc.activation(SM[:, 0:rows, :], SM[:, 2:2 + rows, :], ACT.Sqrt)\
                    .then_inc(stat_act, 1)

            def hi_tiles(name, kts, src, shift=None, ntok=TOK, xs_stage=None, t_wait=True):
                for k in range(kts):
                    if t_wait:
                        act.wait_ge(t_ready, T0[name] + k + 1)
                    else:
                        s, c = XSN[xs_stage, k]
                        act.wait_ge(xs_loaded[s], c)
                    if k == 0 and name not in INPUT_AT:
                        act.wait_ge(chunk_done, FIRST[name])
                    if shift is None:
                        sc.activation(hk(HH, k, ntok, name), src(k), ACT.Copy)\
                            .then_inc(hi_ready, 1)
                    else:
                        sc.activation(hk(HH, k, ntok), src(k), ACT.Identity, bias=shift(k))\
                            .then_inc(hi_ready, 1)

            act.wait_ge(vec_loaded, 16)
            sc.activation(CS[:], vcol("c", 0, 8), ACT.Silu).then_inc(silu_c, 1)
            for k in range(8):
                act.wait_ge(x_loaded[k], 16)
                squares("a_in", k, rk(k))
            rstd("a_in")
            first_chunk(0)
            hi_tiles("a_in", 8, lambda k: xs(k % 3), lambda k: MOD[:, k:k + 1])
            def a_in(c):
                for i in range(4):
                    g, par = 4 * c + i, i % 2
                    act.wait_ge(w_loaded[1 - par], 16 * (2 * c + (i + 1) // 2 + 1))
                    act.wait_ge(chunk_done, g)
                    sc.activation(WH[:, 1 - par, :], WST[:, 1 - par, :], ACT.Copy).then_inc(w_hi, 1)
                    if i == 0:
                        act.wait_ge(chunk_done, g + 1)
                        sc.activation(two(work(0)), chunk_psum(par), ACT.Copy)\
                            .then_inc(psum_freed, 1)
                    if i == 3:
                        act.wait_ge(chunk_done, g + 1)
                        act.wait_ge(psum_freed, g)
                        sc.activation(two(work(3)), chunk_psum(par), ACT.Silu)\
                            .then_inc(psum_freed, 1)
            a_in(0)
            repeat(act, 1, 8, a_in)
            hi_tiles("a_out", 8, lambda k: xs(k % 3), xs_stage="y", t_wait=False)

            def out_squares(stat):
                def body(m, j, g, par):
                    act.wait_ge(psum_freed, g + 1)
                    act.wait_ge(acc_done, SQ[stat][2] + (2 * m - 1 if stat == "l0" else m))
                    sc.activation(work(j), rk(m), ACT.Square).then_inc(sq_done, 1)
                return body
            stage("a_out", [(8, out_squares("kv"))], "kv")
            rstd("kv")
            hi_tiles("kv", 8, lambda k: xs(k % 3), lambda k: MOD[:, 24 + k:25 + k])
            store_kv = store_chunk("kv", tiles(kv_d))

            def kv_chunk(m, j, g, par):
                store_kv(m, j, g, par)
                if m in (3, 5):
                    n = (m - 3) // 2
                    act.wait_ge(tab_seq, 2 + 7 * (n + 1))
                    sc.activation(table(4 + n), table(3 - 3 * n), ACT.Sin).then_inc(sin_done, 1)
                    act.wait_ge(sin_done, n + 1)
                    act.dma_start(cs_d[1 - n], table(4 + n)).then_inc(tab_stored, 16)
            head_chunks("kv", 6, kv_chunk)
            stage("kv", [(16, store_kv)], "qz", begin=6)
            act.wait_ge(tab_stored, 32)
            hi_tiles("qz", 8, lambda k: xs(k % 3), lambda k: MOD[:, 40 + k:41 + k])
            stage("qz", [(8, store_chunk("qz", tiles(qz_d))),
                         (16, store_chunk("qz", tiles(qz_d), ACT.Silu))])

            def hi_head(a, h, j, which):
                n = 3 * h + which
                s, c = xs_count(a.name, which, 3, h)
                act.wait_ge(xs_loaded[s], c)
                if which == 2:
                    if a is mmx and isinstance(h, int) and h == 0:
                        act.wait_ge(tr_done, v_count(mla, MLA_HEADS - 1, mla.vsteps - 1))
                    elif not (isinstance(h, int) and h == 0):
                        act.wait_ge(tr_done, v_count(a, h - 1, a.vsteps - 1,
                                                     isinstance(h, int) and h == 1))
                    sc.activation(VV[:, 0:a.nk], xs(2, a.nk), ACT.Copy).then_inc(qk_hi, 1)
                    return
                if a is mmx or not (isinstance(h, int) and h < 2):
                    act.wait_ge(s_done, 8 * (a.head0 + h - 1))
                r = P if a.stacked else a.rows
                if which == 0:
                    sc.activation(QH[0:r, j, :], xs(0, TOK, r), ACT.Copy).then_inc(qk_hi, 1)
                else:
                    sc.activation(WH[0:r, j, 0:a.nk], xs(1, a.nk, r), ACT.Copy).then_inc(qk_hi, 1)

            def scores_in(t, n):
                if n <= HALF:
                    return PS[:, 2 * (t % 2), 0:n]
                return PS[:, 2 * (t % 2):2 * (t % 2) + 2, :].rearrange("p a b -> p (a b)")[:, 0:n]

            def prob(a, h, t):
                u = 8 * (a.head0 + h) + t
                n = a.nkt[t] * P
                if a.causal:
                    act.wait_ge(s_done, u + 1)
                    sc.activation(SC[:, t % 4, 0:n], scores_in(t, n), ACT.Sigmoid, scale=-a.scale)\
                        .then_inc(e_done, 1)
                else:
                    act.wait_ge(nb_done, a.soft0 + 8 * h + t + 1)
                    sc.activation(SC[:, t % 4, 0:n], scores_in(t, n), ACT.Exp, scale=a.scale,
                                  bias=COLS[:, t, 1:2], accum_out=COLS[:, t, 2:3])\
                        .then_inc(e_done, 1)

            def hi_tile(a, h, j, t, half, last):
                dst, n = keys_by_queries(HH, a, t, half)
                act.wait_ge(tr_done, tl_count(a, h, t, half, last))
                src = PS[:, 4 + parity(a, t, half, j, last), 0:n * P]
                sc.activation(dst, src.rearrange("p (k q) -> p k q", q=P), ACT.Copy)\
                    .then_inc(th_done, 1)

            def lower(a, h, hf):
                act.wait_ge(av_done, 2 * (a.head0 + h) + hf + 1)
                act.wait_ge(oo_done, 2 * (a.head0 + h))
                sc.activation(ACC[0:HEAD, hf, 0:HALF], PS[HEAD:P, 6 + hf, :], ACT.Copy)\
                    .then_inc(ob_done, 1)

            def begin(a):
                for t in range(a.e_ahead):
                    prob(a, 0, t)

            def attend(a, following=None):

                def head(h, j, first, last):
                    for t in range(8):
                        if t == 0 and not first:
                            lower(a, h - 1, 0)
                        nxt = (h, t + a.e_ahead) if t + a.e_ahead < 8 else \
                            (h + 1, t + a.e_ahead - 8)
                        hi_tile(a, h, j, t, 0, last)
                        if t + a.e_ahead < 8 or not last:
                            prob(a, *nxt)
                        if a.halves[t] == 2:
                            hi_tile(a, h, j, t, 1, last)
                        if t == 4 and not first:
                            lower(a, h - 1, 1)
                        if t in (2, 3, 4) and not last:
                            hi_head(a, h + 1, 1 - j, t - 2)
                        if t in (2, 3, 4) and last and following:
                            hi_head(following, 0, 0, t - 2)
                heads_of(act, a, head)
                if following:
                    begin(following)
                for hf in range(2):
                    lower(a, a.heads - 1, hf)

            for w in range(3):
                hi_head(sbk, 0, 0, w)
            for s in range(2):
                act.wait_ge(es_stored[s], STORED["qz"][s])
            begin(sbk)
            attend(sbk)
            act.wait_ge(chunk_done, FIRST["b_out"])
            first_chunk(FIRST["b_out"])
            hi_tiles("b_out", 8, lambda k: xs(k % 3))
            stage("b_out", [(8, out_squares("l0"))], "l0")
            rstd("l0")
            hi_tiles("l0", 8, lambda k: xs(k % 3))
            store_l0 = store_chunk("l0", tiles(l0_d))

            def latent_chunk(m, j, g, par):
                if m == 4:
                    rstd("uq")
                if m == 6:
                    rstd("ukv")
                if m >= LATENT:
                    store_l0(m, j, g, par)
                else:
                    act.wait_ge(chunk_done, g + 1)
                    sc.activation(two(latent(m)), chunk_psum(par), ACT.Copy)\
                        .then_inc(psum_freed, 1)
                    act.wait_ge(psum_freed, g + 1)
                    name, k = ("uq", m) if m < Q_LORA_T else ("ukv", m - Q_LORA_T)
                    squares(name, k, latent(m))
                if m == 6:
                    act.wait_ge(mem_loaded, 16)
                    for k in range(8):
                        squares("mem", k, mem_tile(k), N_MEM)
                if m == 7:
                    rstd("mem")
            head_chunks("l0", 8, latent_chunk)
            stage("l0", [(16, store_chunk("l0", tiles(l0_d), ACT.Silu))], "uq", begin=8)

            hi_tiles("uq", Q_LORA_T, latent)
            hi_tiles("ukv", KV_LORA_T, lambda k: latent(Q_LORA_T + k))
            hi_tiles("mem", 8, mem_tile, ntok=N_MEM)
            stage("uq", [(9, store_chunk("uq", tiles(q2_d)))], "ukv")
            stage("ukv", [(12, store_chunk("ukv", tiles(kv2_d)))], "mem")
            stage("mem", [(4, store_chunk("mem", tiles(mkv_d), ntok=N_MEM))])
            for w in range(3):
                hi_head(mla, 0, 0, w)
            for s in range(2):
                act.wait_ge(es_stored[s], ES_END[s])
            begin(mla)
            attend(mla, mmx)
            attend(mmx)
            act.wait_ge(chunk_done, FIRST["l0_out"])
            first_chunk(FIRST["l0_out"])
            hi_tiles("l0_out", 8, lambda k: xs(k % 3))
            stage("l0_out", [(8, out_squares("final"))])
            rstd("final")

        @block.vector
        def _(dve):
            v = nc.vector

            def sum_clear(name):
                v.memset(SC[:, 2:4, 0:TOK] if name == "l0" else work(2), 0.0).then_inc(acc_done, 1)

            def sum_add(name, m, j, ntok=TOK):
                q0, _, a0 = SQ[name]
                dve.wait_ge(sq_done, q0 + m + 1)
                dve.wait_ge(acc_done, a0 + (2 * m if name == "l0" else m) + 1)
                if name == "l0":
                    v.scalar_tensor_tensor(out=work(3), in0=square(name, j),
                                           scalar=G2[:, bass.ds(m, 1)], in1=work(3), op0=ALU.mult,
                                           op1=ALU.add).then_inc(acc_done, 1)
                v.tensor_tensor(work(2, ntok), work(2, ntok), square(name, j, ntok), ALU.add)\
                    .then_inc(acc_done, 1)

            def stats(name, size, ntok=TOK):
                n, (_, mm, st) = ntok // P, STAT[name]
                dve.wait_ge(stat_mm, mm + 1)
                v.tensor_scalar(SM[:, 0, 0:n], PS[:, 4, 0:n], 1.0 / size, EPS, ALU.mult, ALU.add)\
                    .then_inc(stat_dve, 1)
                dve.wait_ge(stat_dve, st + 1)
                v.reciprocal(SM[:, 2, 0:n], SM[:, 0, 0:n]).then_inc(stat_dve, 1)
                dve.wait_ge(stat_mm, mm + 2)

            def stats_twice():
                _, mm, st = STAT["l0"]
                dve.wait_ge(stat_mm, mm + 1)
                v.tensor_scalar(SM[:, 0, :], PS[:, 4, 0:8], 1.0 / D, EPS, ALU.mult, ALU.add)\
                    .then_inc(stat_dve, 1)
                dve.wait_ge(stat_dve, st + 1)
                v.tensor_scalar(SM[:, 2, :], SM[:, 0, :], EPS, None, ALU.mult).then_inc(stat_dve, 1)
                dve.wait_ge(stat_dve, st + 2)
                v.scalar_tensor_tensor(out=SM[:, 1, :], in0=PS[:, 4, 8:16], scalar=1.0 / D,
                                       in1=SM[:, 2, :], op0=ALU.mult, op1=ALU.add)\
                    .then_inc(stat_dve, 1)
                dve.wait_ge(stat_dve, st + 3)
                v.reciprocal(SM[:, 2:4, :], SM[:, 0:2, :]).then_inc(stat_dve, 1)
                dve.wait_ge(stat_mm, mm + 2)

            def rstd_rows(ntok=TOK):
                return PS[:, 5:7, :] if ntok == TOK else PS[:, 5, 0:ntok]

            def normed(name, kts, src, tmp, gain, shift=None, ntok=TOK):
                def scaled(k):
                    if H0[name] + k >= 3:
                        dve.wait_ge(h_ready, H0[name] + max(0, k - 2))
                    v.scalar_tensor_tensor(out=like(tmp(k), ntok), in0=like(src(k), ntok),
                                           scalar=gain(k), in1=rstd_rows(ntok), op0=ALU.mult,
                                           op1=ALU.mult).then_inc(t_ready, 1)
                for k in range(min(2, kts)):
                    scaled(k)
                for k in range(kts):
                    dve.wait_ge(hi_ready, H0[name] + k + 1)
                    if shift is None:
                        v.tensor_tensor(hk(HL, k, ntok), tmp(k), hk(HH, k, ntok).bitcast(F32),
                                        ALU.subtract).then_inc(h_ready, 1)
                    else:
                        v.scalar_tensor_tensor(out=hk(HL, k), in0=tmp(k), scalar=shift(k),
                                               in1=hk(HH, k).bitcast(F32), op0=ALU.add,
                                               op1=ALU.subtract).then_inc(h_ready, 1)
                    if k + 2 < kts:
                        scaled(k + 2)

            def mod_add(n, grp, kt, slot, count, first):
                dve.wait_ge(xs_loaded[slot], count)
                if first:
                    dve.wait_ge(acc_clear, 1 if isinstance(n, int) and n < 16 else 2)
                else:
                    dve.wait_ge(mod_acc, n - (1 if isinstance(n, int) and n < 16 else 5))
                v.scalar_tensor_tensor(out=ACC[:, grp, :], in0=xs(slot), scalar=kt,
                                       in1=ACC[:, grp, :], op0=ALU.mult, op1=ALU.add)\
                    .then_inc(mod_acc, 1)

            dve.wait_ge(consts, 4)
            v.tensor_copy(IDR[:], IDF[:]).then_inc(consts_r, 1)
            v.memset(ACC[:, 0:2, :], 0.0).then_inc(acc_clear, 1)
            sum_clear("a_in")
            dve.wait_ge(silu_c, 1)
            for n in range(16):
                slot, count = XSN["mod_a", n]
                mod_add(n, n % 2, CS[:, n // 2:n // 2 + 1], slot, count, n < 2)
                if n % 2:
                    sum_add("a_in", n // 2, n // 2 % 2)
            dve.wait_ge(mod_mm, 1)
            v.tensor_tensor(MOD[:, 0:16], PS[:, 7, 0:16], vcol("a_b", 0, 16), ALU.add)\
                .then_inc(mod_ready, 1)
            dve.wait_ge(mod_ready, 1)
            v.scalar_tensor_tensor(out=GS[:, 0:8], in0=MOD[:, 8:16], scalar=1.0,
                                   in1=vcol("a_g", 0, 8), op0=ALU.add, op1=ALU.mult)\
                .then_inc(mod_ready, 1)
            v.memset(ACC[:], 0.0).then_inc(acc_clear, 1)
            stats("a_in", D)
            dve.wait_ge(mod_ready, 2)
            normed("a_in", 8, rk, lambda k: xs(k % 3), lambda k: GS[:, k:k + 1],
                   lambda k: MOD[:, k:k + 1])

            v.memset(SC[:, 1, 0:2], 0.0).then_inc(acc_clear, 1)
            dve.wait_ge(acc_clear, 3)

            def a_in(c, first):
                def mods(i0):
                    for i in range(i0, i0 + 3):
                        slot, _ = XSN["mod_rest", i]
                        count = XSN["mod_rest", i][1] + 32 * c
                        mod_add(16 + 6 * c + i, i, CS[:, bass.ds(c, 1)], slot, count, first)
                cu, t = SC[:, 1, :], work(2)
                dve.wait_ge(chunk_done, 4 * c + 2)
                dve.wait_ge(psum_freed, 4 * c + 1)
                v.tensor_tensor(two(cu[:, 2:2 + TOK]), chunk_psum(1), two(work(0)), ALU.mult)\
                    .then_inc(psum_freed, 1)
                dve.wait_ge(psum_freed, 4 * c + 2)
                dve.wait_ge(y_stored, 16 * c)
                tap = lambda i: VEC[:, bass.ds(COL["conv"] + 8 * i + c, 1)]
                v.tensor_scalar(t, cu[:, 2:2 + TOK], tap(2), None, ALU.mult).then_inc(conv_seq, 1)
                for i in (1, 0):
                    dve.wait_ge(conv_seq, 3 * c + 2 - i)
                    v.scalar_tensor_tensor(out=t, in0=cu[:, i:i + TOK], scalar=tap(i), in1=t,
                                           op0=ALU.mult, op1=ALU.add).then_inc(conv_seq, 1)
                mods(0)
                dve.wait_ge(chunk_done, 4 * c + 3)
                dve.wait_ge(conv_seq, 3 * c + 3)
                v.tensor_tensor(two(t), chunk_psum(0), two(t), ALU.mult).then_inc(psum_freed, 1)
                mods(3)
                dve.wait_ge(psum_freed, 4 * c + 4)
                v.tensor_tensor(t, t, work(3), ALU.mult).then_inc(y_ready, 1)
            a_in(0, True)
            repeat(dve, 1, 8, lambda c: a_in(c, False))
            dve.wait_ge(mod_mm, 2)
            v.tensor_tensor(MOD[:, 16:64], PS[:, 7, 0:48], vcol("a_b", 16, 48), ALU.add)\
                .then_inc(mod_ready, 1)
            dve.wait_ge(mod_ready, 3)
            for at_, name, g_ in ((32, "kv_g", 8), (48, "b_g", 16)):
                v.scalar_tensor_tensor(out=GS[:, g_:g_ + 8], in0=MOD[:, at_:at_ + 8], scalar=1.0,
                                       in1=vcol(name, 0, 8), op0=ALU.add, op1=ALU.mult)\
                    .then_inc(mod_ready, 1)

            v.tensor_tensor(G2[:, 0:8], vcol("f1_g", 0, 8), vcol("f1_g", 0, 8), ALU.mult)\
                .then_inc(mod_ready, 1)
            v.tensor_tensor(G2[:, 8:16], vcol("f1_g", 0, 8), vcol("l0_g", 0, 8), ALU.mult)\
                .then_inc(mod_ready, 1)

            def lo_tiles(name, stage):
                for k in range(8):
                    dve.wait_ge(hi_ready, H0[name] + k + 1)
                    v.tensor_tensor(hk(HL, k), xs(k % 3), hk(HH, k).bitcast(F32), ALU.subtract)\
                        .then_inc(h_ready, 1)

            def out_chunks(name, stat, gate):
                g0, n = FIRST[name], COUNT[name]

                def pair(i):
                    for j in range(2):
                        m, par = 2 * i + j, (g0 + j) % 2
                        dve.wait_ge(chunk_done, g0 + m + 1)
                        v.scalar_tensor_tensor(out=two(rk(m)), in0=chunk_psum(par),
                                               scalar=gate(m), in1=two(rk(m)), op0=ALU.mult,
                                               op1=ALU.add).then_inc(psum_freed, 1)
                        sum_add(stat, m, j)
                repeat(dve, 0, n // 2, pair)

            lo_tiles("a_out", "y")
            sum_clear("kv")
            out_chunks("a_out", "kv", lambda m: MOD[:, bass.ds(16 + m, 1)])
            stats("kv", D)
            dve.wait_ge(mod_ready, 7)
            normed("kv", 8, rk, lambda k: xs(k % 3), lambda k: GS[:, 8 + k:9 + k],
                   lambda k: MOD[:, 24 + k:25 + k])
            dve.wait_ge(pos_loaded, 16)
            v.tensor_copy(table(0), table(4).bitcast(I32)).then_inc(tab_seq, 1)
            dve.wait_ge(tab_seq, 1)
            v.tensor_scalar(table(1), table(0), VEC[0:6 * RH, COL["freq"]:COL["freq"] + 1],
                            None, ALU.mult).then_inc(tab_seq, 1)
            for n, turn in enumerate((0.0, 0.25)):
                ang, k_, r_ = table(1), table(2), table(3 - 3 * n)
                b_ = 2 + 7 * n
                dve.wait_ge(tab_seq, b_)
                v.tensor_scalar(k_, ang, 1.0 / TWO_PI, turn, ALU.mult, ALU.add).then_inc(tab_seq, 1)
                dve.wait_ge(tab_seq, b_ + 1)
                v.tensor_scalar(k_, k_, MAGIC, MAGIC, ALU.add, ALU.subtract).then_inc(tab_seq, 1)
                dve.wait_ge(tab_seq, b_ + 2)
                v.scalar_tensor_tensor(out=r_, in0=k_, scalar=-C1, in1=ang, op0=ALU.mult,
                                       op1=ALU.add).then_inc(tab_seq, 1)
                for i, part in enumerate((C2, C3)):
                    dve.wait_ge(tab_seq, b_ + 3 + i)
                    v.scalar_tensor_tensor(out=r_, in0=k_, scalar=-part, in1=r_, op0=ALU.mult,
                                           op1=ALU.add).then_inc(tab_seq, 1)
                dve.wait_ge(tab_seq, b_ + 5)
                v.tensor_scalar(r_, r_, turn * TWO_PI, PI_F, ALU.add, ALU.min).then_inc(tab_seq, 1)
                dve.wait_ge(tab_seq, b_ + 6)
                v.tensor_scalar(r_, r_, -PI_F, None, ALU.max).then_inc(tab_seq, 1)
            normed("qz", 8, rk, lambda k: xs(k % 3), lambda k: GS[:, 16 + k:17 + k],
                   lambda k: MOD[:, 40 + k:41 + k])

            def row_max(a, h, t):
                u = 8 * (a.head0 + h) + t
                s = a.soft0 + 8 * h + t
                dve.wait_ge(s_done, u + 1)
                src = PS[:, 2 * (t % 2):2 * (t % 2) + 2, :] if a.nk > HALF else \
                    PS[:, 2 * (t % 2), 0:a.nk]
                v.reduce_max(COLS[:, t, 0:1], src, AX.XY if a.nk > HALF else AX.X)\
                    .then_inc(m_done, 1)
                dve.wait_ge(m_done, s + 1)
                v.tensor_scalar(COLS[:, t, 1:2], COLS[:, t, 0:1], -a.scale, None, ALU.mult)\
                    .then_inc(nb_done, 1)

            def probs(a, h, t):
                u = 8 * (a.head0 + h) + t
                n = a.nkt[t] * P
                if a.causal:
                    dve.wait_ge(e_done, u + 1)
                    v.memset(SC[:, t % 4, n:n + 1], 1.0).then_inc(scan_done, 1)
                    s = SC[:, t % 4, 0:n]
                    v.tensor_tensor_scan(s[:, ::-1], s[:, ::-1], MASK[:, TOK - n:][:, ::-1].bitcast(F32), 1.0,
                                         ALU.mult, ALU.max).then_inc(scan_done, 1)
                    dve.wait_ge(scan_done, 2 * u + 2)
                    v.tensor_tensor(s, SC[:, t % 4, 1:n + 1], s, ALU.subtract).then_inc(p_done, 1)
                else:
                    dve.wait_ge(e_done, u + 1)
                    v.reciprocal(COLS[:, t, 3:4], COLS[:, t, 2:3]).then_inc(rc_done, 1)
                    dve.wait_ge(rc_done, a.soft0 + 8 * h + t + 1)
                    v.tensor_scalar(SC[:, t % 4, 0:n], SC[:, t % 4, 0:n], COLS[:, t, 3:4], None,
                                    ALU.mult).then_inc(p_done, 1)

            def lo_half(a, h, j, t, half, last):
                hi, n = keys_by_queries(HH, a, t, half)
                lo, _ = keys_by_queries(HL, a, t, half)
                dve.wait_ge(th_done, th_count(a, h, t, half))
                src = PS[:, 4 + parity(a, t, half, j, last), 0:n * P].rearrange("p (k q) -> p k q", q=P)
                v.tensor_tensor(lo, src, hi.bitcast(F32), ALU.subtract).then_inc(tl_done, 1)

            def v_tiles(a, h, j, first=False):
                for step in range(a.vsteps):
                    n = min(HALF, a.nk - HALF * step)
                    c = v_count(a, h, step, first)
                    dve.wait_ge(tr_done, c)
                    v.tensor_copy(VS[:, j, HALF * step:HALF * step + n],
                                  PS[:, 4 + v_parity(a, step, j, first), 0:n].bitcast(F32R))\
                        .then_inc(tl_done, 1)

            def output(a, h, hf):
                g = a.head0 + h
                dve.wait_ge(ob_done, 2 * g + hf + 1)
                dve.wait_ge(o_stored[hf], 16 * g)
                v.tensor_tensor(ACC[0:HEAD, 2 + hf, 0:HALF], PS[0:HEAD, 6 + hf, :],
                                ACC[0:HEAD, hf, 0:HALF], ALU.add).then_inc(oo_done, 1)

            def begin(a):
                v_tiles(a, 0, 0, True)
                if not a.causal:
                    for t in range(a.s_ahead):
                        row_max(a, 0, t)
                for t in range(a.p_ahead):
                    probs(a, 0, t)

            def attend(a, following=None):

                def head(h, j, first, last):
                    def ahead(t, n):
                        return (h, t + n) if t + n < 8 else (h + 1, t + n - 8)
                    for t in range(8):
                        if t == 7 and not last:
                            v_tiles(a, h + 1, 1 - j)
                        if t == 0 and not first:
                            output(a, h - 1, 0)
                        if a.causal and (t + a.p_ahead < 8 or not last):
                            probs(a, *ahead(t, a.p_ahead))
                        lo_half(a, h, j, t, 0, last)
                        if not a.causal and (t + a.p_ahead < 8 or not last):
                            probs(a, *ahead(t, a.p_ahead))
                        if not a.causal and (t + a.s_ahead < 8 or not last):
                            row_max(a, *ahead(t, a.s_ahead))
                        if a.halves[t] == 2:
                            lo_half(a, h, j, t, 1, last)
                        if t == 4 and not first:
                            output(a, h - 1, 1)
                heads_of(dve, a, head)
                if following:
                    begin(following)
                for hf in range(2):
                    output(a, a.heads - 1, hf)

            v.memset(work(3), 0.0).then_inc(acc_clear, 1)
            dve.wait_ge(acc_clear, 4)
            v.tensor_copy(MASK[:, 0:TOK - P], work(3, TOK - P)).then_inc(acc_clear, 1)
            v.tensor_copy(MASK[:, TOK - P:], LATER[:]).then_inc(acc_clear, 1)
            dve.wait_ge(acc_clear, 6)
            begin(sbk)
            attend(sbk)

            def products(name, stage):
                def product(k):
                    s, c = XSN[stage, k]
                    dve.wait_ge(xs_loaded[s], c)
                    dve.wait_ge(gate_loaded[k % 2], G0[name] + 16 * (k // 2 + 1))
                    v.tensor_tensor(xs(k % 3), xs(k % 3), ACC[:, 4 + k % 2, :], ALU.mult)\
                        .then_inc(t_ready, 1)
                product(0)
                for k in range(8):
                    if k + 1 < 8:
                        product(k + 1)
                    dve.wait_ge(hi_ready, H0[name] + k + 1)
                    v.tensor_tensor(hk(HL, k), xs(k % 3), hk(HH, k).bitcast(F32), ALU.subtract)\
                        .then_inc(h_ready, 1)
            products("b_out", "bo")
            sum_clear("l0")
            out_chunks("b_out", "l0", lambda m: MOD[:, bass.ds(56 + m, 1)])
            stats_twice()
            normed("l0", 8, rk, lambda k: xs(k % 3), lambda k: G2[:, 8 + k:9 + k])
            dve.wait_ge(t_ready, T0["l0"] + 8)
            dve.wait_ge(stat_mm, STAT["l0"][1] + 3)
            for k in range(8):
                v.scalar_tensor_tensor(out=two(rk(k)), in0=two(rk(k)), scalar=vcol("f1_g", k),
                                       in1=rstd_rows(), op0=ALU.mult, op1=ALU.mult)\
                    .then_inc(x3_ready, 1)
            parts = (("uq", Q_LORA_T, TOK, latent, "q_g"),
                     ("ukv", KV_LORA_T, TOK, lambda k: latent(Q_LORA_T + k), "ckv_g"),
                     ("mem", 8, N_MEM, mem_tile, "mem_g"))
            for name, kts, ntok, src, gain in parts:
                sum_clear(name)
                for k in range(kts):
                    sum_add(name, k, k % 2, ntok)
                stats(name, kts * P, ntok)
                for k in range(kts):
                    v.scalar_tensor_tensor(out=like(src(k), ntok), in0=like(src(k), ntok),
                                           scalar=vcol(gain, k), in1=rstd_rows(ntok),
                                           op0=ALU.mult, op1=ALU.mult).then_inc(t_ready, 1)
            for name, kts, ntok, src, _ in parts:
                for k in range(kts):
                    dve.wait_ge(hi_ready, H0[name] + k + 1)
                    v.tensor_tensor(hk(HL, k, ntok, name), src(k),
                                    hk(HH, k, ntok, name).bitcast(F32), ALU.subtract)\
                        .then_inc(h_ready, 1)
            dve.wait_ge(cs_loaded, 32)
            for b in range(3):
                n = 6 * RH if b else RH
                t1, t2, m = (XS[0:n, i, :] for i in range(3))
                cos, sin = (ACC[0:n, 4 + i, :] for i in range(2))
                o1, o2 = (SC[0:n, 2 + i, 0:TOK] for i in range(2))
                r0 = ROPE_STEPS * b
                for s in range(2):
                    s_, c_ = XSN["rope", 2 * b + s]
                    dve.wait_ge(xs_loaded[s_], c_)
                if b:
                    for s in range(2):
                        dve.wait_ge(rope_stored[s], 16 * b)
                v.tensor_tensor(o1, t1, cos, ALU.mult).then_inc(rope_seq, 1)
                v.tensor_tensor(m, t2, sin, ALU.mult).then_inc(rope_seq, 1)
                dve.wait_ge(rope_seq, r0 + 2)
                v.tensor_tensor(o1, o1, m, ALU.subtract).then_inc(rope_seq, 1)
                v.tensor_tensor(o2, t2, cos, ALU.mult).then_inc(rope_seq, 1)
                dve.wait_ge(rope_seq, r0 + 4)
                v.tensor_tensor(m, t1, sin, ALU.mult).then_inc(rope_seq, 1)
                dve.wait_ge(rope_seq, r0 + 5)
                v.tensor_tensor(o2, o2, m, ALU.add).then_inc(rope_seq, 1)
            begin(mla)
            attend(mla, mmx)
            attend(mmx)
            products("l0_out", "lo")
            sum_clear("final")
            dve.wait_ge(x3_ready, 8)
            out_chunks("l0_out", "final", lambda m: ONE[:, 0:1])
            stats("final", D)
            for k in range(8):
                if k >= 4:
                    dve.wait_ge(out_stored[k % 4], 16)
                v.scalar_tensor_tensor(out=two(work(k % 4)), in0=two(rk(k)), scalar=vcol("f2_g", k),
                                       in1=rstd_rows(), op0=ALU.mult, op1=ALU.mult)\
                    .then_inc(out_ready, 1)

        @block.tensor
        def _(pe):
            t_ = nc.tensor

            def mod_columns(groups, done):
                for grp in range(groups):
                    for f in range(8):
                        last = t_.matmul(PS[:, 7, 8 * grp + f:8 * grp + f + 1],
                                         ACC[:, grp, f * P:(f + 1) * P], ONE[:, 0:1],
                                         start=True, stop=True)
                last.then_inc(mod_mm, 1)

            def column_sums(name, ntok=TOK):
                _, c, a0 = SQ[name]
                n, sums = ntok // P, 2 if name == "l0" else 1
                pe.wait_ge(acc_done, a0 + 1 + sums * c)
                for i in range(sums):
                    for t in range(n):
                        last = t_.matmul(PS[:, 4, n * i + t:n * i + t + 1],
                                         SC[:, 2 + i, t * P:(t + 1) * P], ONE[:, 0:1],
                                         start=True, stop=True)
                last.then_inc(stat_mm, 1)

            def spread_rstd(name, ntok=TOK, row=0):
                n = ntok // P
                pe.wait_ge(stat_act, STAT[name][0] + 1)
                for t in range(n):
                    last = t_.matmul(PS[:, 5 + t // 4, (t % 4) * P:(t % 4 + 1) * P],
                                     SM[:, row, t:t + 1].to_broadcast([P, P]), IDF[:],
                                     start=True, stop=True)
                last.then_inc(stat_mm, 1)

            def first_rstd():
                pe.wait_ge(t_ready, T0["l0"] + 8)
                spread_rstd("l0", row=0)

            def stats(name, ntok=TOK):
                column_sums(name, ntok)
                spread_rstd(name, ntok)

            def chunk(name, g, par, first, ntok=TOK):
                kts = KTILES.get(name, KT)
                pe.wait_ge(w_lo, g + 1)
                if not (isinstance(g, int) and g < 2):
                    pe.wait_ge(psum_freed, g - 1)
                for hf in range(1 if ntok < TOK else 2):
                    n = min(ntok, HALF)
                    dst = PS[:, 2 * par + hf, 0:n]
                    for k in range(kts):
                        if first and hf == 0:
                            pe.wait_ge(h_ready, H0[name] + k + 1)
                        w = slice(k * P, (k + 1) * P)
                        c = INPUT_AT.get(name, 0) + k * ntok + hf * HALF
                        h = slice(c, c + n)
                        for i, (a, b) in enumerate(((WH, HH), (WL, HH), (WH, HL))):
                            last = t_.matmul(dst, a[:, par, w], b[:, h], start=(k == 0 and i == 0),
                                             stop=(k == kts - 1 and i == 2))
                last.then_inc(chunk_done, 1)

            def project(name, ntok=TOK, between={}):
                g0, n = FIRST[name], COUNT[name]
                begin = max(between, default=1) // 2 + 1
                for m in range(2 * begin):
                    chunk(name, g0 + m, (g0 + m) % 2, m == 0, ntok)
                    if m in between:
                        between[m]()

                def pair(i):
                    for j in range(2):
                        chunk(name, g0 + 2 * i + j, (g0 + j) % 2, False, ntok)
                repeat(pe, begin, n // 2, pair)
                if n % 2:
                    chunk(name, g0 + n - 1, (g0 + n - 1) % 2, False, ntok)

            def scores(a, h, j, t, start=False):
                g = a.head0 + h
                u = 8 * g + t
                if t == 0:
                    pe.wait_ge(qk_lo, 3 * g + 2)
                if not (isinstance(u, int) and u < 2):
                    pe.wait_ge(e_done, u - 1)
                n = a.nkt[t] * P
                q = slice(t * P, (t + 1) * P)
                terms = ((QH, WH), (QH, WL)) if a.stacked else ((QH, WH), (QL, WH), (QH, WL))
                r = P if a.stacked else a.rows
                for b in range((n + HALF - 1) // HALF):
                    w = min(HALF, n - b * HALF)
                    for i, (x, y) in enumerate(terms):
                        last = t_.matmul(PS[:, 2 * (t % 2) + b, 0:w], x[0:r, j, q],
                                         y[0:r, j, b * HALF:b * HALF + w],
                                         start=(i == 0), stop=(i == len(terms) - 1))
                last.then_inc(s_done, 1)

            def bank_free(c):
                if not (isinstance(c, int) and c <= 2):
                    pe.wait_ge(tl_done, c - 2)

            def transpose_v(a, h, j, first=False):
                g = a.head0 + h
                pe.wait_ge(qk_lo, 3 * g + 3)
                for step in range(a.vsteps):
                    bank_free(v_count(a, h, step, first))
                    for k in range(4 * step, min(4 * step + 4, a.nk // P)):
                        last = t_.transpose(
                            PS[:, 4 + v_parity(a, step, j, first),
                               (k % 4) * P:(k % 4 + 1) * P].bitcast(F32R),
                            VV[:, k * P:(k + 1) * P], IDR[:])
                    last.then_inc(tr_done, 1)

            def transpose_p(a, h, j, t, half, last_head):
                g = a.head0 + h
                if half == 0:
                    pe.wait_ge(p_done, 8 * g + t + 1)
                bank_free(tl_count(a, h, t, half, last_head))
                for k in range(4 * half, min(4 * half + 4, a.nkt[t])):
                    last = t_.transpose(PS[:, 4 + parity(a, t, half, j, last_head),
                                           (k % 4) * P:(k % 4 + 1) * P],
                                        SC[:, t % 4, k * P:(k + 1) * P], IDF[:])
                last.then_inc(tr_done, 1)

            def values(a, h, j, hf, part, last_head=False):
                g = a.head0 + h
                n = a.nkt[4 * hf + 3]
                each = (n + 3) // 4
                if part == 0:
                    t, half = 4 * hf + 3, a.halves[4 * hf + 3] - 1
                    pe.wait_ge(tl_done, tl_count(a, h, t, half, last_head))
                    if not (isinstance(h, int) and g == 0):
                        pe.wait_ge(oo_done, 2 * g + hf - 1)
                for k in range(each * part, min(n, each * part + each)):
                    c0 = max(0, k * P - hf * HALF) if a.causal else 0
                    for i, H in enumerate((HH, HL)):
                        base = 4096 * hf + HALF * k
                        last = t_.matmul(PS[:, 6 + hf, c0:HALF], VS[:, j, k * P:(k + 1) * P],
                                         H[:, base + c0:base + HALF], start=(k == 0 and i == 0),
                                         stop=(k == n - 1 and i == 1))
                    if k == n - 1:
                        last.then_inc(av_done, 1)

            def begin(a):
                transpose_v(a, 0, 0, True)
                for t in range(a.s_ahead):
                    scores(a, 0, 0, t)

            def attend(a, following=None):

                def head(h, j, first, last):
                    for t in range(8):
                        if t == 7 and not last:
                            transpose_v(a, h + 1, 1 - j)
                        transpose_p(a, h, j, t, 0, last)
                        if t + a.s_ahead < 8:
                            scores(a, h, j, t + a.s_ahead)
                        elif not last:
                            scores(a, h + 1, 1 - j, t + a.s_ahead - 8)
                        if a.halves[t] == 2:
                            transpose_p(a, h, j, t, 1, last)
                        if t >= 4:
                            values(a, h, j, 0, t - 4, last)
                        elif not first:
                            values(a, h - 1, 1 - j, 1, t)
                heads_of(pe, a, head)
                if following:
                    begin(following)
                for part in range(4):
                    values(a, a.heads - 1, (a.heads - 1) % 2, 1, part, True)

            pe.wait_ge(consts, 4)
            pe.wait_ge(mod_acc, 16)
            mod_columns(2, 1)
            stats("a_in")
            project("a_in")
            pe.wait_ge(mod_acc, 16 + 48)
            mod_columns(6, 2)
            project("a_out")
            stats("kv")
            project("kv")
            project("qz")
            pe.wait_ge(consts_r, 1)
            pe.wait_ge(psum_freed, FIRST["b_out"])
            begin(sbk)
            attend(sbk)
            project("b_out")
            column_sums("l0")
            spread_rstd("l0", row=1)
            project("l0", between={0: first_rstd, 3: lambda: column_sums("uq"), 4: lambda: spread_rstd("uq"),
                                   5: lambda: column_sums("ukv"), 6: lambda: spread_rstd("ukv"),
                                   7: lambda: column_sums("mem", N_MEM),
                                   8: lambda: spread_rstd("mem", N_MEM)})
            project("uq")
            project("ukv")
            project("mem", N_MEM)
            pe.wait_ge(psum_freed, FIRST["l0_out"])
            begin(mla)
            attend(mla, mmx)
            attend(mmx)
            project("l0_out")
            stats("final")


def kernel(**inputs):
    import concourse.bacc as bacc
    from concourse.bass_utils import run_bass_kernel_spmd

    a = {k: np.asarray(v) for k, v in inputs.items()}

    def chunks(w, cols):
        kt = w.shape[0] // P
        t = np.stack([w[:, c:c + P] for c in cols]).reshape(len(cols), kt, P, P)
        t = t.transpose(0, 2, 1, 3).reshape(len(cols), P, kt * P)
        full = np.zeros((len(cols), P, D), w.dtype)
        full[:, :, :kt * P] = t
        return full

    every = lambda n: [P * i for i in range(n)]
    nope = [96 * h + i for h in range(MLA_HEADS) for i in range(HEAD)]
    rope = [96 * h + HEAD + RH * s + i for s in range(2) for h in range(MLA_HEADS) for i in range(RH)]
    a_cols = [D * part + P * c for c in range(KT) for part in (1, 2, 0, 3)]
    wall = np.concatenate([
        chunks(a["a_w_in"][0], a_cols), chunks(a["a_w_out"][0], every(8)),
        chunks(a["w_kv"], every(16)), chunks(a["b_w_qz"][0], every(16)),
        chunks(a["b_w_out"][0], every(8)), chunks(a["w_in_l0_2"], L0_COLS),
        chunks(a["w_uq_l0_2"][:, rope + nope], every(9)), chunks(a["w_ukv_l0_2"], every(12)),
        chunks(a["w_mem_kv_l0_2"], every(4)), chunks(a["w_out_l0_2"], every(8))])

    def columns(vec):
        return vec.reshape(-1, P).T

    freq = (1.0 / (np.float32(10000.0) ** (np.arange(0, ROPE, 2, dtype=np.float32) / np.float32(ROPE))))
    vecs = np.concatenate([
        columns(a["c"][0]), columns(a["a_mod_b"][0]), columns(a["kv_mod_b"]),
        columns(a["b_mod_b"][0]), columns(a["a_norm_g"][0]), columns(a["kv_norm_g"]),
        columns(a["b_norm_g"][0]), columns(a["final_norm_g"]), columns(a["norm_g_l0_2"]),
        columns(a["q_norm_g_l0_2"]), columns(a["kv_norm_g_l0_2"]), columns(a["mem_norm_g_l0_2"]),
        columns(a["final_norm_g_2"]), columns(a["a_conv_w"][0].reshape(-1)),
        np.tile(freq.astype(np.float32), P // RH)[:, None]], axis=1)

    am = a["a_mod_w"][0].reshape(KT, P, 3, D).transpose(0, 2, 1, 3)
    km = a["kv_mod_w"].reshape(KT, P, 2, D).transpose(0, 2, 1, 3)
    bm = a["b_mod_w"][0].reshape(KT, P, 3, D).transpose(0, 2, 1, 3)
    arrays = {
        "wall": wall, "vecs": vecs, "xT": a["x"][0].T.reshape(KT, P, TOK),
        "mod_a": am[:, 0:2].reshape(16, P, D),
        "mod_rest": np.concatenate([am[:, 2:3], km, bm], axis=1).reshape(48, P, D),
        "pos": a["positions_2"],
        "memT": a["mem_2"][0].T.reshape(KT, P, N_MEM).transpose(1, 0, 2).reshape(P, KT * N_MEM),
    }
    arrays = {k: np.ascontiguousarray(v) for k, v in arrays.items()}
    nc = bacc.Bacc("TRN2", target_bir_lowering=False, num_devices=1)
    args = [nc.dram_tensor(k, v.shape, mybir.dt.from_np(v.dtype), kind="ExternalInput").ap()
            for k, v in arrays.items()]
    out = nc.dram_tensor("out", (KT, P, TOK), F32, kind="ExternalOutput").ap()
    build(nc, *args, out)
    r = run_bass_kernel_spmd(nc, [arrays], core_ids=[0])
    got = r.results[0]["out"]
    return np.ascontiguousarray(np.asarray(got).reshape(D, TOK).T)[None]
```

```python
import math
from contextlib import ExitStack

import numpy as np
import concourse.bass as bass
import concourse.mybir as mybir

F32 = mybir.dt.float32
F32R = mybir.dt.float32r
I32 = mybir.dt.int32
ALU = mybir.AluOpType
ACT = mybir.ActivationFunctionType
AX = mybir.AxisListType

P = 128
D = 1024
KT = D // P
TOK = 1024
HALF = 512
EPS = 1e-6
HEAD = 64
SB_HEADS = 16
MLA_HEADS = 12
ROPE = 32
RH = ROPE // 2
MEM_HEADS = 4
N_MEM = 256
Q_LORA_T = 3
KV_LORA_T = 2
LATENT = Q_LORA_T + KV_LORA_T
GATE0 = 8
L0_COLS = [0, 128, 256, 384, 512, 640, 672, 800] + [928 + P * j for j in range(8)]

STAGES = [("a_in", 32), ("a_out", 8), ("kv", 16), ("qz", 16), ("b_out", 8), ("l0", 16),
          ("uq", 9), ("ukv", 12), ("mem", 4), ("l0_out", 8)]
FIRST = {}
_n = 0
for _name, _count in STAGES:
    FIRST[_name] = _n
    _n += _count
CHUNKS = _n
COUNT = dict(STAGES)
KTILES = {"uq": Q_LORA_T, "ukv": KV_LORA_T}
LAST = {name: FIRST[name] + count - 1 for name, count in STAGES}
INPUT_AT = {"ukv": Q_LORA_T * 1024, "mem": (Q_LORA_T + KV_LORA_T) * 1024}

VECTORS = [("a_b", 24), ("kv_b", 16), ("b_b", 24), ("a_g", 8), ("kv_g", 8), ("b_g", 8),
           ("f1_g", 8), ("l0_g", 8), ("q_g", 3), ("ckv_g", 2), ("mem_g", 8), ("f2_g", 8),
           ("conv", 24), ("freq", 1)]
COL = {}
_n = 0
for _name, _count in VECTORS:
    COL[_name] = _n
    _n += _count
NVEC = _n

TWO_PI = 2.0 * math.pi
C1 = 6.28125
C2 = float(np.float32(np.round((TWO_PI - C1) * 2.0 ** 23) / 2.0 ** 23))
C3 = TWO_PI - C1 - C2
MAGIC = 1.5 * 2.0 ** 23
PI_F = float(np.nextafter(np.float32(math.pi), np.float32(0)))

SLOT_W = TOK + 4


LOOP = True


PAIRED = ("a_in", "a_out", "kv", "qz", "b_out", "l0", "l0_out")
BEHIND = 1


def repeat(eng, first, end, body):
    if LOOP and end - first > 1:
        with eng.Fori(first, end) as i:
            body(i)
    else:
        for i in range(first, end):
            body(i)


def build(nc, wall, vecs, xT, c_row, mod_w, pos, memT, out):
    ctx = ExitStack()

    def sb(name, shape, dt=F32):
        return ctx.enter_context(nc.sbuf_tensor(name, shape, dt))

    def sem(name):
        return ctx.enter_context(nc.semaphore(name))

    def dram(name, shape):
        return nc.dram_tensor(name, shape, F32, kind="Internal").ap()
    kv_d = dram("kv_d", [2 * D, TOK])
    qz_d = dram("qz_d", [2 * D, TOK])
    o_d = dram("o_d", [D, TOK])
    l0_d = dram("l0_d", [16 * P, TOK])
    q2_d = dram("q2_d", [9 * P, TOK])
    qr_d = dram("qr_d", [2, MLA_HEADS * RH, TOK])
    kr_d = dram("kr_d", [ROPE, TOK])
    kv2_d = dram("kv2_d", [MLA_HEADS * P, TOK])
    mkv_d = dram("mkv_d", [4 * P, N_MEM])
    br_d = dram("br_d", [D, TOK])
    cs_d = dram("cs_d", [2, 6 * RH, TOK])

    with ctx:
        R = sb("R", [P, KT * TOK])
        HH = sb("HH", [P, KT * TOK], F32R)
        HL = sb("HL", [P, KT * TOK], F32R)
        WST = sb("WST", [P, 2, D])
        WH = sb("WH", [P, 2, D], F32R)
        WL = sb("WL", [P, 2, D], F32R)
        ACC = sb("ACC", [P, 6, TOK])
        XS = sb("XS", [P, 3, TOK])
        SC = sb("SC", [P, 4, SLOT_W])
        QH = sb("QH", [P, 2, TOK], F32R)
        QL = sb("QL", [P, 2, TOK], F32R)
        VV = sb("VV", [P, TOK], F32R)
        VS = sb("VS", [P, 2, TOK], F32R)
        IDF = sb("IDF", [P, P])
        IDR = sb("IDR", [P, P], F32R)
        ONE = sb("ONE", [P, P])
        LATER = sb("LATER", [P, P])
        VEC = sb("VEC", [P, NVEC])
        MS = sb("MOD_SUMS", [P, 64])
        MT = sb("MOD_SUMS_12", [P, 12])
        MOD = sb("MOD", [P, 64])
        GS = sb("GS", [P, 24])
        G2 = sb("G2", [P, 16])
        SM = sb("SM", [P, 4, 8])
        COLS = sb("COLS", [P, 8, 4])

        PS = ctx.enter_context(nc.psum_tensor("PS", [P, 8, HALF], F32))

        c_loaded = sem("c_loaded")
        vec_loaded = sem("vec_loaded")
        w_hi = sem("w_hi")
        w_lo = sem("w_lo")
        chunk_done = sem("chunk_done")
        psum_freed = sem("psum_freed")
        consts = sem("consts")
        x3_ready = sem("x3_ready")
        consts_r = sem("consts_r")
        silu_c = sem("silu_c")
        mod_acc = sem("mod_acc")
        acc_clear = sem("acc_clear")
        mod_kept = sem("mod_kept")
        mod_ready = sem("mod_ready")
        sq_done = sem("sq_done")
        acc_done = sem("acc_done")
        stat_mm = sem("stat_mm")
        stat_dve = sem("stat_dve")
        stat_act = sem("stat_act")
        t_ready = sem("t_ready")
        hi_ready = sem("hi_ready")
        h_ready = sem("h_ready")
        y_ready = sem("y_ready")
        conv_seq = sem("conv_seq")
        tab_seq = sem("tab_seq")
        tab_stored = sem("tab_stored")
        sin_done = sem("sin_done")
        rope_seq = sem("rope_seq")
        pos_loaded = sem("pos_loaded")
        cs_loaded = sem("cs_loaded")
        mem_loaded = sem("mem_loaded")
        qk_hi = sem("qk_hi")
        qk_lo = sem("qk_lo")
        s_done = sem("s_done")
        m_done = sem("m_done")
        nb_done = sem("nb_done")
        e_done = sem("e_done")
        rc_done = sem("rc_done")
        p_done = sem("p_done")
        scan_done = sem("scan_done")
        tr_done = sem("tr_done")
        th_done = sem("th_done")
        tl_done = sem("tl_done")
        av_done = sem("av_done")
        ob_done = sem("ob_done")
        oo_done = sem("oo_done")
        out_ready = sem("out_ready")
        x_loaded = [sem(f"x_loaded{i}") for i in range(8)]
        w_loaded = [sem(f"w_loaded{i}") for i in range(2)]
        xs_loaded = [sem(f"xs_loaded{i}") for i in range(3)]
        gate_loaded = [sem(f"gate_loaded{i}") for i in range(2)]
        es_stored = [sem(f"es_stored{i}") for i in range(2)]
        rope_stored = [sem(f"rope_stored{i}") for i in range(2)]
        o_stored = [sem(f"o_stored{i}") for i in range(2)]
        out_stored = [sem(f"out_stored{i}") for i in range(4)]

        MASK = QL[:, 0, :]

        def rk(k):
            return R[:, bass.ds(k * TOK, TOK)]

        def hk(h, k, n=TOK, name=None):
            c = INPUT_AT.get(name, 0) + k * n
            return h[:, c:c + n]

        def width(name):
            return KTILES.get(name, KT) * P

        def two(ap):
            return ap.rearrange("p (a b) -> p a b", a=2)

        def chunk_psum(par, ntok=TOK):
            return PS[:, 2 * par:2 * par + 2, :] if ntok == TOK else PS[:, 2 * par, 0:ntok]

        def like(ap, ntok=TOK):
            return two(ap) if ntok == TOK else ap

        def vcol(name, k=0, n=1):
            return VEC[:, COL[name] + k:COL[name] + k + n]

        def work(s, n=TOK):
            return SC[:, s, 0:n]

        def xs(s, n=TOK, rows=P):
            return XS[0:rows, s, 0:n]

        def tiles(t):
            return t.rearrange("(m p) n -> m p n", p=P)

        def y_tile(k):
            if k < 4:
                return ACC[:, 2 + k, :]
            return xs(k - 4) if k < KT - 1 else work(2)

        def silu_row():
            return ACC[:, 0, :]

        def table(i):
            return ACC[0:6 * RH, i, :]

        def square(name, j, ntok=TOK):
            if name in ("uq", "ukv", "mem"):
                return ACC[:, 2 + j, 0:ntok]
            return work(j, ntok)

        def mem_tile(k):
            return ACC[:, 4 + k // 4, (k % 4) * N_MEM:(k % 4 + 1) * N_MEM]

        def wall_at(g, w):
            return wall[bass.ds(g, 1), :, 0:w].rearrange("a p n -> (a p) n")

        def latent(k):
            return xs(k) if k < Q_LORA_T else ACC[:, k - Q_LORA_T, :]

        XSN = {}
        at = [0, 0, 0]

        def plan(stage, slots, dmas=None):
            for n, s in enumerate(slots):
                at[s] += 16 * (dmas[n] if dmas else 1)
                XSN[stage, n] = (s, at[s])

        plan("mod_a", [n % 3 for n in range(16)])
        plan("mod_rest", [(n + 1) % 3 for n in range(48)])
        plan("sb", [0, 1, 2] * SB_HEADS, [2, 2, 2] * SB_HEADS)
        plan("bo", [k % 3 for k in range(8)])
        plan("rope", [0, 1] * 3)
        plan("mla", [0, 1, 2] * MLA_HEADS, [3, 2, 2] * MLA_HEADS)
        plan("memory", [0, 1, 2] * MEM_HEADS, [2, 2, 2] * MEM_HEADS)
        plan("lo", [k % 3 for k in range(8)])

        def xs_count(stage, n0, per, i):
            s, c = XSN[stage, n0]
            if (stage, n0 + per) not in XSN:
                return s, c
            return s, c + (XSN[stage, n0 + per][1] - c) * i

        H0, hb = {}, 0
        for name, kts in [("a_in", 8), ("a_out", 8), ("kv", 8), ("qz", 8), ("b_out", 8), ("l0", 8),
                          ("uq", 3), ("ukv", 2), ("mem", 8), ("l0_out", 8)]:
            H0[name] = hb
            hb += kts
        T0, tb = {}, 0
        for name, kts in [("a_in", 8), ("kv", 8), ("qz", 8), ("b_out", 8), ("l0", 8),
                          ("uq", 3), ("ukv", 2), ("mem", 8), ("l0_out", 8)]:
            T0[name] = tb
            tb += kts
        SQ, STAT, sq, add = {}, {}, 0, 0
        stat_no = [0, 0, 0]
        for name, c in [("a_in", 8), ("kv", 8), ("l0", 8), ("uq", 3), ("ukv", 2), ("mem", 8),
                        ("final", 8)]:
            SQ[name], STAT[name] = (sq, c, add), tuple(stat_no)
            sq += c
            add += 1 + c * (2 if name == "l0" else 1)
            stat_no = [stat_no[0] + 1, stat_no[1] + (3 if name == "l0" else 2),
                       stat_no[2] + (4 if name == "l0" else 2)]
        ES0, STORED, es = {}, {}, [0, 0]
        for name in ("kv", "qz", "l0", "uq", "ukv", "mem"):
            skip = LATENT if name == "l0" else 0
            ES0[name] = (es[0] - 16 * ((skip + 1) // 2), es[1] - 16 * (skip // 2))
            for m in range(skip, COUNT[name]):
                es[m % 2] += 16
            STORED[name] = tuple(es)
        ES_END = tuple(es)
        G0 = {"b_out": 0, "l0_out": 64}
        TABLE_STEPS = 18
        ROPE_STEPS = 6

        class Pass:

            def __init__(self, name, heads, rows, causal, scale, nk):
                self.name, self.heads, self.rows, self.causal = name, heads, rows, causal
                self.scale, self.nk, self.stacked = scale, nk, rows == HEAD
                self.nkt = [(t + 1 if causal else nk // P) for t in range(8)]
                self.halves = [(n + 3) // 4 for n in self.nkt]
                self.vsteps = (nk // P + 3) // 4
                self.before = [sum(self.halves[:t]) for t in range(8)]
                self.per = sum(self.halves)
                self.s_ahead = 3
                self.e_ahead = 3 if causal else 2
                self.p_ahead = 2 if causal else 1
                self.round_at = (1, 2, 3) if causal else (1, 2, 4)

        sbk = Pass("sb", SB_HEADS, HEAD, True, 1.0 / math.sqrt(HEAD), TOK)
        mla = Pass("mla", MLA_HEADS, HEAD + ROPE, False, 1.0 / math.sqrt(HEAD + ROPE), TOK)
        mmx = Pass("memory", MEM_HEADS, HEAD, False, 1.0 / math.sqrt(HEAD), N_MEM)
        heads = th = tl = soft = 0
        for a in (sbk, mla, mmx):
            a.head0, a.th0, a.tl0, a.soft0 = heads, th, tl, soft
            heads += a.heads
            th += a.heads * a.per
            tl += a.heads * (a.per + a.vsteps)
            soft += 0 if a.causal else 8 * a.heads

        def th_count(a, h, t, half):
            return a.th0 + h * a.per + a.before[t] + half + 1

        def tl_count(a, h, t, half):
            return a.tl0 + h * (a.per + a.vsteps) + a.before[t] + min(t, a.vsteps) + half + 1

        def v_count(a, h, step):
            return a.tl0 + h * (a.per + a.vsteps) + a.before[step + 1] + step + 1

        def heads_of(eng, a, body):
            body(0, 0, True, False)
            body(1, 1, False, False)

            def pair(i):
                for j in range(2):
                    body(2 * i + j, j, False, False)
            repeat(eng, 1, a.heads // 2 - 1, pair)
            body(a.heads - 2, 0, False, False)
            body(a.heads - 1, 1, False, True)

        def keys_by_queries(H, a, t, half):
            lo, hi = 4 * half, min(a.nkt[t], 4 * half + 4)
            hf, q = t // 4, (t % 4) * P
            v = H[:, 4096 * hf:4096 * hf + 4096].rearrange("p (k q) -> p k q", q=HALF)
            return v[:, lo:hi, q:q + P], hi - lo

        def parity(a, t, half, j):
            return (tl_count(a, j, t, half) - 1) % 2

        def v_parity(a, step, j):
            return (v_count(a, j, step) - 1) % 2

        block = ctx.enter_context(nc.Block())

        @block.sync
        def _(sp):
            def xs_load(slot, dst, src):
                sp.dma_start(dst, src).then_inc(xs_loaded[slot], 16)

            def load_chunk(g, par, w=D):
                sp.wait_ge(w_lo, g - 1)
                sp.dma_start(WST[:, par, 0:w], wall_at(g, w)).then_inc(w_loaded[par], 16)

            def stream(first, end, w=D):
                if (end - first) % 2:
                    load_chunk(first, first % 2, w)
                    first += 1

                def pair(i):
                    for j in range(2):
                        load_chunk(first + 2 * i + j, (first + j) % 2, w)
                repeat(sp, 0, (end - first) // 2, pair)

            sp.dma_start(VEC[:], vecs).then_inc(vec_loaded, 16)
            for k in range(8):
                sp.dma_start(rk(k), xT[k]).then_inc(x_loaded[k], 16)
                if k == 3:
                    sp.dma_start(silu_row(), c_row.to_broadcast([P, D])).then_inc(c_loaded, 16)
            for n in range(16):
                if n >= 3:
                    sp.wait_ge(mod_acc, n - 2)
                xs_load(n % 3, xs(n % 3), mod_w[n])
                if n in (6, 9):
                    g = (n - 6) // 3
                    sp.dma_start(WST[:, g, :], wall_at(g, D)).then_inc(w_loaded[g], 16)

            def a_in(c, first):
                for i in range(4):
                    load_chunk(4 * c + i + 2, i % 2)
                    for n in range(3 * i, 3 * i + 3):
                        slot, _ = XSN["mod_rest", n]
                        if first and n < 3:
                            sp.wait_ge(h_ready, 8)
                        else:
                            sp.wait_ge(mod_acc, 16 + 12 * c + n - 2)
                        xs_load(slot, xs(slot),
                                mod_w[bass.ds(16 + 12 * c + n, 1)].rearrange("a p n -> (a p) n"))
            a_in(0, True)
            repeat(sp, 1, 4, lambda c: a_in(c, False))
            stream(4 * 4 + 2, FIRST["kv"])
            sp.wait_ge(h_ready, H0["a_out"] + 8)
            sp.dma_start(table(4).bitcast(I32), pos.to_broadcast([6 * RH, TOK]))\
                .then_inc(pos_loaded, 16)
            stream(FIRST["kv"], FIRST["b_out"] + 2)

            def rows(t, r, n):
                return t[bass.ds(r, n), :]

            def load_head(a, h):
                g = 3 * (a.head0 + h)
                sp.wait_ge(qk_lo, g - 2 if not (isinstance(h, int) and h == 0) else g)
                if a is mla:
                    xs_load(0, XS[0:HEAD, 0, :], rows(q2_d, MLA_HEADS * ROPE + HEAD * h, HEAD))
                    for s in range(2):
                        xs_load(0, XS[HEAD + RH * s:HEAD + RH * s + RH, 0, :],
                                rows(qr_d[s], RH * h, RH))
                else:
                    for s in range(2):
                        xs_load(0, XS[HEAD * s:HEAD * s + HEAD, 0, :],
                                rows(qz_d, HEAD * h, HEAD) if a is sbk else
                                rows(l0_d, 6 * P + HEAD * h, HEAD))
                sp.wait_ge(qk_lo, g - 1 if not (isinstance(h, int) and h == 0) else g)
                if a is mla:
                    xs_load(1, XS[0:HEAD, 1, :], rows(kv2_d, P * h, HEAD))
                    xs_load(1, XS[HEAD:HEAD + ROPE, 1, :], kr_d)
                else:
                    for s in range(2):
                        xs_load(1, XS[HEAD * s:HEAD * s + HEAD, 1, 0:a.nk],
                                rows(kv_d if a is sbk else mkv_d, HEAD * h, HEAD))
                sp.wait_ge(qk_lo, g)
                for s in range(2):
                    src = rows(kv_d, D + HEAD * h, HEAD) if a is sbk else (
                        rows(kv2_d, P * h + HEAD, HEAD) if a is mla else
                        rows(mkv_d, MEM_HEADS * HEAD + HEAD * h, HEAD))
                    xs_load(2, XS[HEAD * s:HEAD * s + HEAD, 2, 0:a.nk], src)

            def store_out(a, h, hf, row0, dst):
                sp.wait_ge(oo_done, 2 * (a.head0 + h) + hf + 1)
                sp.dma_start(dst[bass.ds(row0 + HEAD * h, HEAD), hf * HALF:(hf + 1) * HALF],
                             ACC[0:HEAD, 2 + hf, 0:HALF]).then_inc(o_stored[hf], 16)

            def attend(a, dst, row0, ahead):
                def head(h, j, first, last):
                    if not first:
                        store_out(a, h - 1, 1, row0, dst)
                    if isinstance(h, int) and h >= a.heads - 2:
                        ahead[h - a.heads + 2]()
                    else:
                        load_head(a, h + 2)
                    store_out(a, h, 0, row0, dst)
                heads_of(sp, a, head)
                store_out(a, a.heads - 1, 1, row0, dst)

            def load_product(stage, name, product, gate0, gate_d, head0, heads, tiles_):
                for k in tiles_:
                    if k == 0:
                        sp.wait_ge(qk_lo, 3 * heads)
                    if k >= 2:
                        sp.wait_ge(t_ready, T0[name] + k - 1)
                    sp.dma_start(ACC[:, 4 + k % 2, :], gate_d[gate0 + k])\
                        .then_inc(gate_loaded[k % 2], 16)
                    if k >= 3:
                        sp.wait_ge(h_ready, H0[name] + k - 2)
                    for s in range(2):
                        sp.wait_ge(o_stored[s], 16 * (head0 + 2 * k + 2))
                    xs_load(k % 3, xs(k % 3), product[k * P:(k + 1) * P, :])

            for s in range(2):
                sp.wait_ge(es_stored[s], ES0["qz"][s] + 16)
            sp.wait_ge(h_ready, H0["qz"] + 8)
            load_head(sbk, 0)
            for s in range(2):
                sp.wait_ge(es_stored[s], STORED["qz"][s])

            def load_b_out(tiles_):
                load_product("bo", "b_out", o_d, KT, tiles(qz_d), 0, SB_HEADS, tiles_)
            load_head(sbk, 1)
            attend(sbk, o_d, 0, (lambda: load_b_out(range(0, 2)), lambda: None))
            load_b_out(range(2, 8))
            sp.wait_ge(t_ready, T0["b_out"] + 8)
            sp.dma_start(ACC[:, 4:6, :].rearrange("p a b -> p (a b)"), memT).then_inc(mem_loaded, 16)
            stream(FIRST["b_out"] + 2, FIRST["uq"])

            def load_rope(b):
                n = 6 * RH if b else RH
                if b:
                    sp.wait_ge(rope_seq, ROPE_STEPS * b)
                for s in range(2):
                    row = MLA_HEADS * RH * s + 6 * RH * (b - 1) if b else 5 * P + RH * s
                    xs_load(s, XS[0:n, s, :], (q2_d if b else l0_d)[row:row + n, :])

            def store_rope(b):
                n = 6 * RH if b else RH
                for s in range(2):
                    sp.wait_ge(rope_seq, ROPE_STEPS * b + 3 * s + 3)
                    dst = qr_d[s][n * (b - 1):n * b, :] if b else kr_d[RH * s:RH * s + RH, :]
                    sp.dma_start(dst, SC[0:n, 2 + s, 0:TOK]).then_inc(rope_stored[s], 16)

            def latent_stored(name, m):
                for s in range(2):
                    sp.wait_ge(es_stored[s], ES0[name][s] + 16 * ((m + 1 - s) // 2))

            def first_rope():
                sp.wait_ge(h_ready, H0["mem"] + 8)
                for s in range(2):
                    sp.dma_start(ACC[0:6 * RH, 4 + s, :], cs_d[s]).then_inc(cs_loaded, 16)
                latent_stored("l0", 6)
                load_rope(0)
            between = {4: [first_rope],
                       7: [lambda: store_rope(0)],
                       8: [lambda: latent_stored("uq", Q_LORA_T), lambda: load_rope(1)],
                       13: [lambda: store_rope(1), lambda: load_rope(2)],
                       18: [lambda: store_rope(2)]}
            n = 0
            for name in ("uq", "ukv", "mem"):
                for g in range(FIRST[name], LAST[name] + 1):
                    load_chunk(g, g % 2, width(name))
                    for step in between.get(n, []):
                        step()
                    n += 1
            stream(FIRST["l0_out"], FIRST["l0_out"] + 2)

            for s in range(2):
                sp.wait_ge(es_stored[s], STORED["ukv"][s])
                sp.wait_ge(rope_stored[s], 48)
            load_head(mla, 0)
            for s in range(2):
                sp.wait_ge(es_stored[s], ES_END[s])

            def load_l0_out(tiles_):
                load_product("lo", "l0_out", br_d, GATE0, tiles(l0_d), SB_HEADS,
                             SB_HEADS + MLA_HEADS + MEM_HEADS, tiles_)
            load_head(mla, 1)
            attend(mla, br_d, 0, (lambda: load_head(mmx, 0), lambda: load_head(mmx, 1)))
            attend(mmx, br_d, MLA_HEADS * HEAD,
                   (lambda: load_l0_out(range(0, 2)), lambda: None))
            load_l0_out(range(2, 8))
            stream(FIRST["l0_out"] + 2, CHUNKS)
            for k in range(8):
                sp.wait_ge(out_ready, k + 1)
                sp.dma_start(out[k], work(k % 4)).then_inc(out_stored[k % 4], 16)
            for s in range(4):
                sp.wait_ge(out_stored[s], 32)

        @block.gpsimd
        def _(pool):
            gp = nc.gpsimd
            gp.memset(ONE[:], 1.0).then_inc(consts, 1)
            gp.memset(IDF[:], 0.0).then_inc(consts, 1)
            pool.wait_ge(consts, 2)
            gp.affine_select(out=IDF[:], in_=IDF[:], compare_op=ALU.not_equal, fill=1.0, base=0,
                             pattern=[[-1, P]], channel_multiplier=1).then_inc(consts, 1)
            gp.affine_select(out=LATER[:], in_=ONE[:], compare_op=ALU.is_ge, fill=0.0, base=0,
                             pattern=[[1, P]], channel_multiplier=-1).then_inc(consts, 1)

            def lo_chunk(g, par, w):
                pool.wait_ge(w_hi, g + 1)
                gp.tensor_tensor(WL[:, par, 0:w], WST[:, par, 0:w], WH[:, par, 0:w].bitcast(F32),
                                 ALU.subtract).then_inc(w_lo, 1)

            def lo_chunks(first, end, w=D):
                if (end - first) % 2:
                    lo_chunk(first, first % 2, w)
                    first += 1

                def pair(i):
                    for j in range(2):
                        lo_chunk(first + 2 * i + j, (first + j) % 2, w)
                repeat(pool, 0, (end - first) // 2, pair)

            def lo_head(a, h, j, which):
                g = 3 * (a.head0 + h)
                pool.wait_ge(qk_lo, g + which)
                pool.wait_ge(qk_hi, g + which + 1)
                r = P if a.stacked else a.rows
                if which == 0 and a.stacked:
                    q = QH[HEAD:P, j, :]
                    gp.tensor_tensor(q, XS[HEAD:P, 0, :], q.bitcast(F32), ALU.subtract)\
                        .then_inc(qk_lo, 1)
                elif which == 0:
                    gp.tensor_tensor(QL[0:r, j, :], XS[0:r, 0, :], QH[0:r, j, :].bitcast(F32),
                                     ALU.subtract).then_inc(qk_lo, 1)
                elif which == 1:
                    gp.tensor_tensor(WL[0:r, j, 0:a.nk], XS[0:r, 1, 0:a.nk],
                                     WH[0:r, j, 0:a.nk].bitcast(F32), ALU.subtract)\
                        .then_inc(qk_lo, 1)
                else:
                    v = VV[HEAD:P, 0:a.nk]
                    gp.tensor_tensor(v, XS[HEAD:P, 2, 0:a.nk], v.bitcast(F32), ALU.subtract)\
                        .then_inc(qk_lo, 1)

            def output(a, h, hf, split):
                g = a.head0 + h
                pool.wait_ge(qk_lo, split)
                pool.wait_ge(ob_done, 2 * (2 * g + hf + 1))
                if not (isinstance(g, int) and g == 0):
                    pool.wait_ge(o_stored[hf], 16 * g)
                gp.tensor_tensor(ACC[0:HEAD, 2 + hf, 0:HALF], ACC[0:HEAD, hf, 0:HALF],
                                 ACC[0:HEAD, hf, HALF:TOK], ALU.add).then_inc(oo_done, 1)

            def attend(a, following=None):
                def head(h, j, first, last):
                    g = a.head0 + h
                    nxt = (a, h + 1, 1 - j) if not last else (following, 0, 0) if following else None
                    if not first:
                        output(a, h - 1, 0, 3 * (g + 1))
                        pool.wait_ge(oo_done, 2 * g - 1)
                    if nxt:
                        lo_head(*nxt, 0)
                        lo_head(*nxt, 1)
                    if not first:
                        output(a, h - 1, 1, 3 * (g + 1) + (2 if nxt else 0))
                        pool.wait_ge(oo_done, 2 * g)
                    if nxt:
                        lo_head(*nxt, 2)
                heads_of(pool, a, head)
                g = a.head0 + a.heads - 1
                for hf in range(2):
                    output(a, a.heads - 1, hf, 3 * (g + (2 if following else 1)))
                    pool.wait_ge(oo_done, 2 * g + hf + 1)

            lo_chunks(0, FIRST["b_out"])
            pool.wait_ge(w_lo, FIRST["b_out"])
            for which in range(3):
                lo_head(sbk, 0, 0, which)
            attend(sbk)
            lo_chunks(FIRST["b_out"], FIRST["uq"])
            for name in ("uq", "ukv", "mem"):
                lo_chunks(FIRST[name], LAST[name] + 1, width(name))
            pool.wait_ge(w_lo, FIRST["l0_out"])
            for which in range(3):
                lo_head(mla, 0, 0, which)
            attend(mla, mmx)
            attend(mmx)
            lo_chunks(FIRST["l0_out"], CHUNKS)

        @block.scalar
        def _(act):
            sc = nc.scalar

            def stage(name, bodies, following=None, begin=0):
                g0, n = FIRST[name], COUNT[name]

                def step(body, m, j, half, last):
                    g, par = g0 + m, (g0 + j) % 2
                    if (following or not last) and not (
                            name in PAIRED and isinstance(m, int) and m == 0):
                        w = width(following if last else name)
                        act.wait_ge(w_loaded[1 - par], 16 * (half + par + 1))
                        act.wait_ge(chunk_done, g)
                        sc.activation(WH[:, 1 - par, 0:w], WST[:, 1 - par, 0:w], ACT.Copy)\
                            .then_inc(w_hi, 1)
                    body(m, j, g, par)

                begin //= 2
                for end, body in bodies:
                    def pair(i, last=False):
                        for j in range(2):
                            step(body, 2 * i + j, j, (g0 + j) // 2 + i, last and j == 1)
                    pairs = end // 2
                    tail = end == n and n % 2 == 0
                    if begin == 0:
                        pair(0)
                        begin = 1
                    repeat(act, begin, pairs - tail, pair)
                    if tail:
                        pair(pairs - 1, True)
                    begin = pairs
                if n % 2:
                    step(body, n - 1, 0, (g0 + n - 1) // 2, True)

            def head_chunks(name, end, body):
                for m in range(end):
                    g = FIRST[name] + m
                    par = g % 2
                    if m > 0:
                        act.wait_ge(w_loaded[1 - par], 16 * (g // 2 + par + 1))
                        act.wait_ge(chunk_done, g)
                        sc.activation(WH[:, 1 - par, :], WST[:, 1 - par, :], ACT.Copy)\
                            .then_inc(w_hi, 1)
                    body(m, m % 2, g, par)

            def first_chunk(g):
                act.wait_ge(w_loaded[g % 2], 16 * (g // 2 + 1))
                sc.activation(WH[:, g % 2, :], WST[:, g % 2, :], ACT.Copy).then_inc(w_hi, 1)

            def second_chunk(name):
                g = FIRST[name] + 1
                act.wait_ge(w_loaded[g % 2], 16 * (g // 2 + 1))
                if g > 1:
                    act.wait_ge(chunk_done, g - 1)
                sc.activation(WH[:, g % 2, :], WST[:, g % 2, :], ACT.Copy).then_inc(w_hi, 1)

            def store_chunk(name, dst, func=ACT.Copy, ntok=TOK):
                def body(m, j, g, par):
                    act.wait_ge(chunk_done, g + 1)
                    act.wait_ge(es_stored[j], ES0[name][j] + 8 * (m - j))
                    sc.activation(like(work(j, ntok), ntok), chunk_psum(par, ntok), func)\
                        .then_inc(psum_freed, 1)
                    act.wait_ge(psum_freed, g + 1)
                    act.dma_start(dst[bass.ds(m, 1)].rearrange("a p n -> (a p) n"),
                                  work(j, ntok)).then_inc(es_stored[j], 16)
                return body

            def squares(name, k, src, ntok=TOK):
                act.wait_ge(acc_done, SQ[name][2] + k)
                sc.activation(square(name, k % 2, ntok), src, ACT.Square).then_inc(sq_done, 1)

            def rstd(name):
                act.wait_ge(stat_dve, STAT[name][2] + (4 if name == "l0" else 2))
                rows = 2 if name == "l0" else 1
                sc.activation(SM[:, 0:rows, :], SM[:, 2:2 + rows, :], ACT.Sqrt)\
                    .then_inc(stat_act, 1)

            def hi_tiles(name, kts, src, shift=None, ntok=TOK, ready=None):
                for k in range(kts):
                    if ready is None:
                        act.wait_ge(t_ready, T0[name] + k + 1)
                    else:
                        act.wait_ge(ready, k + 1)
                    if k == 0 and name not in INPUT_AT:
                        act.wait_ge(chunk_done, FIRST[name])
                    if shift is None:
                        sc.activation(hk(HH, k, ntok, name), src(k), ACT.Copy)\
                            .then_inc(hi_ready, 1)
                    else:
                        sc.activation(hk(HH, k, ntok), src(k), ACT.Identity, bias=shift(k))\
                            .then_inc(hi_ready, 1)

            for k in range(8):
                act.wait_ge(x_loaded[k], 16)
                squares("a_in", k, rk(k))
                if k == 5:
                    act.wait_ge(c_loaded, 16)
                    sc.activation(silu_row(), silu_row(), ACT.Silu).then_inc(silu_c, 1)
            rstd("a_in")
            first_chunk(0)
            second_chunk("a_in")
            hi_tiles("a_in", 8, lambda k: xs(k % 3), lambda k: MOD[:, k:k + 1])
            def a_in(c, first=False):
                for i in range(4):
                    g, par = 4 * c + i, i % 2
                    if i or not first:
                        act.wait_ge(w_loaded[1 - par], 16 * (2 * c + (i + 1) // 2 + 1))
                        act.wait_ge(chunk_done, g)
                        sc.activation(WH[:, 1 - par, :], WST[:, 1 - par, :], ACT.Copy)\
                            .then_inc(w_hi, 1)
                    if i == 0:
                        act.wait_ge(chunk_done, g + 1)
                        sc.activation(two(work(0)), chunk_psum(par), ACT.Copy)\
                            .then_inc(psum_freed, 1)
                    if i == 3:
                        act.wait_ge(chunk_done, g + 1)
                        act.wait_ge(psum_freed, g)
                        sc.activation(two(work(3)), chunk_psum(par), ACT.Silu)\
                            .then_inc(psum_freed, 1)
            a_in(0, True)
            repeat(act, 1, 8, a_in)
            second_chunk("a_out")
            hi_tiles("a_out", 8, y_tile, ready=y_ready)

            def out_squares(stat):
                def body(m, j, g, par):
                    act.wait_ge(psum_freed, g + 1)
                    act.wait_ge(acc_done, SQ[stat][2] + (2 * m - 1 if stat == "l0" else m))
                    sc.activation(work(j), rk(m), ACT.Square).then_inc(sq_done, 1)
                return body
            stage("a_out", [(8, out_squares("kv"))], "kv")
            second_chunk("kv")
            rstd("kv")
            hi_tiles("kv", 8, lambda k: xs(k % 3), lambda k: MOD[:, 24 + k:25 + k])
            store_kv = store_chunk("kv", tiles(kv_d))

            def kv_chunk(m, j, g, par):
                store_kv(m, j, g, par)
                if m in (3, 5):
                    n = (m - 3) // 2
                    act.wait_ge(tab_seq, 2 + 7 * (n + 1))
                    sc.activation(table(4 + n), table(3 - 3 * n), ACT.Sin).then_inc(sin_done, 1)
                    act.wait_ge(sin_done, n + 1)
                    act.dma_start(cs_d[1 - n], table(4 + n)).then_inc(tab_stored, 16)
            head_chunks("kv", 6, kv_chunk)
            stage("kv", [(16, store_kv)], "qz", begin=6)
            act.wait_ge(tab_stored, 32)
            second_chunk("qz")
            hi_tiles("qz", 8, lambda k: xs(k % 3), lambda k: MOD[:, 40 + k:41 + k])
            stage("qz", [(8, store_chunk("qz", tiles(qz_d))),
                         (16, store_chunk("qz", tiles(qz_d), ACT.Silu))])

            def hi_head(a, h, j, which):
                n = 3 * h + which
                s, c = xs_count(a.name, which, 3, h)
                act.wait_ge(xs_loaded[s], c)
                if which == 2:
                    if a is mmx and isinstance(h, int) and h == 0:
                        act.wait_ge(tr_done, v_count(mla, MLA_HEADS - 1, mla.vsteps - 1))
                    elif not (isinstance(h, int) and h == 0):
                        act.wait_ge(tr_done, v_count(a, h - 1, a.vsteps - 1))
                    sc.activation(VV[:, 0:a.nk], xs(2, a.nk), ACT.Copy).then_inc(qk_hi, 1)
                    return
                if a is mmx or not (isinstance(h, int) and h < 2):
                    act.wait_ge(s_done, 8 * (a.head0 + h - 1))
                r = P if a.stacked else a.rows
                if which == 0:
                    sc.activation(QH[0:r, j, :], xs(0, TOK, r), ACT.Copy).then_inc(qk_hi, 1)
                else:
                    sc.activation(WH[0:r, j, 0:a.nk], xs(1, a.nk, r), ACT.Copy).then_inc(qk_hi, 1)

            def scores_in(t, n):
                if n <= HALF:
                    return PS[:, 2 * (t % 2), 0:n]
                return PS[:, 2 * (t % 2):2 * (t % 2) + 2, :].rearrange("p a b -> p (a b)")[:, 0:n]

            def prob(a, h, t):
                u = 8 * (a.head0 + h) + t
                n = a.nkt[t] * P
                if a.causal:
                    act.wait_ge(s_done, u + 1)
                    sc.activation(SC[:, t % 4, 0:n], scores_in(t, n), ACT.Sigmoid, scale=-a.scale)\
                        .then_inc(e_done, 1)
                else:
                    act.wait_ge(nb_done, a.soft0 + 8 * h + t + 1)
                    sc.activation(SC[:, t % 4, 0:n], scores_in(t, n), ACT.Exp, scale=a.scale,
                                  bias=COLS[:, t, 1:2], accum_out=COLS[:, t, 2:3])\
                        .then_inc(e_done, 1)

            def hi_tile(a, h, j, t, half):
                dst, n = keys_by_queries(HH, a, t, half)
                act.wait_ge(tr_done, tl_count(a, h, t, half))
                src = PS[:, 4 + parity(a, t, half, j), 0:n * P]
                sc.activation(dst, src.rearrange("p (k q) -> p k q", q=P), ACT.Copy)\
                    .then_inc(th_done, 1)

            def lower(a, h, hf):
                act.wait_ge(av_done, 2 * (a.head0 + h) + hf + 1)
                if not (isinstance(h, int) and a.head0 + h == 0):
                    act.wait_ge(oo_done, 2 * (a.head0 + h))
                for i in range(2):
                    sc.activation(ACC[0:HEAD, hf, i * HALF:i * HALF + HALF],
                                  PS[HEAD * i:HEAD * i + HEAD, 6 + hf, :], ACT.Copy)\
                        .then_inc(ob_done, 1)

            def v_tile(a, h, j, step):
                n = min(HALF, a.nk - HALF * step)
                c = v_count(a, h, step)
                act.wait_ge(tr_done, c)
                act.wait_ge(tl_done, c - 1)
                sc.activation(VS[:, j, HALF * step:HALF * step + n],
                              PS[:, 4 + v_parity(a, step, j), 0:n].bitcast(F32R),
                              ACT.Copy).then_inc(tl_done, 1)

            def begin(a):
                for t in range(a.e_ahead):
                    prob(a, 0, t)

            def attend(a, following=None):

                def head(h, j, first, last):
                    for t in range(8):
                        nxt = (h, t + a.e_ahead) if t + a.e_ahead < 8 else \
                            (h + 1, t + a.e_ahead - 8)
                        if not a.causal:
                            if t in (0, 4) and not first:
                                lower(a, h - 1, t // 4)
                            if 1 <= t <= a.vsteps:
                                v_tile(a, h, j, t - 1)
                        hi_tile(a, h, j, t, 0)
                        if t + a.e_ahead < 8 or not last:
                            prob(a, *nxt)
                        if a.halves[t] == 2:
                            hi_tile(a, h, j, t, 1)
                        if t in a.round_at:
                            if not last:
                                hi_head(a, h + 1, 1 - j, a.round_at.index(t))
                            elif following:
                                hi_head(following, 0, 0, a.round_at.index(t))
                        if a.causal and t in (0, 4) and not first:
                            lower(a, h - 1, t // 4)
                heads_of(act, a, head)
                if following:
                    begin(following)
                for hf in range(2):
                    lower(a, a.heads - 1, hf)

            for w in range(3):
                hi_head(sbk, 0, 0, w)
            for s in range(2):
                act.wait_ge(es_stored[s], STORED["qz"][s])
            begin(sbk)
            attend(sbk)
            act.wait_ge(chunk_done, FIRST["b_out"])
            first_chunk(FIRST["b_out"])
            second_chunk("b_out")
            hi_tiles("b_out", 8, lambda k: xs(k % 3))
            stage("b_out", [(8, out_squares("l0"))], "l0")
            second_chunk("l0")
            rstd("l0")
            hi_tiles("l0", 8, lambda k: xs(k % 3))
            store_l0 = store_chunk("l0", tiles(l0_d))

            def latent_chunk(m, j, g, par):
                if m == 4:
                    rstd("uq")
                if m == 6:
                    rstd("ukv")
                if m >= LATENT:
                    store_l0(m, j, g, par)
                else:
                    act.wait_ge(chunk_done, g + 1)
                    sc.activation(two(latent(m)), chunk_psum(par), ACT.Copy)\
                        .then_inc(psum_freed, 1)
                    act.wait_ge(psum_freed, g + 1)
                    name, k = ("uq", m) if m < Q_LORA_T else ("ukv", m - Q_LORA_T)
                    squares(name, k, latent(m))
                if m == 6:
                    act.wait_ge(mem_loaded, 16)
                    for k in range(8):
                        squares("mem", k, mem_tile(k), N_MEM)
                if m == 7:
                    rstd("mem")
            head_chunks("l0", 8, latent_chunk)
            stage("l0", [(16, store_chunk("l0", tiles(l0_d), ACT.Silu))], "uq", begin=8)

            hi_tiles("uq", Q_LORA_T, latent)
            hi_tiles("ukv", KV_LORA_T, lambda k: latent(Q_LORA_T + k))
            hi_tiles("mem", 8, mem_tile, ntok=N_MEM)
            stage("uq", [(9, store_chunk("uq", tiles(q2_d)))], "ukv")
            stage("ukv", [(12, store_chunk("ukv", tiles(kv2_d)))], "mem")
            stage("mem", [(4, store_chunk("mem", tiles(mkv_d), ntok=N_MEM))])
            for w in range(3):
                hi_head(mla, 0, 0, w)
            for s in range(2):
                act.wait_ge(es_stored[s], ES_END[s])
            begin(mla)
            attend(mla, mmx)
            attend(mmx)
            act.wait_ge(chunk_done, FIRST["l0_out"])
            first_chunk(FIRST["l0_out"])
            second_chunk("l0_out")
            hi_tiles("l0_out", 8, lambda k: xs(k % 3))
            stage("l0_out", [(8, out_squares("final"))])
            rstd("final")

        @block.vector
        def _(dve):
            v = nc.vector

            def sum_clear(name):
                v.memset(SC[:, 2:4, 0:TOK] if name == "l0" else work(2), 0.0).then_inc(acc_done, 1)

            def sum_add(name, m, j, ntok=TOK):
                q0, _, a0 = SQ[name]
                dve.wait_ge(sq_done, q0 + m + 1)
                dve.wait_ge(acc_done, a0 + (2 * m if name == "l0" else m) + 1)
                if name == "l0":
                    v.scalar_tensor_tensor(out=work(3), in0=square(name, j),
                                           scalar=G2[:, bass.ds(m, 1)], in1=work(3), op0=ALU.mult,
                                           op1=ALU.add).then_inc(acc_done, 1)
                v.tensor_tensor(work(2, ntok), work(2, ntok), square(name, j, ntok), ALU.add)\
                    .then_inc(acc_done, 1)

            def stats(name, size, ntok=TOK):
                mean_squares(name, size, ntok)
                dve.wait_ge(stat_mm, STAT[name][1] + 2)

            def mean_squares(name, size, ntok=TOK):
                n, (_, mm, st) = ntok // P, STAT[name]
                dve.wait_ge(stat_mm, mm + 1)
                v.tensor_scalar(SM[:, 0, 0:n], PS[:, 4, 0:n], 1.0 / size, EPS, ALU.mult, ALU.add)\
                    .then_inc(stat_dve, 1)
                dve.wait_ge(stat_dve, st + 1)
                v.reciprocal(SM[:, 2, 0:n], SM[:, 0, 0:n]).then_inc(stat_dve, 1)

            def stats_twice():
                _, mm, st = STAT["l0"]
                dve.wait_ge(stat_mm, mm + 1)
                v.tensor_scalar(SM[:, 0, :], PS[:, 4, 0:8], 1.0 / D, EPS, ALU.mult, ALU.add)\
                    .then_inc(stat_dve, 1)
                dve.wait_ge(stat_dve, st + 1)
                v.tensor_scalar(SM[:, 2, :], SM[:, 0, :], EPS, None, ALU.mult).then_inc(stat_dve, 1)
                dve.wait_ge(stat_dve, st + 2)
                v.scalar_tensor_tensor(out=SM[:, 1, :], in0=PS[:, 4, 8:16], scalar=1.0 / D,
                                       in1=SM[:, 2, :], op0=ALU.mult, op1=ALU.add)\
                    .then_inc(stat_dve, 1)
                dve.wait_ge(stat_dve, st + 3)
                v.reciprocal(SM[:, 2:4, :], SM[:, 0:2, :]).then_inc(stat_dve, 1)
                dve.wait_ge(stat_mm, mm + 2)

            def rstd_rows(ntok=TOK):
                return PS[:, 5:7, :] if ntok == TOK else PS[:, 5, 0:ntok]

            def normed(name, kts, src, tmp, gain, shift=None, ntok=TOK):
                def scaled(k):
                    if H0[name] + k >= 3:
                        dve.wait_ge(h_ready, H0[name] + max(0, k - 2))
                    v.scalar_tensor_tensor(out=like(tmp(k), ntok), in0=like(src(k), ntok),
                                           scalar=gain(k), in1=rstd_rows(ntok), op0=ALU.mult,
                                           op1=ALU.mult).then_inc(t_ready, 1)
                for k in range(min(2, kts)):
                    scaled(k)
                for k in range(kts):
                    dve.wait_ge(hi_ready, H0[name] + k + 1)
                    if shift is None:
                        v.tensor_tensor(hk(HL, k, ntok), tmp(k), hk(HH, k, ntok).bitcast(F32),
                                        ALU.subtract).then_inc(h_ready, 1)
                    else:
                        v.scalar_tensor_tensor(out=hk(HL, k), in0=tmp(k), scalar=shift(k),
                                               in1=hk(HH, k).bitcast(F32), op0=ALU.add,
                                               op1=ALU.subtract).then_inc(h_ready, 1)
                    if k + 2 < kts:
                        scaled(k + 2)

            def mod_sum(column, slot, count):
                dve.wait_ge(xs_loaded[slot], count)
                v.tensor_tensor_reduce(xs(slot), xs(slot), silu_row(), 1.0, 0.0, ALU.mult, ALU.add,
                                       column).then_inc(mod_acc, 1)

            dve.wait_ge(consts, 4)
            v.tensor_copy(IDR[:], IDF[:]).then_inc(consts_r, 1)
            sum_clear("a_in")
            for k in range(8):
                sum_add("a_in", k, k % 2)
            dve.wait_ge(silu_c, 1)
            for n in range(16):
                slot, count = XSN["mod_a", n]
                mod_sum(MS[:, n:n + 1], slot, count)
                if n == 3:
                    mean_squares("a_in", D)
            dve.wait_ge(mod_acc, 16)
            dve.wait_ge(vec_loaded, 16)
            v.tensor_tensor(MOD[:, 0:16], MS[:, 0:16], vcol("a_b", 0, 16), ALU.add)\
                .then_inc(mod_ready, 1)
            dve.wait_ge(mod_ready, 1)
            v.scalar_tensor_tensor(out=GS[:, 0:8], in0=MOD[:, 8:16], scalar=1.0,
                                   in1=vcol("a_g", 0, 8), op0=ALU.add, op1=ALU.mult)\
                .then_inc(mod_ready, 1)
            dve.wait_ge(mod_ready, 2)
            dve.wait_ge(stat_mm, 2)
            normed("a_in", 8, rk, lambda k: xs(k % 3), lambda k: GS[:, k:k + 1],
                   lambda k: MOD[:, k:k + 1])

            v.memset(SC[:, 1, 0:2], 0.0).then_inc(acc_clear, 1)
            dve.wait_ge(acc_clear, 1)

            def a_in(c, dst, mods=False):
                def four_mods(i0):
                    if mods:
                        for i in range(i0, i0 + 4):
                            slot, count = XSN["mod_rest", i]
                            mod_sum(MT[:, i:i + 1], slot, count + 64 * c)
                cu, t = SC[:, 1, :], work(2)
                dve.wait_ge(chunk_done, 4 * c + 2)
                dve.wait_ge(psum_freed, 4 * c + 1)
                v.tensor_tensor(two(cu[:, 2:2 + TOK]), chunk_psum(1), two(work(0)), ALU.mult)\
                    .then_inc(psum_freed, 1)
                dve.wait_ge(psum_freed, 4 * c + 2)
                if not (isinstance(c, int) and c == 0):
                    dve.wait_ge(y_ready, c)
                tap = lambda i: VEC[:, bass.ds(COL["conv"] + 8 * i + c, 1)]
                v.tensor_scalar(t, cu[:, 2:2 + TOK], tap(2), None, ALU.mult).then_inc(conv_seq, 1)
                for i in (1, 0):
                    dve.wait_ge(conv_seq, 3 * c + 2 - i)
                    v.scalar_tensor_tensor(out=t, in0=cu[:, i:i + TOK], scalar=tap(i), in1=t,
                                           op0=ALU.mult, op1=ALU.add).then_inc(conv_seq, 1)
                four_mods(0)
                dve.wait_ge(chunk_done, 4 * c + 3)
                dve.wait_ge(conv_seq, 3 * c + 3)
                v.tensor_tensor(two(t), chunk_psum(0), two(t), ALU.mult).then_inc(psum_freed, 1)
                four_mods(4)
                dve.wait_ge(psum_freed, 4 * c + 4)
                v.tensor_tensor(dst, t, work(3), ALU.mult).then_inc(y_ready, 1)
                four_mods(8)
                if mods:
                    dve.wait_ge(mod_acc, 16 + 12 * (c + 1))
                    v.tensor_copy(MS[:, bass.ds(16 + 12 * c, 12)], MT[:]).then_inc(mod_kept, 1)
                    dve.wait_ge(mod_kept, c + 1)

            def y_slot(big, i):
                return big[:, bass.ds(i, 1), :].rearrange("p a n -> p (a n)")
            a_in(0, y_tile(0), mods=True)
            repeat(dve, 1, 4, lambda c: a_in(c, y_slot(ACC, 2 + c), mods=True))
            v.tensor_tensor(MOD[:, 16:64], MS[:, 16:64], vcol("a_b", 16, 48), ALU.add)\
                .then_inc(mod_ready, 1)
            dve.wait_ge(mod_ready, 3)
            for at_, name, g_ in ((32, "kv_g", 8), (48, "b_g", 16)):
                v.scalar_tensor_tensor(out=GS[:, g_:g_ + 8], in0=MOD[:, at_:at_ + 8], scalar=1.0,
                                       in1=vcol(name, 0, 8), op0=ALU.add, op1=ALU.mult)\
                    .then_inc(mod_ready, 1)
            repeat(dve, 4, 7, lambda c: a_in(c, y_slot(XS, c - 4)))
            a_in(7, y_tile(7))
            v.tensor_tensor(G2[:, 0:8], vcol("f1_g", 0, 8), vcol("f1_g", 0, 8), ALU.mult)\
                .then_inc(mod_ready, 1)
            v.tensor_tensor(G2[:, 8:16], vcol("f1_g", 0, 8), vcol("l0_g", 0, 8), ALU.mult)\
                .then_inc(mod_ready, 1)

            def lo_tiles(name):
                for k in range(8):
                    dve.wait_ge(hi_ready, H0[name] + k + 1)
                    v.tensor_tensor(hk(HL, k), y_tile(k), hk(HH, k).bitcast(F32), ALU.subtract)\
                        .then_inc(h_ready, 1)

            def out_chunks(name, stat, gate):
                g0, n = FIRST[name], COUNT[name]

                def pair(i):
                    for j in range(2):
                        m, par = 2 * i + j, (g0 + j) % 2
                        dve.wait_ge(chunk_done, g0 + m + 1)
                        v.scalar_tensor_tensor(out=two(rk(m)), in0=chunk_psum(par),
                                               scalar=gate(m), in1=two(rk(m)), op0=ALU.mult,
                                               op1=ALU.add).then_inc(psum_freed, 1)
                        sum_add(stat, m, j)
                repeat(dve, 0, n // 2, pair)

            dve.wait_ge(y_ready, 8)
            lo_tiles("a_out")
            dve.wait_ge(h_ready, H0["a_out"] + 8)
            sum_clear("kv")
            out_chunks("a_out", "kv", lambda m: MOD[:, bass.ds(16 + m, 1)])
            stats("kv", D)
            dve.wait_ge(mod_ready, 7)
            normed("kv", 8, rk, lambda k: xs(k % 3), lambda k: GS[:, 8 + k:9 + k],
                   lambda k: MOD[:, 24 + k:25 + k])
            dve.wait_ge(pos_loaded, 16)
            v.tensor_copy(table(0), table(4).bitcast(I32)).then_inc(tab_seq, 1)
            dve.wait_ge(tab_seq, 1)
            v.tensor_scalar(table(1), table(0), VEC[0:6 * RH, COL["freq"]:COL["freq"] + 1],
                            None, ALU.mult).then_inc(tab_seq, 1)
            for n, turn in enumerate((0.0, 0.25)):
                ang, k_, r_ = table(1), table(2), table(3 - 3 * n)
                b_ = 2 + 7 * n
                dve.wait_ge(tab_seq, b_)
                v.tensor_scalar(k_, ang, 1.0 / TWO_PI, turn, ALU.mult, ALU.add).then_inc(tab_seq, 1)
                dve.wait_ge(tab_seq, b_ + 1)
                v.tensor_scalar(k_, k_, MAGIC, MAGIC, ALU.add, ALU.subtract).then_inc(tab_seq, 1)
                dve.wait_ge(tab_seq, b_ + 2)
                v.scalar_tensor_tensor(out=r_, in0=k_, scalar=-C1, in1=ang, op0=ALU.mult,
                                       op1=ALU.add).then_inc(tab_seq, 1)
                for i, part in enumerate((C2, C3)):
                    dve.wait_ge(tab_seq, b_ + 3 + i)
                    v.scalar_tensor_tensor(out=r_, in0=k_, scalar=-part, in1=r_, op0=ALU.mult,
                                           op1=ALU.add).then_inc(tab_seq, 1)
                dve.wait_ge(tab_seq, b_ + 5)
                v.tensor_scalar(r_, r_, turn * TWO_PI, PI_F, ALU.add, ALU.min).then_inc(tab_seq, 1)
                dve.wait_ge(tab_seq, b_ + 6)
                v.tensor_scalar(r_, r_, -PI_F, None, ALU.max).then_inc(tab_seq, 1)
            normed("qz", 8, rk, lambda k: xs(k % 3), lambda k: GS[:, 16 + k:17 + k],
                   lambda k: MOD[:, 40 + k:41 + k])

            def row_max(a, h, t):
                dve.wait_ge(s_done, 8 * (a.head0 + h) + t + 1)
                src = PS[:, 2 * (t % 2):2 * (t % 2) + 2, :] if a.nk > HALF else \
                    PS[:, 2 * (t % 2), 0:a.nk]
                v.reduce_max(COLS[:, t, 0:1], src, AX.XY if a.nk > HALF else AX.X)\
                    .then_inc(m_done, 1)

            def exp_bias(a, h, t):
                dve.wait_ge(m_done, a.soft0 + 8 * h + t + 1)
                v.tensor_scalar(COLS[:, t, 1:2], COLS[:, t, 0:1], -a.scale, None, ALU.mult)\
                    .then_inc(nb_done, 1)

            def running(a, h, t):
                u = 8 * (a.head0 + h) + t
                n = a.nkt[t] * P
                dve.wait_ge(e_done, u + 1)
                if a.causal:
                    v.memset(SC[:, t % 4, n:n + 1], 1.0).then_inc(scan_done, 1)
                    s = SC[:, t % 4, 0:n][:, ::-1]
                    v.tensor_tensor_scan(s, s, MASK[:, TOK - n:][:, ::-1].bitcast(F32), 1.0,
                                         ALU.mult, ALU.max).then_inc(scan_done, 1)
                else:
                    v.reciprocal(COLS[:, t, 3:4], COLS[:, t, 2:3]).then_inc(rc_done, 1)

            def probs(a, h, t):
                u = 8 * (a.head0 + h) + t
                n = a.nkt[t] * P
                s = SC[:, t % 4, 0:n]
                if a.causal:
                    dve.wait_ge(scan_done, 2 * u + 2)
                    v.tensor_tensor(s, SC[:, t % 4, 1:n + 1], s, ALU.subtract).then_inc(p_done, 1)
                else:
                    dve.wait_ge(rc_done, a.soft0 + 8 * h + t + 1)
                    v.tensor_scalar(s, s, COLS[:, t, 3:4], None, ALU.mult).then_inc(p_done, 1)

            def lo_half(a, h, j, t, half):
                hi, n = keys_by_queries(HH, a, t, half)
                lo, _ = keys_by_queries(HL, a, t, half)
                dve.wait_ge(th_done, th_count(a, h, t, half))
                src = PS[:, 4 + parity(a, t, half, j), 0:n * P].rearrange("p (k q) -> p k q", q=P)
                v.tensor_tensor(lo, src, hi.bitcast(F32), ALU.subtract).then_inc(tl_done, 1)

            def v_tile(a, h, j, step):
                n = min(HALF, a.nk - HALF * step)
                c = v_count(a, h, step)
                dve.wait_ge(tr_done, c)
                v.tensor_copy(VS[:, j, HALF * step:HALF * step + n],
                              PS[:, 4 + v_parity(a, step, j), 0:n].bitcast(F32R))\
                    .then_inc(tl_done, 1)

            def begin(a):
                if not a.causal:
                    for t in range(a.s_ahead):
                        row_max(a, 0, t)
                        exp_bias(a, 0, t)
                for t in range(a.p_ahead):
                    running(a, 0, t)
                    probs(a, 0, t)

            def attend(a, following=None):

                def head(h, j, first, last):
                    def ahead(t, n):
                        return (h, t + n) if t + n < 8 else (h + 1, t + n - 8)
                    for t in range(8):
                        probs_ahead = t + a.p_ahead < 8 or not last
                        max_ahead = not a.causal and (t + a.s_ahead < 8 or not last)
                        if probs_ahead:
                            running(a, *ahead(t, a.p_ahead))
                        if a.causal and 1 <= t <= a.vsteps:
                            v_tile(a, h, j, t - 1)
                        if not a.causal and probs_ahead:
                            probs(a, *ahead(t, a.p_ahead))
                        lo_half(a, h, j, t, 0)
                        if a.causal and probs_ahead:
                            probs(a, *ahead(t, a.p_ahead))
                        if max_ahead:
                            row_max(a, *ahead(t, a.s_ahead))
                        if a.halves[t] == 2:
                            lo_half(a, h, j, t, 1)
                        if max_ahead:
                            exp_bias(a, *ahead(t, a.s_ahead))
                heads_of(dve, a, head)
                if following:
                    begin(following)

            v.memset(work(3), 0.0).then_inc(acc_clear, 1)
            dve.wait_ge(acc_clear, 2)
            v.tensor_copy(MASK[:, 0:TOK - P], work(3, TOK - P)).then_inc(acc_clear, 1)
            v.tensor_copy(MASK[:, TOK - P:], LATER[:]).then_inc(acc_clear, 1)
            dve.wait_ge(acc_clear, 4)
            begin(sbk)
            attend(sbk)

            def products(name, stage):
                def product(k):
                    s, c = XSN[stage, k]
                    dve.wait_ge(xs_loaded[s], c)
                    dve.wait_ge(gate_loaded[k % 2], G0[name] + 16 * (k // 2 + 1))
                    v.tensor_tensor(xs(k % 3), xs(k % 3), ACC[:, 4 + k % 2, :], ALU.mult)\
                        .then_inc(t_ready, 1)
                product(0)
                for k in range(8):
                    if k + 1 < 8:
                        product(k + 1)
                    dve.wait_ge(hi_ready, H0[name] + k + 1)
                    v.tensor_tensor(hk(HL, k), xs(k % 3), hk(HH, k).bitcast(F32), ALU.subtract)\
                        .then_inc(h_ready, 1)
            products("b_out", "bo")
            sum_clear("l0")
            out_chunks("b_out", "l0", lambda m: MOD[:, bass.ds(56 + m, 1)])
            stats_twice()
            normed("l0", 8, rk, lambda k: xs(k % 3), lambda k: G2[:, 8 + k:9 + k])
            dve.wait_ge(t_ready, T0["l0"] + 8)
            dve.wait_ge(stat_mm, STAT["l0"][1] + 3)
            for k in range(8):
                v.scalar_tensor_tensor(out=two(rk(k)), in0=two(rk(k)), scalar=vcol("f1_g", k),
                                       in1=rstd_rows(), op0=ALU.mult, op1=ALU.mult)\
                    .then_inc(x3_ready, 1)
            parts = (("uq", Q_LORA_T, TOK, latent, "q_g"),
                     ("ukv", KV_LORA_T, TOK, lambda k: latent(Q_LORA_T + k), "ckv_g"),
                     ("mem", 8, N_MEM, mem_tile, "mem_g"))
            for name, kts, ntok, src, gain in parts:
                sum_clear(name)
                for k in range(kts):
                    sum_add(name, k, k % 2, ntok)
                stats(name, kts * P, ntok)
                for k in range(kts):
                    v.scalar_tensor_tensor(out=like(src(k), ntok), in0=like(src(k), ntok),
                                           scalar=vcol(gain, k), in1=rstd_rows(ntok),
                                           op0=ALU.mult, op1=ALU.mult).then_inc(t_ready, 1)
            for name, kts, ntok, src, _ in parts:
                for k in range(kts):
                    dve.wait_ge(hi_ready, H0[name] + k + 1)
                    v.tensor_tensor(hk(HL, k, ntok, name), src(k),
                                    hk(HH, k, ntok, name).bitcast(F32), ALU.subtract)\
                        .then_inc(h_ready, 1)
            dve.wait_ge(cs_loaded, 32)
            for b in range(3):
                n = 6 * RH if b else RH
                t1, t2, m = (XS[0:n, i, :] for i in range(3))
                cos, sin = (ACC[0:n, 4 + i, :] for i in range(2))
                o1, o2 = (SC[0:n, 2 + i, 0:TOK] for i in range(2))
                r0 = ROPE_STEPS * b
                for s in range(2):
                    s_, c_ = XSN["rope", 2 * b + s]
                    dve.wait_ge(xs_loaded[s_], c_)
                if b:
                    for s in range(2):
                        dve.wait_ge(rope_stored[s], 16 * b)
                v.tensor_tensor(o1, t1, cos, ALU.mult).then_inc(rope_seq, 1)
                v.tensor_tensor(m, t2, sin, ALU.mult).then_inc(rope_seq, 1)
                dve.wait_ge(rope_seq, r0 + 2)
                v.tensor_tensor(o1, o1, m, ALU.subtract).then_inc(rope_seq, 1)
                v.tensor_tensor(o2, t2, cos, ALU.mult).then_inc(rope_seq, 1)
                dve.wait_ge(rope_seq, r0 + 4)
                v.tensor_tensor(m, t1, sin, ALU.mult).then_inc(rope_seq, 1)
                dve.wait_ge(rope_seq, r0 + 5)
                v.tensor_tensor(o2, o2, m, ALU.add).then_inc(rope_seq, 1)
            begin(mla)
            attend(mla, mmx)
            attend(mmx)
            products("l0_out", "lo")
            sum_clear("final")
            dve.wait_ge(x3_ready, 8)
            out_chunks("l0_out", "final", lambda m: ONE[:, 0:1])
            stats("final", D)
            for k in range(8):
                if k >= 4:
                    dve.wait_ge(out_stored[k % 4], 16)
                v.scalar_tensor_tensor(out=two(work(k % 4)), in0=two(rk(k)), scalar=vcol("f2_g", k),
                                       in1=rstd_rows(), op0=ALU.mult, op1=ALU.mult)\
                    .then_inc(out_ready, 1)

        @block.tensor
        def _(pe):
            t_ = nc.tensor

            def column_sums(name, ntok=TOK):
                _, c, a0 = SQ[name]
                n, sums = ntok // P, 2 if name == "l0" else 1
                pe.wait_ge(acc_done, a0 + 1 + sums * c)
                for i in range(sums):
                    for t in range(n):
                        last = t_.matmul(PS[:, 4, n * i + t:n * i + t + 1],
                                         SC[:, 2 + i, t * P:(t + 1) * P], ONE[:, 0:1],
                                         start=True, stop=True)
                last.then_inc(stat_mm, 1)

            def spread_rstd(name, ntok=TOK, row=0):
                n = ntok // P
                pe.wait_ge(stat_act, STAT[name][0] + 1)
                for t in range(n):
                    last = t_.matmul(PS[:, 5 + t // 4, (t % 4) * P:(t % 4 + 1) * P],
                                     SM[:, row, t:t + 1].to_broadcast([P, P]), IDF[:],
                                     start=True, stop=True)
                last.then_inc(stat_mm, 1)

            def first_rstd():
                pe.wait_ge(t_ready, T0["l0"] + 8)
                spread_rstd("l0", row=0)

            def stats(name, ntok=TOK):
                column_sums(name, ntok)
                spread_rstd(name, ntok)

            def chunk_ready(g):
                pe.wait_ge(w_lo, g + 1)
                if not (isinstance(g, int) and g < 2):
                    pe.wait_ge(psum_freed, g - 1)

            def feature_tile(name, par, hf, k, ntok=TOK):
                kts, n = KTILES.get(name, KT), min(ntok, HALF)
                w = slice(k * P, (k + 1) * P)
                c = INPUT_AT.get(name, 0) + k * ntok + hf * HALF
                for i, (a, b) in enumerate(((WH, HH), (WL, HH), (WH, HL))):
                    last = t_.matmul(PS[:, 2 * par + hf, 0:n], a[:, par, w], b[:, c:c + n],
                                     start=(k == 0 and i == 0), stop=(k == kts - 1 and i == 2))
                return last

            def chunk(name, g, par, first, ntok=TOK):
                chunk_ready(g)
                for hf in range(1 if ntok < TOK else 2):
                    for k in range(KTILES.get(name, KT)):
                        if first and hf == 0:
                            pe.wait_ge(h_ready, H0[name] + k + 1)
                        last = feature_tile(name, par, hf, k, ntok)
                last.then_inc(chunk_done, 1)

            def first_pair(name):
                g0 = FIRST[name]
                for n in range(KT + BEHIND):
                    for c, k in ((0, n), (1, n - BEHIND)):
                        if not 0 <= k < KT:
                            continue
                        if k == 0:
                            chunk_ready(g0 + c)
                        if c == 0:
                            pe.wait_ge(h_ready, H0[name] + k + 1)
                        for hf in range(2):
                            last = feature_tile(name, (g0 + c) % 2, hf, k)
                        if k == KT - 1:
                            last.then_inc(chunk_done, 1)

            def project(name, ntok=TOK, between={}):
                g0, n = FIRST[name], COUNT[name]
                begin = max(between, default=1) // 2 + 1
                if name in PAIRED:
                    first_pair(name)
                for m in range(2 * begin):
                    if m > 1 or name not in PAIRED:
                        chunk(name, g0 + m, (g0 + m) % 2, m == 0, ntok)
                    if m in between:
                        between[m]()

                def pair(i):
                    for j in range(2):
                        chunk(name, g0 + 2 * i + j, (g0 + j) % 2, False, ntok)
                repeat(pe, begin, n // 2, pair)
                if n % 2:
                    chunk(name, g0 + n - 1, (g0 + n - 1) % 2, False, ntok)

            def scores(a, h, j, t, start=False):
                g = a.head0 + h
                u = 8 * g + t
                if t == 0:
                    pe.wait_ge(qk_lo, 3 * g + 2)
                if not (isinstance(u, int) and u < 2):
                    pe.wait_ge(e_done, u - 1)
                n = a.nkt[t] * P
                q = slice(t * P, (t + 1) * P)
                terms = ((QH, WH), (QH, WL)) if a.stacked else ((QH, WH), (QL, WH), (QH, WL))
                r = P if a.stacked else a.rows
                for b in range((n + HALF - 1) // HALF):
                    w = min(HALF, n - b * HALF)
                    for i, (x, y) in enumerate(terms):
                        last = t_.matmul(PS[:, 2 * (t % 2) + b, 0:w], x[0:r, j, q],
                                         y[0:r, j, b * HALF:b * HALF + w],
                                         start=(i == 0), stop=(i == len(terms) - 1))
                last.then_inc(s_done, 1)

            def bank_free(c):
                if not (isinstance(c, int) and c <= 2):
                    pe.wait_ge(tl_done, c - 2)

            def transpose_v(a, h, j, step):
                g = a.head0 + h
                pe.wait_ge(qk_lo, 3 * g + 3)
                bank_free(v_count(a, h, step))
                for k in range(4 * step, min(4 * step + 4, a.nk // P)):
                    last = t_.transpose(PS[:, 4 + v_parity(a, step, j),
                                           (k % 4) * P:(k % 4 + 1) * P].bitcast(F32R),
                                        VV[:, k * P:(k + 1) * P], IDR[:])
                last.then_inc(tr_done, 1)

            def transpose_p(a, h, j, t, half):
                g = a.head0 + h
                if half == 0:
                    pe.wait_ge(p_done, 8 * g + t + 1)
                bank_free(tl_count(a, h, t, half))
                for k in range(4 * half, min(4 * half + 4, a.nkt[t])):
                    last = t_.transpose(PS[:, 4 + parity(a, t, half, j),
                                           (k % 4) * P:(k % 4 + 1) * P],
                                        SC[:, t % 4, k * P:(k + 1) * P], IDF[:])
                last.then_inc(tr_done, 1)

            def values(a, h, j, hf, part):
                g = a.head0 + h
                n = a.nkt[4 * hf + 3]
                each = (n + 3) // 4
                if part == 0:
                    t, half = 4 * hf + 3, a.halves[4 * hf + 3] - 1
                    pe.wait_ge(tl_done, tl_count(a, h, t, half))
                    if not (isinstance(h, int) and g == 0):
                        pe.wait_ge(ob_done, 2 * (2 * g + hf - 1))
                for k in range(each * part, min(n, each * part + each)):
                    c0 = max(0, k * P - hf * HALF) if a.causal else 0
                    for i, H in enumerate((HH, HL)):
                        base = 4096 * hf + HALF * k
                        last = t_.matmul(PS[:, 6 + hf, c0:HALF], VS[:, j, k * P:(k + 1) * P],
                                         H[:, base + c0:base + HALF], start=(k == 0 and i == 0),
                                         stop=(k == n - 1 and i == 1))
                    if k == n - 1:
                        last.then_inc(av_done, 1)

            def begin(a):
                for t in range(a.s_ahead):
                    scores(a, 0, 0, t)

            def attend(a, following=None):

                def head(h, j, first, last):
                    for t in range(8):
                        if 1 <= t <= a.vsteps:
                            transpose_v(a, h, j, t - 1)
                        transpose_p(a, h, j, t, 0)
                        if t + a.s_ahead < 8:
                            scores(a, h, j, t + a.s_ahead)
                        elif not last:
                            scores(a, h + 1, 1 - j, t + a.s_ahead - 8)
                        if a.halves[t] == 2:
                            transpose_p(a, h, j, t, 1)
                        if t >= 4:
                            values(a, h, j, 0, t - 4)
                        elif not first:
                            values(a, h - 1, 1 - j, 1, t)
                heads_of(pe, a, head)
                if following:
                    begin(following)
                for part in range(4):
                    values(a, a.heads - 1, (a.heads - 1) % 2, 1, part)

            pe.wait_ge(consts, 4)
            stats("a_in")
            project("a_in")
            project("a_out")
            stats("kv")
            project("kv")
            project("qz")
            pe.wait_ge(consts_r, 1)
            pe.wait_ge(psum_freed, FIRST["b_out"])
            begin(sbk)
            attend(sbk)
            project("b_out")
            column_sums("l0")
            spread_rstd("l0", row=1)
            project("l0", between={1: first_rstd, 3: lambda: column_sums("uq"), 4: lambda: spread_rstd("uq"),
                                   5: lambda: column_sums("ukv"), 6: lambda: spread_rstd("ukv"),
                                   7: lambda: column_sums("mem", N_MEM),
                                   8: lambda: spread_rstd("mem", N_MEM)})
            project("uq")
            project("ukv")
            project("mem", N_MEM)
            pe.wait_ge(psum_freed, FIRST["l0_out"])
            begin(mla)
            attend(mla, mmx)
            attend(mmx)
            project("l0_out")
            stats("final")


def kernel(**inputs):
    import concourse.bacc as bacc
    from concourse.bass_utils import run_bass_kernel_spmd

    a = {k: np.asarray(v) for k, v in inputs.items()}

    def chunks(w, cols):
        kt = w.shape[0] // P
        t = np.stack([w[:, c:c + P] for c in cols]).reshape(len(cols), kt, P, P)
        t = t.transpose(0, 2, 1, 3).reshape(len(cols), P, kt * P)
        full = np.zeros((len(cols), P, D), w.dtype)
        full[:, :, :kt * P] = t
        return full

    every = lambda n: [P * i for i in range(n)]
    nope = [96 * h + i for h in range(MLA_HEADS) for i in range(HEAD)]
    rope = [96 * h + HEAD + RH * s + i for s in range(2) for h in range(MLA_HEADS) for i in range(RH)]
    a_cols = [D * part + P * c for c in range(KT) for part in (1, 2, 0, 3)]
    wall = np.concatenate([
        chunks(a["a_w_in"][0], a_cols), chunks(a["a_w_out"][0], every(8)),
        chunks(a["w_kv"], every(16)), chunks(a["b_w_qz"][0], every(16)),
        chunks(a["b_w_out"][0], every(8)), chunks(a["w_in_l0_2"], L0_COLS),
        chunks(a["w_uq_l0_2"][:, rope + nope], every(9)), chunks(a["w_ukv_l0_2"], every(12)),
        chunks(a["w_mem_kv_l0_2"], every(4)), chunks(a["w_out_l0_2"], every(8))])

    def columns(vec):
        return vec.reshape(-1, P).T

    freq = (1.0 / (np.float32(10000.0) ** (np.arange(0, ROPE, 2, dtype=np.float32) / np.float32(ROPE))))
    vecs = np.concatenate([
        columns(a["a_mod_b"][0]), columns(a["kv_mod_b"]),
        columns(a["b_mod_b"][0]), columns(a["a_norm_g"][0]), columns(a["kv_norm_g"]),
        columns(a["b_norm_g"][0]), columns(a["final_norm_g"]), columns(a["norm_g_l0_2"]),
        columns(a["q_norm_g_l0_2"]), columns(a["kv_norm_g_l0_2"]), columns(a["mem_norm_g_l0_2"]),
        columns(a["final_norm_g_2"]), columns(a["a_conv_w"][0].reshape(-1)),
        np.tile(freq.astype(np.float32), P // RH)[:, None]], axis=1)

    mods = np.concatenate([a["a_mod_w"][0], a["kv_mod_w"], a["b_mod_w"][0]], axis=1)
    arrays = {
        "wall": wall, "vecs": vecs, "xT": a["x"][0].T.reshape(KT, P, TOK),
        "c_row": a["c"], "mod_w": mods.T.reshape(64, P, D),
        "pos": a["positions_2"],
        "memT": a["mem_2"][0].T.reshape(KT, P, N_MEM).transpose(1, 0, 2).reshape(P, KT * N_MEM),
    }
    arrays = {k: np.ascontiguousarray(v) for k, v in arrays.items()}
    nc = bacc.Bacc("TRN2", target_bir_lowering=False, num_devices=1)
    args = [nc.dram_tensor(k, v.shape, mybir.dt.from_np(v.dtype), kind="ExternalInput").ap()
            for k, v in arrays.items()]
    out = nc.dram_tensor("out", (KT, P, TOK), F32, kind="ExternalOutput").ap()
    build(nc, *args, out)
    r = run_bass_kernel_spmd(nc, [arrays], core_ids=[0])
    got = r.results[0]["out"]
    return np.ascontiguousarray(np.asarray(got).reshape(D, TOK).T)[None]
```
